# Optimizing a Trainium2 kernel written in Bass

```python
import jax, jax.numpy as jnp
from jax import lax
import numpy as np

D_MODEL = 2048
BATCH = 1
SEQ = 256
DEPTH = 1

CHUNK = 64
EPS = 1e-6

M_HEADS = 8
M_QK_DIM = 128
M_V_DIM = D_MODEL // M_HEADS
M_CONV = 4
M_QK = M_HEADS * M_QK_DIM
M_V = M_HEADS * M_V_DIM

A_HEADS = 32
A_KV_HEADS = 4
A_HEAD_DIM = D_MODEL // A_HEADS
A_Q = A_HEADS * A_HEAD_DIM
A_KV = A_KV_HEADS * A_HEAD_DIM
WINDOW = 128
WINDOW_CHUNKS = WINDOW // CHUNK

P_HEADS = 8
P_KEYS = 128
P_EXPERTS = P_KEYS * P_KEYS
P_TOPK = 16
P_QDIM = 256
P_HALF = P_QDIM // 2
P_TOKEN_BLOCK = 128

IN_SPLITS = (M_QK, M_QK, M_V, M_V, M_HEADS, M_HEADS, A_Q, A_KV, A_KV, D_MODEL, D_MODEL)
N_IN = M_QK * 2 + M_V * 2 + M_HEADS * 2 + A_Q + A_KV * 2 + D_MODEL * 2

kernel_name = "hybrid_mlstm_swa_sink_peer_block"

def rms_norm(x, w):
    xf = x.astype(jnp.float32)
    y = xf * lax.rsqrt(jnp.mean(xf * xf, axis=-1, keepdims=True) + EPS)
    return (y * w.astype(jnp.float32)).astype(x.dtype)

def causal_dwconv(x, w):
    k_width, c = w.shape
    return lax.conv_general_dilated(
        x, w[:, None, :].astype(x.dtype), window_strides=(1,),
        padding=[(k_width - 1, 0)], dimension_numbers=('NWC', 'WIO', 'NWC'),
        feature_group_count=c)

def _mlstm_chunk_step(carry, xs):
    c_state, n_state, m_state = carry
    q, k, v, logf, ig = xs
    L = q.shape[-2]
    causal = jnp.tril(jnp.ones((L, L), dtype=bool))
    b = jnp.cumsum(logf, axis=-1)
    d = jnp.where(causal, b[..., :, None] - b[..., None, :] + ig[..., None, :], -jnp.inf)
    inter = b + m_state[..., None]
    m_t = jnp.maximum(jnp.max(d, axis=-1), inter)
    s = jnp.einsum('bhtd,bhsd->bhts', q, k) * jnp.exp(d - m_t[..., None])
    w_inter = jnp.exp(inter - m_t)
    num = jnp.einsum('bhts,bhsv->bhtv', s, v) + w_inter[..., None] * jnp.einsum('bhtd,bhdv->bhtv', q, c_state)
    den = jnp.sum(s, axis=-1) + w_inter * jnp.einsum('bhtd,bhd->bht', q, n_state)
    h = num / jnp.maximum(jnp.abs(den), jnp.exp(-m_t))[..., None]
    b_last = b[..., -1]
    a = b_last[..., None] - b + ig
    m_new = jnp.maximum(b_last + m_state, jnp.max(a, axis=-1))
    w_a = jnp.exp(a - m_new[..., None])
    decay = jnp.exp(b_last + m_state - m_new)
    c_new = decay[..., None, None] * c_state + jnp.einsum('bhs,bhsd,bhsv->bhdv', w_a, k, v)
    n_new = decay[..., None] * n_state + jnp.einsum('bhs,bhsd->bhd', w_a, k)
    return (c_new, n_new, m_new), h

def mlstm_mixer(q, k, v, i_pre, f_pre):
    B, S, H, dk = q.shape
    dv = v.shape[-1]
    nc = S // CHUNK
    f32 = jnp.float32

    def to_chunks(t):
        t = t.astype(f32).reshape(B, nc, CHUNK, H, -1)
        return jnp.transpose(t, (1, 0, 3, 2, 4))

    def gate_chunks(t):
        t = t.astype(f32).reshape(B, nc, CHUNK, H)
        return jnp.transpose(t, (1, 0, 3, 2))

    qc = to_chunks(q) * (dk ** -0.5)
    kc = to_chunks(k)
    vc = to_chunks(v)
    logf = gate_chunks(jax.nn.log_sigmoid(f_pre.astype(f32)))
    ig = gate_chunks(i_pre)
    init = (jnp.zeros((B, H, dk, dv), f32), jnp.zeros((B, H, dk), f32), jnp.zeros((B, H), f32))
    _, h = lax.scan(_mlstm_chunk_step, init, (qc, kc, vc, logf, ig))
    h = jnp.transpose(h, (1, 0, 3, 2, 4)).reshape(B, S, H, dv)
    return h.astype(v.dtype)

def swa_sink_attention(q, k, v, sinks):
    B, S, Hq, dh = q.shape
    Hkv = k.shape[2]
    R = Hq // Hkv
    nc = S // CHUNK
    qc = q.reshape(B, nc, CHUNK, Hkv, R, dh)
    kc = k.reshape(B, nc, CHUNK, Hkv, dh)
    vc = v.reshape(B, nc, CHUNK, Hkv, dh)

    def band(t):
        parts = [jnp.pad(t, ((0, 0), (w, 0), (0, 0), (0, 0), (0, 0)))[:, :nc]
                 for w in reversed(range(WINDOW_CHUNKS))]
        return jnp.concatenate(parts, axis=2)

    kb = band(kc)
    vb = band(vc)
    offs = (WINDOW_CHUNKS - 1) - jnp.arange(WINDOW_CHUNKS)
    valid = (jnp.arange(nc)[:, None] - offs[None, :]) >= 0
    valid = jnp.repeat(valid, CHUNK, axis=1)
    logits = jnp.einsum('bclgrd,bcsgd->bcgrls', qc, kb).astype(jnp.float32) * (dh ** -0.5)
    logits = jnp.where(valid[None, :, None, None, None, :], logits, -jnp.inf)
    sink = jnp.broadcast_to(sinks.astype(jnp.float32).reshape(Hkv, R)[None, None, :, :, None, None],
                            logits.shape[:-1] + (1,))
    p = jax.nn.softmax(jnp.concatenate([logits, sink], axis=-1), axis=-1)[..., :-1]
    out = jnp.einsum('bcgrls,bcsgd->bclgrd', p.astype(v.dtype), vb)
    return out.reshape(B, S, Hq * dh)

def peer(x, w_q, sub_keys, expert_u, expert_v):
    B, S, D = x.shape
    T = B * S
    xt = x.reshape(T, D)
    q = (xt @ w_q).reshape(T, P_HEADS, 2, P_HALF)
    s = jnp.einsum('thcd,ckd->thck', q, sub_keys).astype(jnp.float32)
    v1, i1 = lax.top_k(s[:, :, 0], P_TOPK)
    v2, i2 = lax.top_k(s[:, :, 1], P_TOPK)
    cand = (v1[..., :, None] + v2[..., None, :]).reshape(T, P_HEADS, P_TOPK * P_TOPK)
    best, pos = lax.top_k(cand, P_TOPK)
    e_idx = (jnp.take_along_axis(i1, pos // P_TOPK, axis=-1) * P_KEYS
             + jnp.take_along_axis(i2, pos % P_TOPK, axis=-1))
    g = jax.nn.softmax(best, axis=-1)
    nb = T // P_TOKEN_BLOCK

    def block(args):
        xb, eb, gb = args
        u = expert_u[eb]
        act = jax.nn.gelu(jnp.einsum('thkd,td->thk', u, xb).astype(jnp.float32), approximate=False)
        return jnp.einsum('thk,thkd->td', (gb * act).astype(xb.dtype), expert_v[eb])

    out = lax.map(block, (xt.reshape(nb, P_TOKEN_BLOCK, D),
                          e_idx.reshape(nb, P_TOKEN_BLOCK, P_HEADS, P_TOPK),
                          g.reshape(nb, P_TOKEN_BLOCK, P_HEADS, P_TOPK)))
    return out.reshape(B, S, D)

def hybrid_layer(x, norm1_w, w_in, conv_w, b_igate, b_fgate, mlstm_norm_w, q_norm_w, k_norm_w,
                 sinks, w_proj_m, w_proj_a, w_out, norm2_w, w_peer_q, sub_keys, expert_u, expert_v):
    B, S, D = x.shape
    xn = rms_norm(x, norm1_w)
    proj = xn @ w_in
    cuts = [int(c) for c in np.cumsum(IN_SPLITS)[:-1]]
    (q_m, k_m, v_m, o_m, i_m, f_m, q_a, k_a, v_a, g_m, g_a) = jnp.split(proj, cuts, axis=-1)

    qk = jax.nn.silu(causal_dwconv(jnp.concatenate([q_m, k_m], axis=-1), conv_w))
    qm = qk[..., :M_QK].reshape(B, S, M_HEADS, M_QK_DIM)
    km = qk[..., M_QK:].reshape(B, S, M_HEADS, M_QK_DIM)
    vm = v_m.reshape(B, S, M_HEADS, M_V_DIM)
    hm = mlstm_mixer(qm, km, vm, i_m + b_igate, f_m + b_fgate)
    hm = rms_norm(hm, mlstm_norm_w).reshape(B, S, M_V) * jax.nn.sigmoid(o_m)

    qa = rms_norm(q_a.reshape(B, S, A_HEADS, A_HEAD_DIM), q_norm_w)
    ka = rms_norm(k_a.reshape(B, S, A_KV_HEADS, A_HEAD_DIM), k_norm_w)
    va = v_a.reshape(B, S, A_KV_HEADS, A_HEAD_DIM)
    ha = swa_sink_attention(qa, ka, va, sinks)

    y = jax.nn.sigmoid(g_m) * (hm @ w_proj_m) + jax.nn.sigmoid(g_a) * (ha @ w_proj_a)
    x = x + y @ w_out

    x = x + peer(rms_norm(x, norm2_w), w_peer_q, sub_keys, expert_u, expert_v)
    return x

def setup_inputs(seed: int = 0) -> dict:
    key = jax.random.key(seed)
    ks = jax.random.split(key, 20)
    f32 = jnp.float32
    L = DEPTH

    def nrm(k, shape, scale):
        return jax.random.normal(k, shape, f32) * scale

    return {
        'x': jax.random.normal(ks[0], (BATCH, SEQ, D_MODEL), f32),
        'norm1_w': 1.0 + nrm(ks[1], (L, D_MODEL), 0.02),
        'w_in': nrm(ks[2], (L, D_MODEL, N_IN), D_MODEL ** -0.5),
        'conv_w': nrm(ks[3], (L, M_CONV, 2 * M_QK), M_CONV ** -0.5),
        'b_igate': nrm(ks[4], (L, M_HEADS), 0.1),
        'b_fgate': 3.0 + 3.0 * jax.random.uniform(ks[5], (L, M_HEADS), f32),
        'mlstm_norm_w': 1.0 + nrm(ks[6], (L, M_V_DIM), 0.02),
        'q_norm_w': 1.0 + nrm(ks[7], (L, A_HEAD_DIM), 0.02),
        'k_norm_w': 1.0 + nrm(ks[8], (L, A_HEAD_DIM), 0.02),
        'sinks': nrm(ks[9], (L, A_HEADS), 0.5),
        'w_proj_m': nrm(ks[10], (L, M_V, D_MODEL), M_V ** -0.5),
        'w_proj_a': nrm(ks[11], (L, A_Q, D_MODEL), A_Q ** -0.5),
        'w_out': nrm(ks[12], (L, D_MODEL, D_MODEL), D_MODEL ** -0.5),
        'norm2_w': 1.0 + nrm(ks[13], (L, D_MODEL), 0.02),
        'w_peer_q': nrm(ks[14], (L, D_MODEL, P_HEADS * P_QDIM), D_MODEL ** -0.5),
        'sub_keys': nrm(ks[15], (L, 2, P_KEYS, P_HALF), P_HALF ** -0.5),
        'expert_u': nrm(ks[16], (L, P_EXPERTS, D_MODEL), D_MODEL ** -0.5),
        'expert_v': nrm(ks[17], (L, P_EXPERTS, D_MODEL), P_HEADS ** -0.5),
    }

def reference(x, norm1_w, w_in, conv_w, b_igate, b_fgate, mlstm_norm_w, q_norm_w, k_norm_w,
              sinks, w_proj_m, w_proj_a, w_out, norm2_w, w_peer_q, sub_keys, expert_u, expert_v):
    for l in range(DEPTH):
        x = hybrid_layer(x, norm1_w[l], w_in[l], conv_w[l], b_igate[l], b_fgate[l], mlstm_norm_w[l],
                         q_norm_w[l], k_norm_w[l], sinks[l], w_proj_m[l], w_proj_a[l], w_out[l],
                         norm2_w[l], w_peer_q[l], sub_keys[l], expert_u[l], expert_v[l])
    return x


_drawn_inputs = setup_inputs


def setup_inputs(seed=0):
    import zlib

    import numpy as np

    out = dict(_drawn_inputs(seed))
    spreads = {}
    factors = {'b_igate': 64.0,
     'mlstm_norm_w': 10.242,
     'q_norm_w': 8.0,
     'k_norm_w': 7.537,
     'sinks': 8.0,
     'norm2_w': 8.895}
    for name, (base, spread) in spreads.items():
        noise = np.random.default_rng([zlib.crc32(name.encode()), seed]).standard_normal(out[name].shape)
        drawn = base * np.exp(spread * noise) if base else spread * noise
        out[name] = __import__('jax').numpy.asarray(drawn.astype(out[name].dtype))
    for name, factor in factors.items():
        out[name] = (out[name] * factor).astype(out[name].dtype)
    return out
```

```python
from contextlib import ExitStack

import numpy as np
import concourse.bass as bass
from concourse import mybir

F32 = mybir.dt.float32
R32 = mybir.dt.float32r
U32 = mybir.dt.uint32
I32 = mybir.dt.int32
ALU = mybir.AluOpType
ACT = mybir.ActivationFunctionType
AX = mybir.AxisListType

P = 128
T = 256
D = 2048
TT = T // P
KC = D // P
EPS = 1e-6
BLK = 512
UW = 1024
BU = D * BLK // P // UW
RAW, HI, LO = 4, 4, 2

MH, MV = 8, 256
AH, KVH, DH, CH = 32, 4, 64, 64
NCH = T // CH
PAIRS = AH // KVH // 2
PH, PK, TOP = 8, 128, 16

B_BIG = 12
B_GATE = 12
B_IN = 1 + B_BIG + B_GATE
B_MAT = D // BLK
B_PA, B_PM, B_WO, B_PQ = (B_IN + B_MAT * i for i in range(4))
B_END = B_PQ + B_MAT
U_U = B_END * BU
CU = P * D // P // UW
CPB = 4
U_V = U_U + PK * CU
UNITS = U_V + PK * CU
NEG = -1.0e30


def block_program(nc, units, w_if, x_d, norm1, norm2, conv_w, if_bias, mnorm, qk_w, sinks, subk_d,
                  out_d, gates_d, x2_d):
    with ExitStack() as ctx:
        def sem(name):
            return ctx.enter_context(nc.semaphore(name))

        def sb(stack, name, shape, dt=F32):
            return stack.enter_context(nc.sbuf_tensor(name, shape, dt))

        raw = sb(ctx, "raw", [P, RAW, UW])
        whi = sb(ctx, "whi", [P, HI, UW], R32)
        wlo = sb(ctx, "wlo", [P, LO, UW], R32)
        t1hi = sb(ctx, "t1hi", [P, KC, T], R32)
        t1lo = sb(ctx, "t1lo", [P, KC, T], R32)
        ident = sb(ctx, "ident", [P, P])
        small = sb(ctx, "small", [P, 8])
        eps_t, ss, sd, rs = small[:, 0:1], small[:, 2:4], small[:, 4:6], small[:, 6:8]

        with ExitStack() as p1:
            t2hi = sb(p1, "t2hi", [P, KC, T], R32)
            t2lo = sb(p1, "t2lo", [P, KC, T], R32)
            big = sb(p1, "big", [P, TT, B_BIG * BLK])
            kv = sb(p1, "kv", [P, TT, BLK])
            bt = sb(p1, "bt", [P, KC, T])
            stage = sb(p1, "stage", [P, 2, TT * BLK])
            stage4 = sb(p1, "stage4", [P, 2, TT * BLK])
            n1 = sb(p1, "n1", [P, KC])
            n2 = sb(p1, "n2", [P, KC])
            cw = sb(p1, "cw", [P, KC, 4])
            ifb = sb(p1, "ifb", [P, 16])
            mw = sb(p1, "mw", [P, KC])
            qkw = sb(p1, "qkw", [P, 2])
            sink = sb(p1, "sink", [P, KC])
            gt = sb(p1, "gt", [P, 8, TT, 16])
            qs = sb(p1, "qs", [P, 3, TT, 36])
            ast = sb(p1, "ast", [P, 2, 7, PAIRS])
            hs = sb(p1, "hs", [P, 3, TT, MH])
            hd = sb(p1, "hd", [P, 2, 2, TT])
            ones = sb(p1, "ones", [P, 2])
            mrow = sb(p1, "mrow", [MH, 3, T])
            tri = sb(p1, "tri", [P, T])
            mask = sb(p1, "mask", [P, T])
            with ExitStack() as pa:
                kte = sb(pa, "kte", [P, KVH, T])
                kto = sb(pa, "kto", [P, KVH, T])
                vb2 = sb(pa, "vb2", [P, KVH * DH])
            with ExitStack() as pm:
                wg = sb(pm, "wg", [P, KC, 16])
                wghi = sb(pm, "wghi", [P, KC, 16], R32)
                wglo = sb(pm, "wglo", [P, KC, 16], R32)
        sqj = [s[:].rearrange("p a b -> p (a b)") for s in (stage, stage4)]
        ksq = kto[:, 0:2, :]
        kd = stage4[:, 0, :].rearrange("p (t g r d) -> p t g r d", t=TT, g=KVH, r=2)
        prob = stage[:, 0, :].rearrange("p (b j n) -> p b j n", b=2, j=PAIRS)
        probT = stage[:, 1, :].rearrange("p (b j n) -> p b j n", b=2, j=PAIRS)
        ee = stage[:, 0, 0:6 * P].rearrange("p (b n) -> p b n", b=2)
        pp = stage[:, 1, 0:6 * P].rearrange("p (b n) -> p b n", b=2)
        hsq = sqj[1].rearrange("p (s n) -> p s n", n=MV)
        R0, R1, R2 = (big[:, :, i * D:(i + 1) * D] for i in range(3))
        o_sb = bt[:].rearrange("p k t -> p (k t)").rearrange("p (a n) -> p a n", a=TT)

        def qT_of(kc):
            return big[:, kc // 8, kc % 8 * T:(kc % 8 + 1) * T]

        with ExitStack() as q0:
            qp = sb(q0, "qp", [P, TT, D])
            qT = sb(q0, "qT", [P, 2 * PH, T])
            sc = sb(q0, "sc", [P, TT, 2 * PH, PK])
            subk = sb(q0, "subk", [P, 2, PK])
            tv = sb(q0, "tv", [P, TT, 2 * PH, TOP])
            ti = sb(q0, "ti", [P, TT, 2 * PH, TOP], U32)
            tif = sb(q0, "tif", [P, TT, 2 * PH, TOP])
            cand = sb(q0, "cand", [P, TT, PH, TOP * TOP])
            bv = sb(q0, "bv", [P, TT, PH, TOP])
            bi = sb(q0, "bi", [P, TT, PH, TOP], U32)
            ba = sb(q0, "ba", [P, 2, TT, PH * TOP], U32)
            baf = sb(q0, "baf", [P, 2, TT, PH * TOP])
            eq = sb(q0, "eq", [P, TT, PH * TOP, TOP])
            hk = sb(q0, "hk", [P, 3, TT, PH * TOP])
            gsum = sb(q0, "gsum", [P, 2, TT, PH])
        g = sb(ctx, "g", [P, PK, T])
        hkT = sb(ctx, "hkT", [P, 3, T])
        iota = sb(ctx, "iota", [P, P])
        with ExitStack() as q2:
            oha = sb(q2, "oha", [P, 2, P])
            ohb = sb(q2, "ohb", [P, 2, P])
        with ExitStack() as q3:
            gel = sb(q3, "gel", [P, 2, T])
        iota32 = gel[:, 0, 0:P].bitcast(I32)
        x2_back = [t[:, KC // 2:KC, :].rearrange("p k t -> p (k t)").bitcast(F32) for t in (t1hi, t1lo)]
        PS = ctx.enter_context(nc.psum_tensor("PS", [P, 8, BLK], F32))

        pre, fab, fexp, fln, fmin = (gt[:, i, :, :] for i in range(5))
        logf, a_in, bsum = gt[:, 5, :, 0:8], gt[:, 5, :, 8:16], gt[:, 6, :, 0:8]
        mt, expnm = gt[:, 6, :, 8:16], gt[:, 7, :, 0:8]
        mfin = mrow[:, 2, :]

        raw_landed = [sem(f"raw_landed{i}") for i in range(RAW)]
        hi_made, lo_made, unit_used = sem("hi_made"), sem("lo_made"), sem("unit_used")
        block_out = sem("block_out")
        consts, eps_set, iota_set = sem("consts"), sem("eps_set"), sem("iota_set")
        x_in, w_small, wif_in, subk_in = sem("x_in"), sem("w_small"), sem("wif_in"), sem("subk_in")
        gate_stored = [sem("gate_stored0"), sem("gate_stored1")]
        o_in, ga_in, gm_in, xr_in = sem("o_in"), sem("ga_in"), sem("gm_in"), sem("xr_in")
        x2_stored, x2_in, out_stored = sem("x2_stored"), sem("x2_in"), sem("out_stored")
        n_sq, n_root, n_rs, n_scaled = sem("n_sq"), sem("n_root"), sem("n_rs"), sem("n_scaled")
        turned, t_hi, t_lo = sem("turned"), sem("t_hi"), sem("t_lo")
        wg_hi, wg_lo, if_mm, if_sb = sem("wg_hi"), sem("wg_lo"), sem("if_mm"), sem("if_sb")
        gate_act, f_min, logf_s, b_mm, b_sb, a_s = (sem("gate_act"), sem("f_min"), sem("logf_s"), sem("b_mm"),
                                                    sem("b_sb"), sem("a_s"))
        at_mm, m_step, mt_mm, mt_s, expnm_s = sem("at_mm"), sem("m_step"), sem("mt_mm"), sem("mt_s"), sem("expnm_s")
        qk_turned, conv_step, conv_done, sig_done, silu_done = (
            sem("qk_turned"), sem("conv_step"), sem("conv_done"), sem("sig_done"), sem("silu_done"))
        q_sq, q_sum, q_root, q_rs, q_scaled = sem("q_sq"), sem("q_sum"), sem("q_root"), sem("q_rs"), sem("q_scaled")
        k_zero, q_turned, q_out, vb2_s = sem("k_zero"), sem("q_turned"), sem("q_out"), sem("vb2_s")
        st_peak, st_sum, st_rec = sem("st_peak"), sem("st_sum"), sem("st_rec")
        logits_s, st_step, st_max, prob_exp, prob_norm = (
            sem("logits_s"), sem("st_step"), sem("st_max"), sem("prob_exp"), sem("prob_norm"))
        prob_turned, probT_sb, av_mm, av_hi, av_lo = (
            sem("prob_turned"), sem("probT_sb"), sem("av_mm"), sem("av_hi"), sem("av_lo"))
        ms_mm, ms_arg, ms_exp, ms_p, mn_mm, mn_step, h_out, h_sq = (
            sem("ms_mm"), sem("ms_arg"), sem("ms_exp"), sem("ms_p"), sem("mn_mm"), sem("mn_step"),
            sem("h_out"), sem("h_sq"))
        h_root, h_rs, h_gated, pm_mul, y_add = (sem("h_root"), sem("h_rs"), sem("h_gated"), sem("pm_mul"),
                                                sem("y_add"))
        qp_turned, qT_sb, score_mm, score_sb = sem("qp_turned"), sem("qT_sb"), sem("score_mm"), sem("score_sb")
        route, best_sub, best_exp, hk_turned, hkT_sb = (
            sem("route"), sem("best_sub"), sem("best_exp"), sem("hk_turned"), sem("hkT_sb"))
        hk_ready = sem("hk_ready")
        onehots, g_mm, g_out = sem("onehots"), sem("g_mm"), sem("g_out")
        gelu_done, w_made = sem("gelu_done"), sem("w_made")
        wch_hi, wch_lo = sem("wch_hi"), sem("wch_lo")
        y_out = sem("y_out")
        block = ctx.enter_context(nc.Block())

        def load_unit(sp, u, k, first=False):
            if not first:
                sp.wait_ge(lo_made, u - RAW + 1)
            sp.dma_start(raw[:, k % RAW, :], units[bass.ds(u, 1), :, :].rearrange("a p n -> p (a n)")
                         ).then_inc(raw_landed[k % RAW], 16)

        def hi_unit(act, u, k, landed):
            act.wait_ge(raw_landed[k % RAW], landed)
            if not (isinstance(u, int) and u < HI):
                act.wait_ge(unit_used, u - HI + 1)
            act.activation(whi[:, k % HI, :], raw[:, k % RAW, :], ACT.Copy).then_inc(hi_made, 1)

        def lo_unit(dve, u, k):
            dve.wait_ge(hi_made, u + 1)
            if not (isinstance(u, int) and u < LO):
                dve.wait_ge(unit_used, u - LO + 1)
            dve.tensor_tensor(wlo[:, k % LO, :], raw[:, k % RAW, :], whi[:, k % HI, :].bitcast(F32),
                              ALU.subtract).then_inc(lo_made, 1)

        def hi_block(act, b, evacuate=None):
            for k in range(BU):
                hi_unit(act, b * BU + k, k, b * (BU // RAW * 16) + (k // RAW + 1) * 16)
                if k == HI - 1 and evacuate is not None:
                    evacuate()

        def lo_block(dve, b, evacuate=None):
            for k in range(BU):
                lo_unit(dve, b * BU + k, k)
                if k == LO - 1 and evacuate is not None:
                    evacuate()

        def mm_block(pe, b, odd, thi, tlo):
            if not (isinstance(b, int) and b < 2):
                pe.wait_ge(block_out, b - 1)
            for k in range(BU):
                pe.wait_ge(lo_made, b * BU + k + 1)
                for kk in range(2):
                    kc = 2 * k + kk
                    vh = whi[:, k % HI, kk * BLK:(kk + 1) * BLK]
                    vl = wlo[:, k % LO, kk * BLK:(kk + 1) * BLK]
                    for tt in range(TT):
                        o = PS[:, 2 * odd + tt, :]
                        sh, sl = thi[:, kc, tt * P:(tt + 1) * P], tlo[:, kc, tt * P:(tt + 1) * P]
                        pe.matmul(o, sh, vh, start=(kc == 0), stop=False)
                        pe.matmul(o, sh, vl, start=False, stop=False)
                        mm = pe.matmul(o, sl, vh, start=False, stop=(kc == KC - 1))
                mm.then_inc(unit_used, 1)

        def mm_matrix(pe, first, thi, tlo):
            for b in range(first, first + B_MAT):
                mm_block(pe, b, b % 2, thi, tlo)

        def turn(pe, n, src):
            for kc in range(KC):
                if n or kc >= 4:
                    pe.wait_ge(t_lo, KC * n + kc - 3)
                for tt in range(TT):
                    mm = pe.transpose(PS[:, 4 + kc % 4, tt * P:(tt + 1) * P], src[:, tt, kc * P:(kc + 1) * P],
                                      ident[:])
                mm.then_inc(turned, 1)

        def turn_hi(act, n, thi, w):
            for kc in range(KC):
                act.wait_ge(turned, KC * n + kc + 1)
                act.activation(thi[:, kc, :], PS[:, 4 + kc % 4, 0:T], ACT.Copy,
                               scale=(1.0 if w is None else w[:, kc:kc + 1])).then_inc(t_hi, 1)

        def turn_lo(dve, n, thi, tlo, w):
            for kc in range(KC):
                dve.wait_ge(t_hi, KC * n + kc + 1)
                dve.scalar_tensor_tensor(tlo[:, kc, :], PS[:, 4 + kc % 4, 0:T],
                                         1.0 if w is None else w[:, kc:kc + 1],
                                         thi[:, kc, :].bitcast(F32), ALU.mult, ALU.subtract).then_inc(t_lo, 1)

        def norm_act(act, n, xin):
            for tt in range(TT):
                act.activation(sqj[tt], xin[:, tt, :], ACT.Square, accum_out=ss[:, tt:tt + 1]).then_inc(n_sq, 1)
            act.wait_ge(n_sq, TT * (n + 1))
            act.activation(sd, ss, ACT.Sqrt, scale=1.0 / D, bias=eps_t).then_inc(n_root, 1)

        def norm_dve(dve, n, xin, out):
            dve.wait_ge(n_root, n + 1)
            dve.reciprocal(rs, sd).then_inc(n_rs, 1)
            dve.wait_ge(n_rs, n + 1)
            for tt in range(TT):
                dve.tensor_scalar(out[:, tt, :], xin[:, tt, :], rs[:, tt:tt + 1], None, ALU.mult
                                  ).then_inc(n_scaled, 1)

        def window(c):
            return {0: [(0, 0, CH)], 1: [(0, 0, P)], 2: [(0, P, P + CH), (CH, CH, P)], 3: [(0, CH * 2, T)]}[c]

        def keys_of(c):
            return CH if c == 0 else P

        @block.sync
        def _(sp):
            for u in range(RAW):
                load_unit(sp, u, u, first=True)
            with sp.Fori(1, UNITS // RAW) as i:
                for k in range(RAW):
                    load_unit(sp, i * RAW + k, k)

        @block.gpsimd
        def _(pool):
            pool.dma_start(R2, x_d).then_inc(x_in, 16)
            for dst, src in ((n1, norm1), (n2, norm2), (cw, conv_w), (ifb, if_bias), (mw, mnorm), (qkw, qk_w),
                             (sink, sinks)):
                pool.dma_start(dst[:], src).then_inc(w_small, 16)
            pool.dma_start(wg[:], w_if).then_inc(wif_in, 16)
            pool.memset(small[:], EPS).then_inc(eps_set, 1)
            pool.memset(ones[:], 1.0).then_inc(consts, 1)
            pool.memset(ident[:], 0.0).then_inc(consts, 1)
            pool.memset(tri[:], 1.0).then_inc(consts, 1)
            pool.memset(mask[:], 0.0).then_inc(consts, 1)
            pool.wait_ge(consts, 4)
            pool.affine_select(out=ident[:], in_=ident[:], compare_op=ALU.not_equal, fill=1.0, base=0,
                               pattern=[[-1, P]], channel_multiplier=1).then_inc(consts, 1)
            pool.affine_select(out=tri[:], in_=tri[:], compare_op=ALU.is_ge, fill=0.0, base=0,
                               pattern=[[1, T]], channel_multiplier=-1).then_inc(consts, 1)
            pool.affine_select(out=mask[:], in_=mask[:], compare_op=ALU.is_ge, fill=NEG, base=0,
                               pattern=[[1, T]], channel_multiplier=-1).then_inc(consts, 1)
            for n in range(B_GATE):
                pool.wait_ge(block_out, 1 + B_BIG + n + 1)
                pool.dma_start(gates_d[n], stage[:, n % 2, :]).then_inc(gate_stored[n % 2], 16)
            for s in gate_stored:
                pool.wait_ge(s, 16 * B_GATE // 2)

            def gates_back(dst, first, s):
                for n in range(B_MAT):
                    pool.dma_start(dst[:, :, n * BLK:(n + 1) * BLK],
                                   gates_d[first + n].rearrange("p (a n) -> p a n", a=TT)).then_inc(s, 16)

            pool.wait_ge(av_lo, KVH * NCH)
            gates_back(R0, 2 * B_MAT, ga_in)
            pool.wait_ge(mn_mm, MH)
            gates_back(o_sb, 0, o_in)
            gates_back(R1, B_MAT, gm_in)
            pool.wait_ge(turned, 2 * KC)
            pool.dma_start(R2, x_d).then_inc(xr_in, 16)
            pool.wait_ge(block_out, B_WO + B_MAT)
            pool.dma_start(x2_d, R2).then_inc(x2_stored, 16)
            pool.wait_ge(x2_stored, 16)
            pool.wait_ge(t_lo, 4 * KC)
            pool.dma_start(subk[:], subk_d).then_inc(subk_in, 16)
            pool.iota(iota32, pattern=[[1, P]], base=0, channel_multiplier=0).then_inc(iota_set, 1)
            pool.wait_ge(iota_set, 1)
            pool.tensor_copy(iota[:], iota32).then_inc(iota_set, 1)
            pool.wait_ge(unit_used, U_V)
            for tt in range(TT):
                pool.dma_start(x2_back[tt], x2_d[:, tt, :]).then_inc(x2_in, 16)
            for tt in range(TT):
                pool.wait_ge(y_out, tt + 1)
                pool.dma_start(out_d[:, tt, :], g[:, 8 * tt:8 * tt + 8, :].rearrange("p k t -> p (k t)")
                               ).then_inc(out_stored, 16)
            pool.wait_ge(out_stored, 16 * TT)

        @block.scalar
        def _(act):
            act.wait_ge(x_in, 16)
            act.wait_ge(eps_set, 1)
            norm_act(act, 0, R2)
            act.wait_ge(w_small, 7 * 16)
            turn_hi(act, 0, t1hi, n1)
            act.wait_ge(wif_in, 16)
            act.activation(wghi[:], wg[:], ACT.Copy).then_inc(wg_hi, 1)

            def out_kv():
                act.activation(kv[:], PS[:, 0:TT, :], ACT.Copy).then_inc(block_out, 1)

            def out_big(b, odd):
                act.activation(big[:, :, bass.ds((b - 1) * BLK, BLK)], PS[:, 2 * odd:2 * odd + TT, :], ACT.Copy
                               ).then_inc(block_out, 1)

            def out_gate(odd, stored=None):
                if stored is not None:
                    act.wait_ge(gate_stored[1 - odd], stored)
                act.activation(stage[:, 1 - odd, :].rearrange("p (a n) -> p a n", a=TT),
                               PS[:, 2 * odd:2 * odd + TT, :], ACT.Sigmoid).then_inc(block_out, 1)

            hi_block(act, 0)
            hi_block(act, 1, out_kv)
            with act.Fori(1, 1 + B_BIG // 2) as i:
                hi_block(act, i * 2, lambda: out_big(i * 2 - 1, 1))
                hi_block(act, i * 2 + 1, lambda: out_big(i * 2, 0))
            hi_block(act, 14, lambda: out_gate(1))
            hi_block(act, 15, lambda: out_gate(0))
            with act.Fori(1, B_GATE // 2 - 1) as i:
                hi_block(act, i * 2 + 14, lambda: out_gate(1, i * 16))
                hi_block(act, i * 2 + 15, lambda: out_gate(0, i * 16))
            hi_block(act, 24, lambda: out_gate(1, 80))
            act.wait_ge(unit_used, B_IN * BU)
            out_gate(0, 80)

            act.wait_ge(consts, 7)
            act.wait_ge(if_sb, 1)
            act.activation(fab, pre, ACT.Abs).then_inc(gate_act, 1)
            act.wait_ge(gate_act, 1)
            act.activation(fexp, fab, ACT.Exp, scale=-1.0).then_inc(gate_act, 1)
            act.wait_ge(gate_act, 2)
            act.activation(fln, fexp, ACT.Ln, bias=ones[:, 0:1]).then_inc(gate_act, 1)
            act.wait_ge(mt_s, 1)
            act.activation(expnm, mt, ACT.Exp, scale=-1.0).then_inc(expnm_s, 1)

            for s in gate_stored:
                act.wait_ge(s, 16 * B_GATE // 2)
            for n in range(4):
                act.wait_ge(conv_done, 4 * n + 4)
                act.activation((stage, stage4)[n // 2][:, n % 2, :],
                               bt[:, 4 * n:4 * n + 4, :].rearrange("p k t -> p (k t)"), ACT.Sigmoid
                               ).then_inc(sig_done, 1)

            act.wait_ge(silu_done, 4)
            for tt in range(TT):
                act.activation(sqj[tt], R2[:, tt, :], ACT.Square).then_inc(q_sq, 1)
            act.activation(ksq, kv[:, :, 0:T], ACT.Square).then_inc(q_sq, 1)
            act.wait_ge(q_sum, 3)
            act.activation(qs[:, 1, :, :], qs[:, 0, :, :], ACT.Sqrt, scale=1.0 / DH, bias=eps_t).then_inc(q_root, 1)

            n_it = KVH * NCH
            for s in range(n_it + 2):
                if s < n_it:
                    b, w = s % 2, keys_of(s % NCH)
                    act.wait_ge(st_max, s + 1)
                    if s >= 2:
                        act.wait_ge(prob_turned, s - 1)
                    for j in range(PAIRS):
                        act.activation(prob[:, b, j, 0:w], PS[:, 4 + b, j * P:j * P + w], ACT.Exp,
                                       bias=ast[:, b, 1, j:j + 1], accum_out=ast[:, b, 3, j:j + 1])
                    act.activation(ast[:, b, 4, :], ast[:, b, 2, :], ACT.Exp).then_inc(prob_exp, 1)
                if 1 <= s <= n_it:
                    i, b = s - 1, (s - 1) % 2
                    act.wait_ge(prob_turned, i + 1)
                    if i >= 2:
                        act.wait_ge(av_mm, i - 1)
                    act.activation(probT[:, b], PS[:, 6, :].rearrange("p (j n) -> p j n", j=PAIRS), ACT.Copy
                                   ).then_inc(probT_sb, 1)
                if s >= 2:
                    i = s - 2
                    gq, c = i // NCH, i % NCH
                    act.wait_ge(av_mm, i + 1)
                    act.activation(t2hi[:, PAIRS * gq:PAIRS * (gq + 1), c * CH:(c + 1) * CH],
                                   PS[:, 7, 0:T].rearrange("p (j l) -> p j l", j=PAIRS), ACT.Copy
                                   ).then_inc(av_hi, 1)

            for s in range(MH + 1):
                if s < MH:
                    b = s % 2
                    act.wait_ge(ms_arg, s + 1)
                    act.activation(ee[:, b, 0:T], ee[:, b, 0:T], ACT.Exp, bias=a_in[:, 0, s:s + 1])
                    act.activation(ee[:, b, T:3 * P], ee[:, b, T:3 * P], ACT.Exp, bias=a_in[:, 1, s:s + 1]
                                   ).then_inc(ms_exp, 1)
                if s >= 1:
                    h = s - 1
                    act.wait_ge(h_out, h + 1)
                    if h >= 4:
                        act.wait_ge(h_sq, 2 * (h - 3))
                    for tt in range(TT):
                        act.activation(hsq[:, (2 * h + tt) % 8, :], R2[:, tt, h * MV:(h + 1) * MV], ACT.Square,
                                       accum_out=hs[:, 0, tt, h:h + 1]).then_inc(h_sq, 1)
            act.wait_ge(h_sq, 2 * MH)
            act.activation(hs[:, 1], hs[:, 0], ACT.Sqrt, scale=1.0 / MV, bias=eps_t).then_inc(h_root, 1)
            turn_hi(act, 1, t1hi, mw)

            with act.Fori(B_PA, B_PM + B_MAT) as b:
                hi_block(act, b)
            turn_hi(act, 2, t2hi, None)
            with act.Fori(B_WO, B_WO + B_MAT) as b:
                hi_block(act, b)
            act.wait_ge(block_out, B_WO + B_MAT)
            norm_act(act, 1, R2)
            turn_hi(act, 3, t1hi, n2)
            with act.Fori(B_PQ, B_PQ + B_MAT) as b:
                hi_block(act, b)

            for n in range(2 * PH):
                act.wait_ge(qp_turned, n + 1)
                act.activation(qT[:, n, :], PS[:, 4 + n % 4, 0:T], ACT.Copy).then_inc(qT_sb, 1)
            for n in range(PH):
                act.wait_ge(score_mm, n + 1)
                act.activation(sc[:, :, 2 * n:2 * n + 2, :].rearrange("p a c k -> p c a k"),
                               PS[:, n % 4, :].rearrange("p (c a k) -> p c a k", c=2, a=TT), ACT.Copy
                               ).then_inc(score_sb, 1)
            act.wait_ge(best_sub, 1)
            act.activation(bv[:], bv[:], ACT.Exp).then_inc(best_exp, 1)

            with act.Fori(0, T // 8) as i:
                for b in range(2):
                    act.wait_ge(g_mm, i * 8 + 4 * b + 4)
                    act.activation(g[:, :, bass.ds(i * 8 + 4 * b, 4)].rearrange("p k t -> p t k"),
                                   PS[:, 6 + b, :].rearrange("p (t k) -> p t k", t=4), ACT.Copy).then_inc(g_out, 1)

            def gelu_chunk(c, k):
                if not (isinstance(c, int) and c < 2):
                    act.wait_ge(w_made, c - 1)
                act.activation(gel[:, k % 2, :], PS[:, k % 4, 0:T], ACT.Gelu).then_inc(gelu_done, 1)

            def u_body(i, lag):
                for k in range(CPB):
                    for j in range(CU):
                        n = CU * k + j
                        u = i * (CPB * CU) + (U_U + n)
                        hi_unit(act, u, n, i * (CPB * CU // RAW * 16) + (U_U // RAW + n // RAW + 1) * 16)
                    if lag or k >= 2:
                        gelu_chunk(i * CPB + (k - 2), k - 2 + CPB)

            u_body(0, False)
            with act.Fori(1, PK // CPB) as i:
                u_body(i, True)
            for c in (PK - 2, PK - 1):
                act.wait_ge(unit_used, U_U + CU * (c + 1))
                gelu_chunk(c, c)

            def v_body(i, first):
                for k in range(CPB):
                    c = i * CPB + k
                    if first:
                        act.wait_ge(w_made, PK)
                    else:
                        act.wait_ge(unit_used, i * (CPB * CU) + (U_V + CU * (k - 3)))
                    act.activation(t1hi[:, k, :], g[:, bass.ds(c, 1), :].rearrange("p a t -> p (a t)"), ACT.Copy
                                   ).then_inc(wch_hi, 1)
                    for j in range(CU):
                        n = CU * k + j
                        hi_unit(act, i * (CPB * CU) + (U_V + n), n,
                                i * (CPB * CU // RAW * 16) + (U_V // RAW + n // RAW + 1) * 16)

            v_body(0, True)
            with act.Fori(1, PK // CPB) as i:
                v_body(i, False)

        @block.tensor
        def _(pe):
            pe.wait_ge(consts, 7)
            pe.wait_ge(n_scaled, TT)
            turn(pe, 0, R2)
            pe.wait_ge(t_lo, KC)
            mm_block(pe, 0, 0, t1hi, t1lo)
            mm_block(pe, 1, 1, t1hi, t1lo)
            with pe.Fori(1, B_IN // 2) as i:
                mm_block(pe, i * 2, 0, t1hi, t1lo)
                mm_block(pe, i * 2 + 1, 1, t1hi, t1lo)
            mm_block(pe, B_IN - 1, 0, t1hi, t1lo)

            pe.wait_ge(wg_lo, 1)
            for tt in range(TT):
                for kc in range(KC):
                    sh, sl = t1hi[:, kc, tt * P:(tt + 1) * P], t1lo[:, kc, tt * P:(tt + 1) * P]
                    o = PS[:, 4, tt * 16:(tt + 1) * 16]
                    pe.matmul(o, sh, wghi[:, kc, :], start=(kc == 0), stop=False)
                    pe.matmul(o, sh, wglo[:, kc, :], start=False, stop=False)
                    mm = pe.matmul(o, sl, wghi[:, kc, :], start=False, stop=(kc == KC - 1))
            mm.then_inc(if_mm, 1)
            pe.wait_ge(logf_s, 1)
            pe.matmul(PS[:, 5, 0:MH], tri[:, 0:P], logf[:, 0, :], start=True, stop=True)
            pe.matmul(PS[:, 5, MH:2 * MH], tri[:, P:T], logf[:, 0, :], start=True, stop=False)
            pe.matmul(PS[:, 5, MH:2 * MH], tri[:, 0:P], logf[:, 1, :], start=False, stop=True).then_inc(b_mm, 1)
            pe.wait_ge(a_s, 1)
            for tt in range(TT):
                mm = pe.matmul(PS[0:MH, 6, tt * P:(tt + 1) * P], a_in[:, tt, :], ident[:], start=True, stop=True)
            mm.then_inc(at_mm, 1)
            pe.wait_ge(m_step, 10)
            for tt in range(TT):
                mm = pe.matmul(PS[:, 7, tt * MH:(tt + 1) * MH], mfin[:, tt * P:(tt + 1) * P], ident[0:MH, 0:MH],
                               start=True, stop=True)
            mm.then_inc(mt_mm, 1)

            pe.wait_ge(block_out, B_IN)
            pe.wait_ge(mt_s, 1)
            for n in range(KC):
                if n >= 4:
                    pe.wait_ge(conv_done, n - 3)
                for tt in range(TT):
                    mm = pe.transpose(PS[:, 4 + n % 4, tt * P:(tt + 1) * P], R0[:, tt, n * P:(n + 1) * P], ident[:])
                mm.then_inc(qk_turned, 1)

            pe.wait_ge(conv_done, KC)
            pe.wait_ge(q_scaled, 2 + 2 * TT)
            for n in range(KC + KVH):
                if n >= 4:
                    pe.wait_ge(q_out, n - 3)
                for tt in range(TT):
                    src = (R2[:, tt, n * P:(n + 1) * P] if n < KC else
                           kd[:, tt, n - KC, :, :].rearrange("p r d -> p (r d)"))
                    mm = pe.transpose(PS[:, 4 + n % 4, tt * P:(tt + 1) * P], src, ident[:])
                mm.then_inc(q_turned, 1)

            pe.wait_ge(q_out, KC + KVH)
            pe.wait_ge(vb2_s, 1)
            n_it = KVH * NCH
            for s in range(n_it + 2):
                if s < n_it:
                    b, gq, c = s % 2, s // NCH, s % NCH
                    if s >= 2:
                        pe.wait_ge(prob_exp, s - 1)
                    for j in range(PAIRS):
                        qj = qT_of(PAIRS * gq + j)[:, c * CH:(c + 1) * CH]
                        for par, kt in ((0, kte), (1, kto)):
                            for at, k0, k1 in window(c):
                                mm = pe.matmul(PS[par * CH:(par + 1) * CH, 4 + b, j * P + at:j * P + at + k1 - k0],
                                               qj, kt[:, gq, k0:k1], start=True, stop=True)
                    mm.then_inc(logits_s, 1)
                if 1 <= s <= n_it:
                    i, b = s - 1, (s - 1) % 2
                    pe.wait_ge(prob_norm, i + 1)
                    if i >= 1:
                        pe.wait_ge(probT_sb, i)
                    for j in range(PAIRS):
                        mm = pe.transpose(PS[:, 6, j * P:(j + 1) * P], prob[:, b, j, :], ident[:])
                    mm.then_inc(prob_turned, 1)
                if s >= 2:
                    i, b = s - 2, s % 2
                    gq, c = i // NCH, i % NCH
                    pe.wait_ge(probT_sb, i + 1)
                    if i >= 1:
                        pe.wait_ge(av_lo, i)
                    cols = slice(T + gq * DH, T + (gq + 1) * DH)
                    v = (kv[:, 0, cols], kv[:, 0, cols], vb2[:, gq * DH:(gq + 1) * DH], kv[:, 1, cols])[c]
                    for par in range(2):
                        mm = pe.matmul(PS[par * DH:(par + 1) * DH, 7, 0:T], v,
                                       probT[:, b, :, par * CH:(par + 1) * CH], start=True, stop=True)
                    mm.then_inc(av_mm, 1)

            pe.wait_ge(silu_done, 4)
            pe.wait_ge(av_lo, n_it)
            for s in range(MH + 1):
                if s < MH:
                    b = s % 2
                    if s >= 2:
                        pe.wait_ge(ms_p, s - 1)
                    pe.matmul(PS[:, b, 0:T], ident[0:MH, s:s + 1].to_broadcast([MH, P]), mfin, start=True, stop=True)
                    pe.matmul(PS[:, 2 + b, 0:T], bt[:, MH + s, 0:P], bt[:, s, :], start=True, stop=True)
                    pe.matmul(PS[:, 2 + b, T:3 * P], bt[:, MH + s, P:T], bt[:, s, P:T], start=True, stop=True
                              ).then_inc(ms_mm, 1)
                if s >= 1:
                    h, b = s - 1, (s - 1) % 2
                    pe.wait_ge(ms_p, h + 1)
                    if h >= 2:
                        pe.wait_ge(h_out, h - 1)
                    v = [R1[:, tt, h * MV:(h + 1) * MV] for tt in range(TT)]
                    for rhs, at in ((v, slice(0, MV)), ([ones[:, 0:1]] * TT, slice(MV, MV + 1))):
                        pe.matmul(PS[:, 4 + 2 * b, at], pp[:, b, 0:P], rhs[0], start=True, stop=True)
                        pe.matmul(PS[:, 5 + 2 * b, at], pp[:, b, P:T], rhs[0], start=True, stop=False)
                        mm = pe.matmul(PS[:, 5 + 2 * b, at], pp[:, b, T:3 * P], rhs[1], start=False, stop=True)
                    mm.then_inc(mn_mm, 1)

            pe.wait_ge(h_gated, TT)
            turn(pe, 1, R2)
            mm_matrix(pe, B_PA, t2hi, t2lo)
            pe.wait_ge(t_lo, 2 * KC)
            mm_matrix(pe, B_PM, t1hi, t1lo)
            pe.wait_ge(y_add, B_MAT)
            turn(pe, 2, R0)
            pe.wait_ge(t_lo, 3 * KC)
            mm_matrix(pe, B_WO, t2hi, t2lo)
            pe.wait_ge(n_scaled, 2 * TT)
            turn(pe, 3, R0)
            pe.wait_ge(t_lo, 4 * KC)
            mm_matrix(pe, B_PQ, t1hi, t1lo)

            pe.wait_ge(block_out, B_END)
            for n in range(2 * PH):
                if n >= 4:
                    pe.wait_ge(qT_sb, n - 3)
                for tt in range(TT):
                    mm = pe.transpose(PS[:, 4 + n % 4, tt * P:(tt + 1) * P], qp[:, tt, n * P:(n + 1) * P], ident[:])
                mm.then_inc(qp_turned, 1)
            pe.wait_ge(subk_in, 16)
            for n in range(PH):
                pe.wait_ge(qT_sb, 2 * n + 2)
                if n >= 4:
                    pe.wait_ge(score_sb, n - 3)
                for c in range(2):
                    for tt in range(TT):
                        at = (c * TT + tt) * PK
                        mm = pe.matmul(PS[:, n % 4, at:at + PK], qT[:, 2 * n + c, tt * P:(tt + 1) * P], subk[:, c, :],
                                       start=True, stop=True)
                mm.then_inc(score_mm, 1)
            for n in range(3):
                pe.wait_ge(hk_ready, 1)
                pe.wait_ge(qT_sb, 2 * PH)
                for tt in range(TT):
                    mm = pe.transpose(PS[:, 4 + n, tt * P:(tt + 1) * P], hk[:, n, tt, :], ident[:])
                mm.then_inc(hk_turned, 1)

            pe.wait_ge(hkT_sb, 3)

            def g_group(i, b, first):
                for k in range(4):
                    t = i * 8 + (4 * b + k)
                    pe.wait_ge(onehots, t + 1)
                    if k == 0 and not first:
                        pe.wait_ge(g_out, i * 2 + b - 1)
                    pe.matmul(PS[:, 6 + b, k * PK:(k + 1) * PK], oha[:, k % 2, :], ohb[:, k % 2, :],
                              start=True, stop=True).then_inc(g_mm, 1)

            for b in range(2):
                g_group(0, b, True)
            with pe.Fori(1, T // 8) as i:
                for b in range(2):
                    g_group(i, b, False)

            def u_body(i, first):
                for k in range(CPB):
                    if not first:
                        pe.wait_ge(gelu_done, i * CPB + (k - 3))
                    for j in range(CU):
                        n = CU * k + j
                        pe.wait_ge(lo_made, i * (CPB * CU) + (U_U + n + 1))
                        for kk in range(UW // P):
                            kc = j * (UW // P) + kk
                            wh = whi[:, n % HI, kk * P:(kk + 1) * P]
                            wl = wlo[:, n % LO, kk * P:(kk + 1) * P]
                            o = PS[:, k % 4, 0:T]
                            pe.matmul(o, wh, t1hi[:, kc, :], start=(kc == 0), stop=False)
                            pe.matmul(o, wh, t1lo[:, kc, :], start=False, stop=False)
                            mm = pe.matmul(o, wl, t1hi[:, kc, :], start=False, stop=(kc == KC - 1))
                        mm.then_inc(unit_used, 1)

            u_body(0, True)
            with pe.Fori(1, PK // CPB) as i:
                u_body(i, False)

            pe.wait_ge(gelu_done, PK)
            pe.wait_ge(g_out, T // 4)

            def v_body(i, first, last):
                for k in range(CPB):
                    pe.wait_ge(wch_lo, i * CPB + (k + 1))
                    for j in range(CU):
                        n = CU * k + j
                        pe.wait_ge(lo_made, i * (CPB * CU) + (U_V + n + 1))
                        for tt in range(TT):
                            sh, sl = t1hi[:, k, tt * P:(tt + 1) * P], t1lo[:, k, tt * P:(tt + 1) * P]
                            for half in range(2):
                                o = PS[:, 4 * tt + 2 * j + half, :]
                                vh = whi[:, n % HI, half * BLK:(half + 1) * BLK]
                                vl = wlo[:, n % LO, half * BLK:(half + 1) * BLK]
                                pe.matmul(o, sh, vh, start=(first and k == 0), stop=False)
                                pe.matmul(o, sh, vl, start=False, stop=False)
                                mm = pe.matmul(o, sl, vh, start=False, stop=(last and k == CPB - 1))
                        mm.then_inc(unit_used, 1)

            v_body(0, True, False)
            with pe.Fori(1, PK // CPB - 1) as i:
                v_body(i, False, False)
            v_body(PK // CPB - 1, False, True)

        @block.vector
        def _(dve):
            dve.wait_ge(x_in, 16)
            norm_dve(dve, 0, R2, R2)
            dve.wait_ge(w_small, 7 * 16)
            turn_lo(dve, 0, t1hi, t1lo, n1)
            dve.wait_ge(wg_hi, 1)
            dve.tensor_tensor(wglo[:], wg[:], wghi[:].bitcast(F32), ALU.subtract).then_inc(wg_lo, 1)

            lo_block(dve, 0)
            with dve.Fori(1, B_IN) as b:
                lo_block(dve, b)

            dve.wait_ge(if_mm, 1)
            dve.tensor_tensor(pre, PS[:, 4, 0:TT * 16].rearrange("p (a n) -> p a n", a=TT),
                              ifb[:].unsqueeze(1).to_broadcast([P, TT, 16]), ALU.add).then_inc(if_sb, 1)
            dve.wait_ge(if_sb, 1)
            dve.tensor_scalar(fmin, pre, 0.0, None, ALU.min).then_inc(f_min, 1)
            dve.wait_ge(f_min, 1)
            dve.wait_ge(gate_act, 3)
            dve.tensor_tensor(logf, fmin[:, :, 8:16], fln[:, :, 8:16], ALU.subtract).then_inc(logf_s, 1)
            dve.wait_ge(b_mm, 1)
            dve.tensor_copy(bsum, PS[:, 5, 0:TT * MH].rearrange("p (a n) -> p a n", a=TT)).then_inc(b_sb, 1)
            dve.wait_ge(b_sb, 1)
            dve.tensor_tensor(a_in, pre[:, :, 0:8], bsum, ALU.subtract).then_inc(a_s, 1)
            dve.wait_ge(at_mm, 1)
            dve.tensor_copy(mrow[:, 0, :], PS[0:MH, 6, 0:T]).then_inc(m_step, 1)
            for n in range(8):
                w, src, dst = 1 << n, mrow[:, n % 2, :], mrow[:, (n + 1) % 2, :]
                dve.wait_ge(m_step, n + 1)
                dve.tensor_copy(dst[:, 0:w], src[:, 0:w])
                dve.tensor_tensor(dst[:, w:T], src[:, w:T], src[:, 0:T - w], ALU.max).then_inc(m_step, 1)
            dve.wait_ge(m_step, 9)
            dve.tensor_scalar(mfin, mrow[:, 0, :], 0.0, None, ALU.max).then_inc(m_step, 1)
            dve.wait_ge(mt_mm, 1)
            dve.tensor_tensor(mt, PS[:, 7, 0:TT * MH].rearrange("p (a n) -> p a n", a=TT), bsum, ALU.add
                              ).then_inc(mt_s, 1)

            for n in range(KC):
                dve.wait_ge(qk_turned, n + 1)
                x, y = PS[:, 4 + n % 4, 0:T], bt[:, n, :]
                dve.tensor_scalar(y, x, cw[:, n, 3:4], None, ALU.mult).then_inc(conv_step, 1)
                for back in range(1, 4):
                    dve.wait_ge(conv_step, 3 * n + back)
                    dve.scalar_tensor_tensor(y[:, back:T], x[:, 0:T - back], cw[:, n, 3 - back:4 - back],
                                             y[:, back:T], ALU.mult, ALU.add
                                             ).then_inc(conv_step if back < 3 else conv_done, 1)
            for n in range(4):
                dve.wait_ge(sig_done, n + 1)
                y = bt[:, 4 * n:4 * n + 4, :].rearrange("p k t -> p (k t)")
                dve.tensor_tensor(y, y, (stage, stage4)[n // 2][:, n % 2, :], ALU.mult).then_inc(silu_done, 1)

            dve.wait_ge(q_sq, 3)
            for tt in range(TT):
                dve.tensor_reduce(qs[:, 0, tt, 0:AH], sqj[tt].rearrange("p (h d) -> p h d", d=DH), AX.X, ALU.add
                                  ).then_inc(q_sum, 1)
            dve.tensor_reduce(qs[:, 0, :, AH:AH + KVH], ksq.rearrange("p a (h d) -> p a h d", d=DH), AX.X, ALU.add
                              ).then_inc(q_sum, 1)
            dve.wait_ge(q_sum, 3)
            dve.memset(kte[DH:P, :, :], 0.0).then_inc(k_zero, 1)
            dve.memset(kto[0:DH, :, :], 0.0).then_inc(k_zero, 1)
            dve.tensor_copy(vb2[0:CH, :], kv[0:CH, 1, T:2 * T]).then_inc(k_zero, 1)
            dve.tensor_copy(vb2[CH:P, :], kv[CH:P, 0, T:2 * T]).then_inc(k_zero, 1)
            dve.wait_ge(k_zero, 4)
            dve.wait_ge(q_root, 1)
            dve.reciprocal(qs[:, 2], qs[:, 1]).then_inc(q_rs, 1)
            dve.wait_ge(q_rs, 1)
            for tt in range(TT):
                q = R2[:, tt, :].rearrange("p (h d) -> p h d", d=DH)
                dve.tensor_tensor(q, q, qs[:, 2, tt, 0:AH].unsqueeze(2).to_broadcast([P, AH, DH]), ALU.mult
                                  ).then_inc(q_scaled, 1)
                for r in range(2):
                    dve.tensor_tensor(kd[:, tt, :, r, :], kv[:, tt, 0:T].rearrange("p (h d) -> p h d", d=DH),
                                      qs[:, 2, tt, AH:AH + KVH].unsqueeze(2).to_broadcast([P, KVH, DH]), ALU.mult
                                      ).then_inc(q_scaled, 1)
            for n in range(KC + KVH):
                dve.wait_ge(q_turned, n + 1)
                x = PS[:, 4 + n % 4, 0:T]
                if n < KC:
                    dve.tensor_scalar(qT_of(n), x, qkw[:, 0:1], float(DH) ** -0.5, ALU.mult, ALU.mult
                                      ).then_inc(q_out, 1)
                else:
                    dve.tensor_scalar(kte[0:DH, n - KC, :], x[0:DH], qkw[0:DH, 1:2], None, ALU.mult)
                    dve.tensor_scalar(kto[DH:P, n - KC, :], x[DH:P], qkw[DH:P, 1:2], None, ALU.mult
                                      ).then_inc(q_out, 1)
            dve.memset(stage[:, 0, :], 0.0).then_inc(vb2_s, 1)
            dve.wait_ge(vb2_s, 1)

            n_it = KVH * NCH
            for s in range(n_it + 2):
                if s < n_it:
                    b, gq, w = s % 2, s // NCH, keys_of(s % NCH)
                    sk = sink[:, PAIRS * gq:PAIRS * (gq + 1)]
                    dve.wait_ge(logits_s, s + 1)
                    dve.tensor_reduce(ast[:, b, 0, :], PS[:, 4 + b, :].rearrange("p (j n) -> p j n", j=PAIRS)[:, :, 0:w],
                                      AX.X, ALU.max).then_inc(st_step, 1)
                    dve.wait_ge(st_step, s + 1)
                    dve.tensor_tensor(ast[:, b, 0, :], ast[:, b, 0, :], sk, ALU.max).then_inc(st_peak, 1)
                    dve.wait_ge(st_peak, s + 1)
                    dve.tensor_scalar(ast[:, b, 1, :], ast[:, b, 0, :], -1.0, None, ALU.mult)
                    dve.tensor_tensor(ast[:, b, 2, :], sk, ast[:, b, 0, :], ALU.subtract).then_inc(st_max, 1)
                if 1 <= s <= n_it:
                    i, b, w = s - 1, (s - 1) % 2, keys_of((s - 1) % NCH)
                    dve.wait_ge(prob_exp, i + 1)
                    if w < P:
                        dve.memset(prob[:, b, :, w:P], 0.0)
                    dve.tensor_tensor(ast[:, b, 5, :], ast[:, b, 3, :], ast[:, b, 4, :], ALU.add).then_inc(st_sum, 1)
                    dve.wait_ge(st_sum, i + 1)
                    dve.reciprocal(ast[:, b, 6, :], ast[:, b, 5, :]).then_inc(st_rec, 1)
                    dve.wait_ge(st_rec, i + 1)
                    dve.tensor_tensor(prob[:, b, :, 0:w], prob[:, b, :, 0:w],
                                      ast[:, b, 6, :].unsqueeze(2).to_broadcast([P, PAIRS, w]), ALU.mult
                                      ).then_inc(prob_norm, 1)
                if s >= 2:
                    i = s - 2
                    gq, c = i // NCH, i % NCH
                    dve.wait_ge(av_hi, i + 1)
                    at = (slice(None), slice(PAIRS * gq, PAIRS * (gq + 1)), slice(c * CH, (c + 1) * CH))
                    dve.tensor_tensor(t2lo[at], PS[:, 7, 0:T].rearrange("p (j l) -> p j l", j=PAIRS),
                                      t2hi[at].bitcast(F32), ALU.subtract).then_inc(av_lo, 1)

            for s in range(MH + 1):
                if s < MH:
                    b = s % 2
                    dve.wait_ge(ms_mm, s + 1)
                    if s >= 2:
                        dve.wait_ge(ms_p, s - 1)
                    dve.scalar_tensor_tensor(ee[:, b, 0:T], PS[:, b, 0:T], -1.0, mask[:], ALU.mult, ALU.add)
                    dve.scalar_tensor_tensor(ee[:, b, T:3 * P], PS[:, b, P:T], -1.0, mask[:, 0:P], ALU.mult, ALU.add
                                             ).then_inc(ms_arg, 1)
                if s >= 1:
                    h, b = s - 1, (s - 1) % 2
                    if h == 0:
                        dve.wait_ge(expnm_s, 1)
                    dve.wait_ge(mn_mm, h + 1)
                    den = hd[:, b, 0, :]
                    dve.tensor_copy(den, PS[:, 4 + 2 * b:6 + 2 * b, MV:MV + 1].rearrange("p a n -> p (a n)")
                                    ).then_inc(mn_step, 1)
                    dve.wait_ge(mn_step, 4 * h + 1)
                    dve.scalar_tensor_tensor(den, den, -1.0, den, ALU.mult, ALU.max).then_inc(mn_step, 1)
                    dve.wait_ge(mn_step, 4 * h + 2)
                    dve.tensor_tensor(den, den, expnm[:, :, h], ALU.max).then_inc(mn_step, 1)
                    dve.wait_ge(mn_step, 4 * h + 3)
                    dve.reciprocal(hd[:, b, 1, :], den).then_inc(mn_step, 1)
                    dve.wait_ge(mn_step, 4 * h + 4)
                    for tt in range(TT):
                        mm = dve.tensor_scalar(R2[:, tt, h * MV:(h + 1) * MV], PS[:, 4 + 2 * b + tt, 0:MV],
                                               hd[:, b, 1, tt:tt + 1], None, ALU.mult)
                    mm.then_inc(h_out, 1)
                if s < MH:
                    b = s % 2
                    dve.wait_ge(ms_exp, s + 1)
                    if s >= 2:
                        dve.wait_ge(mn_mm, s - 1)
                    dve.scalar_tensor_tensor(pp[:, b, :], PS[:, 2 + b, 0:3 * P], float(P) ** -0.5, ee[:, b, :],
                                             ALU.mult, ALU.mult).then_inc(ms_p, 1)
            dve.wait_ge(h_root, 1)
            dve.reciprocal(hs[:, 2], hs[:, 1]).then_inc(h_rs, 1)
            dve.wait_ge(h_rs, 1)
            dve.wait_ge(o_in, 16 * B_MAT)
            for tt in range(TT):
                y = R2[:, tt, :].rearrange("p (h d) -> p h d", d=MV)
                dve.tensor_tensor(y, y, hs[:, 2, tt, :].unsqueeze(2).to_broadcast([P, MH, MV]), ALU.mult
                                  ).then_inc(h_rs, 1)
            for tt in range(TT):
                dve.wait_ge(h_rs, 2 + tt)
                dve.tensor_tensor(R2[:, tt, :], R2[:, tt, :], o_sb[:, tt, :], ALU.mult).then_inc(h_gated, 1)
            turn_lo(dve, 1, t1hi, t1lo, mw)

            def cols(b):
                n = (b - B_IN) % B_MAT
                return slice(n * BLK, (n + 1) * BLK)

            def banks(b):
                return PS[:, 2 * (b % 2):2 * (b % 2) + TT, :]

            def out_pa(b):
                if b == B_PA:
                    dve.wait_ge(ga_in, 16 * B_MAT)
                dve.tensor_tensor(R0[:, :, cols(b)], banks(b), R0[:, :, cols(b)], ALU.mult).then_inc(block_out, 1)

            def out_pm(b):
                if b == B_PM:
                    dve.wait_ge(gm_in, 16 * B_MAT)
                dve.tensor_tensor(R1[:, :, cols(b)], banks(b), R1[:, :, cols(b)], ALU.mult).then_inc(block_out, 1)
                dve.wait_ge(block_out, b + 1)
                dve.tensor_tensor(R0[:, :, cols(b)], R0[:, :, cols(b)], R1[:, :, cols(b)], ALU.add).then_inc(y_add, 1)

            def out_wo(b):
                if b == B_WO:
                    dve.wait_ge(xr_in, 16)
                dve.tensor_tensor(R2[:, :, cols(b)], banks(b), R2[:, :, cols(b)], ALU.add).then_inc(block_out, 1)

            def out_pq(b):
                dve.tensor_copy(qp[:, :, cols(b)], banks(b)).then_inc(block_out, 1)

            def matrices(first, last, out):
                for b in range(first, last):
                    lo_block(dve, b, None if b == first else lambda: out(b - 1))
                dve.wait_ge(unit_used, last * BU)
                out(last - 1)

            matrices(B_PA, B_WO, lambda b: out_pa(b) if b < B_PM else out_pm(b))
            turn_lo(dve, 2, t2hi, t2lo, None)
            matrices(B_WO, B_PQ, out_wo)
            norm_dve(dve, 1, R2, R0)
            turn_lo(dve, 3, t1hi, t1lo, n2)
            matrices(B_PQ, B_END, out_pq)

            done = [0]

            def step(ins):
                done[0] += 1
                ins.then_inc(route, 1)
                dve.wait_ge(route, done[0])

            def top16(rows):
                for v, tv_, _ in rows:
                    ins = dve.max(tv_[:, 0:8], v)
                step(ins)
                for v, tv_, ti_ in rows:
                    ins = dve.max_index(ti_[:, 0:8], tv_[:, 0:8], v)
                step(ins)
                for v, tv_, _ in rows:
                    ins = dve.match_replace(v, tv_[:, 0:8], v, NEG)
                step(ins)
                for v, tv_, _ in rows:
                    ins = dve.max(tv_[:, 8:16], v)
                step(ins)
                for v, tv_, ti_ in rows:
                    ins = dve.max_index(ti_[:, 8:16], tv_[:, 8:16], v)
                step(ins)

            dve.wait_ge(iota_set, 2)
            for n in range(PH):
                dve.wait_ge(score_sb, n + 1)
                top16([(sc[:, tt, 2 * n + c, :], tv[:, tt, 2 * n + c, :], ti[:, tt, 2 * n + c, :])
                       for tt in range(TT) for c in range(2)])
            step(dve.tensor_copy(tif[:], ti[:]))
            for tt in range(TT):
                v = tv[:, tt, :, :].rearrange("p (h c) k -> p h c k", c=2)
                ins = dve.tensor_tensor(cand[:, tt].rearrange("p h (a b) -> p h a b", a=TOP),
                                        v[:, :, 0, :].unsqueeze(3).to_broadcast([P, PH, TOP, TOP]),
                                        v[:, :, 1, :].unsqueeze(2).to_broadcast([P, PH, TOP, TOP]), ALU.add)
            step(ins)
            for tt in range(TT):
                top16([(cand[:, tt, h, :], bv[:, tt, h, :], bi[:, tt, h, :]) for h in range(PH)])
            step(dve.tensor_copy(gsum[:, 0], bv[:, :, :, 0]))
            dve.tensor_tensor(bv[:], bv[:], gsum[:, 0].unsqueeze(3).to_broadcast([P, TT, PH, TOP]), ALU.subtract
                              ).then_inc(best_sub, 1)
            flat = bi[:].rearrange("p a h k -> p a (h k)")
            dve.tensor_scalar(ba[:, 0], flat, 4, None, ALU.logical_shift_right)
            step(dve.tensor_scalar(ba[:, 1], flat, TOP - 1, None, ALU.bitwise_and))
            step(dve.tensor_copy(baf[:], ba[:]))
            for c in range(2):
                for tt in range(TT):
                    e = eq[:, tt]
                    ins = dve.tensor_tensor(e, baf[:, c, tt].unsqueeze(2).to_broadcast([P, PH * TOP, TOP]),
                                            iota[:, 0:TOP].unsqueeze(1).to_broadcast([P, PH * TOP, TOP]), ALU.is_equal)
                step(ins)
                for tt in range(TT):
                    e = eq[:, tt].rearrange("p (h k) a -> p h k a", h=PH)
                    side = tif[:, tt].rearrange("p (h c) k -> p h c k", c=2)[:, :, c, :]
                    ins = dve.tensor_tensor(e, e, side.unsqueeze(2).to_broadcast([P, PH, TOP, TOP]), ALU.mult)
                step(ins)
                for tt in range(TT):
                    ins = dve.tensor_reduce(hk[:, c, tt], eq[:, tt], AX.X, ALU.add)
                step(ins)
            dve.wait_ge(best_exp, 1)
            step(dve.tensor_reduce(gsum[:, 0], bv[:], AX.X, ALU.add))
            step(dve.reciprocal(gsum[:, 1], gsum[:, 0]))
            dve.tensor_tensor(hk[:, 2].rearrange("p a (h k) -> p a h k", h=PH), bv[:],
                              gsum[:, 1].unsqueeze(3).to_broadcast([P, TT, PH, TOP]), ALU.mult).then_inc(hk_ready, 1)
            for n in range(3):
                dve.wait_ge(hk_turned, n + 1)
                dve.tensor_copy(hkT[:, n, :], PS[:, 4 + n, 0:T]).then_inc(hkT_sb, 1)

            dve.wait_ge(hkT_sb, 3)

            def onehot(t, k, first):
                if not first:
                    dve.wait_ge(g_mm, t - 1)
                at = bass.ds(t, 1)
                dve.tensor_scalar(oha[:, k % 2, :], iota[:], hkT[:, 0, at], hkT[:, 2, at], ALU.is_equal, ALU.mult)
                dve.tensor_scalar(ohb[:, k % 2, :], iota[:], hkT[:, 1, at], None, ALU.is_equal).then_inc(onehots, 1)

            onehot(0, 0, True)
            onehot(1, 1, True)
            with dve.Fori(1, T // 2) as i:
                onehot(i * 2, 0, False)
                onehot(i * 2 + 1, 1, False)

            dve.wait_ge(g_out, T // 4)

            def gate_chunk(c, k):
                dve.wait_ge(gelu_done, c + 1)
                gc = g[:, bass.ds(c, 1), :].rearrange("p a t -> p (a t)")
                dve.tensor_tensor(gc, gel[:, k % 2, :], gc, ALU.mult).then_inc(w_made, 1)

            def u_body(i, lag):
                for k in range(CPB):
                    for j in range(CU):
                        n = CU * k + j
                        lo_unit(dve, i * (CPB * CU) + (U_U + n), n)
                    if lag or k >= 2:
                        gate_chunk(i * CPB + (k - 2), k - 2 + CPB)

            u_body(0, False)
            with dve.Fori(1, PK // CPB) as i:
                u_body(i, True)
            for c in (PK - 2, PK - 1):
                gate_chunk(c, c)

            def v_body(i):
                for k in range(CPB):
                    c = i * CPB + k
                    dve.wait_ge(wch_hi, c + 1)
                    dve.tensor_tensor(t1lo[:, k, :], g[:, bass.ds(c, 1), :].rearrange("p a t -> p (a t)"),
                                      t1hi[:, k, :].bitcast(F32), ALU.subtract).then_inc(wch_lo, 1)
                    for j in range(CU):
                        n = CU * k + j
                        lo_unit(dve, i * (CPB * CU) + (U_V + n), n)

            with dve.Fori(0, PK // CPB) as i:
                v_body(i)

            dve.wait_ge(unit_used, UNITS)
            dve.wait_ge(x2_in, 16 * TT)
            for tt in range(TT):
                dve.tensor_tensor(g[:, 8 * tt:8 * tt + 8, :].rearrange("p k t -> p (k t)"),
                                  PS[:, 4 * tt:4 * tt + 4, :].rearrange("p b n -> p (b n)"), x2_back[tt], ALU.add
                                  ).then_inc(y_out, 1)


def lay_out(inputs):
    a = {k: np.asarray(v) for k, v in inputs.items()}
    w = a["w_in"][0]
    cut = np.cumsum([0, 1024, 1024, 2048, 2048, 8, 8, 2048, 256, 256, 2048, 2048])
    qm, km, vm, om, im, fm, qa, ka, va, gm, ga = (w[:, cut[i]:cut[i + 1]] for i in range(11))

    def blocks(m):
        n = m.shape[1] // BLK
        return m.reshape(BU, 2, P, n, BLK).transpose(3, 0, 2, 1, 4).reshape(n * BU, P, UW)

    u = a["expert_u"][0].reshape(PK, PK, CU, UW // P, P)
    u = u.transpose(1, 2, 4, 3, 0).reshape(PK * CU, P, UW)
    v = a["expert_v"][0].reshape(PK, PK, CU, UW).transpose(1, 2, 0, 3).reshape(PK * CU, P, UW)
    units = np.concatenate([blocks(m) for m in (ka_va(ka, va), qm, km, vm, qa, om, gm, ga, a["w_proj_a"][0],
                                                a["w_proj_m"][0], a["w_out"][0], a["w_peer_q"][0])] + [u, v])

    def column(x):
        return np.ascontiguousarray(x.reshape(KC, P).T)

    def rep(x, n):
        return np.ascontiguousarray(np.broadcast_to(x, (n,) + x.shape))

    x = a["x"][0].reshape(TT, P, D).transpose(1, 0, 2)
    wi = np.concatenate([im, fm], axis=1).reshape(KC, P, 16).transpose(1, 0, 2)
    sinks = np.repeat(a["sinks"][0].reshape(KC, 2).T, CH, axis=0)
    qk = np.stack([np.tile(a["q_norm_w"][0], 2), np.tile(a["k_norm_w"][0], 2)], axis=1)
    return {
        "units": units,
        "w_if": wi,
        "x": x,
        "norm1": column(a["norm1_w"][0]),
        "norm2": column(a["norm2_w"][0]),
        "conv_w": a["conv_w"][0].reshape(4, KC, P).transpose(2, 1, 0),
        "if_bias": rep(np.concatenate([a["b_igate"][0], a["b_fgate"][0]]), P),
        "mnorm": column(np.tile(a["mlstm_norm_w"][0], MH)),
        "qk_w": qk,
        "sinks": sinks,
        "subk": a["sub_keys"][0].transpose(2, 0, 1),
    }


def ka_va(ka, va):
    return np.concatenate([ka, va], axis=1)


def kernel(**inputs):
    import concourse.bacc as _bacc
    from concourse.bass_utils import run_bass_kernel_spmd as _run

    nc = _bacc.Bacc("TRN2", target_bir_lowering=False, num_devices=1)
    arrays, args = {}, []
    for name, v in lay_out(inputs).items():
        v = np.ascontiguousarray(v)
        arrays[f"in_{name}"] = v
        args.append(nc.dram_tensor(f"in_{name}", v.shape, F32, kind="ExternalInput").ap())
    out = nc.dram_tensor("out", (P, TT, D), F32, kind="ExternalOutput").ap()
    gates = nc.dram_tensor("gates_spill", (B_GATE, P, TT * BLK), F32, kind="Internal").ap()
    x2 = nc.dram_tensor("x2_spill", (P, TT, D), F32, kind="Internal").ap()
    block_program(nc, *args, out, gates, x2)
    r = _run(nc, [arrays], core_ids=[0])
    return np.ascontiguousarray(r.results[0]["out"].transpose(1, 0, 2)).reshape(1, T, D)
```

```python
from contextlib import ExitStack

import numpy as np
import concourse.bass as bass
from concourse import mybir

F32 = mybir.dt.float32
R32 = mybir.dt.float32r
U32 = mybir.dt.uint32
I32 = mybir.dt.int32
ALU = mybir.AluOpType
ACT = mybir.ActivationFunctionType
AX = mybir.AxisListType

P = 128
T = 256
D = 2048
TT = T // P
KC = D // P
EPS = 1e-6
BLK = 512
UW = 1024
BU = D * BLK // P // UW
RAW, HI, LO = 4, 4, 2

MH, MV = 8, 256
AH, KVH, DH, CH = 32, 4, 64, 64
NCH = T // CH
PAIRS = AH // KVH // 2
PH, PK, TOP = 8, 128, 16

B_BIG = 12
B_GATE = 12
B_IN = 1 + B_BIG + B_GATE
B_MAT = D // BLK
B_PA, B_PM, B_WO, B_PQ = (B_IN + B_MAT * i for i in range(4))
B_END = B_PQ + B_MAT
U_U = B_END * BU
CU = P * D // P // UW
CPB = 4
U_V = U_U + PK * CU
EXP_BODY = 11
UNITS = U_V + PK * CU
C_G = 60
TPC = 4
NEG = -1.0e30

B_FIX = 1 + B_BIG
K_GATES, K_CONV, K_RMS, K_QK, K_ATT, K_MLSTM = 0, 0, 12, 32, 43, 61
K_HNORM = K_MLSTM + 2 * MH + 1
K_GATED = K_HNORM + 7
N_ITEM = KVH * NCH


def tick_of(b, k=0):
    return (b - B_FIX) * BU + k


K_HM = tick_of(B_PA)
K_X2 = tick_of(B_PQ) - 1


def block_program(nc, units, w_if, x_d, norm1, norm2, conv_w, if_bias, mnorm, qk_w, sinks, subk_d,
                  out_d, gates_d, x2_d, gel_d):
    with ExitStack() as ctx:
        def sem(name):
            return ctx.enter_context(nc.semaphore(name))

        def sb(stack, name, shape, dt=F32):
            return stack.enter_context(nc.sbuf_tensor(name, shape, dt))

        raw = sb(ctx, "raw", [P, RAW, UW])
        whi = sb(ctx, "whi", [P, HI, UW], R32)
        wlo = sb(ctx, "wlo", [P, LO, UW], R32)
        t1hi = sb(ctx, "t1hi", [P, KC, T], R32)
        t1lo = sb(ctx, "t1lo", [P, KC, T], R32)
        ident = sb(ctx, "ident", [P, P])
        small = sb(ctx, "small", [P, 8 + TOP + 8])
        eps_t, ss, sd, rs = small[:, 0:1], small[:, 2:4], small[:, 4:6], small[:, 6:8]
        iota16 = small[:, 8:8 + TOP]
        ss_blk = small[:, 8 + TOP:].rearrange("p (a b) -> p a b", a=TT)

        with ExitStack() as p1:
            t2hi = sb(p1, "t2hi", [P, KC, T], R32)
            t2lo = sb(p1, "t2lo", [P, KC, T], R32)
            big = sb(p1, "big", [P, TT, B_BIG * BLK])
            kv = sb(p1, "kv", [P, TT, BLK])
            bt = sb(p1, "bt", [P, KC, T])
            stage = sb(p1, "stage", [P, 2, TT * BLK])
            stage4 = sb(p1, "stage4", [P, 2, TT * BLK])
            n1 = sb(p1, "n1", [P, KC])
            n2 = sb(p1, "n2", [P, KC])
            cw = sb(p1, "cw", [P, KC, 4])
            ifb = sb(p1, "ifb", [P, 16])
            mw = sb(p1, "mw", [P, KC])
            qkw = sb(p1, "qkw", [P, 2])
            sink = sb(p1, "sink", [P, KC])
            gt = sb(p1, "gt", [P, 8, TT, 16])
            qs = sb(p1, "qs", [P, 3, TT, 36])
            ast = sb(p1, "ast", [P, 2, 7, PAIRS])
            hs = sb(p1, "hs", [P, 3, TT, MH])
            hd = sb(p1, "hd", [P, 2, 2, TT])
            ones = sb(p1, "ones", [P, 2])
            mrow = sb(p1, "mrow", [MH, 3, T])
            tri = sb(p1, "tri", [P, T])
            mask = sb(p1, "mask", [P, T])
            with ExitStack() as pa:
                kte = sb(pa, "kte", [P, KVH, T])
                kto = sb(pa, "kto", [P, KVH, T])
                vb2 = sb(pa, "vb2", [P, KVH * DH])
            with ExitStack() as pm:
                wg = sb(pm, "wg", [P, KC, 16])
                wghi = sb(pm, "wghi", [P, KC, 16], R32)
                wglo = sb(pm, "wglo", [P, KC, 16], R32)
        sqj = [s[:].rearrange("p a b -> p (a b)") for s in (stage, stage4)]
        x2sq = [j[:, n * BLK:(n + 1) * BLK] for j in sqj for n in range(4)]
        qsq = stage4[:, 0, :]
        kd = stage4[:, 0, :].rearrange("p (t g r d) -> p t g r d", t=TT, g=KVH, r=2)
        hsq = stage4[:, 0, :].rearrange("p (s n) -> p s n", n=MV)
        gate_out = stage4[:, 1, :].rearrange("p (a n) -> p a n", a=TT)
        ksq = kto[:, 0:2, :]
        prob = stage[:, 0, :].rearrange("p (b j n) -> p b j n", b=2, j=PAIRS)
        probT = stage[:, 1, :].rearrange("p (b j n) -> p b j n", b=2, j=PAIRS)
        ee = stage[:, 0, 0:6 * P].rearrange("p (b n) -> p b n", b=2)
        pp = stage[:, 1, 0:6 * P].rearrange("p (b n) -> p b n", b=2)
        R0, R1, R2 = (big[:, :, i * D:(i + 1) * D] for i in range(3))
        o_sb = bt[:].rearrange("p k t -> p (k t)").rearrange("p (a n) -> p a n", a=TT)

        def qT_of(kc):
            return big[:, kc // 8, kc % 8 * T:(kc % 8 + 1) * T]

        with ExitStack() as q0:
            qp = sb(q0, "qp", [P, TT, D])
            qT = sb(q0, "qT", [P, 2 * PH, T])
            sc = sb(q0, "sc", [P, TT, 2 * PH, PK])
            subk = sb(q0, "subk", [P, 2, PK])
            tv = sb(q0, "tv", [P, TT, 2 * PH, TOP])
            ti = sb(q0, "ti", [P, TT, 2 * PH, TOP], U32)
            tif = sb(q0, "tif", [P, TT, 2 * PH, TOP])
            cand = sb(q0, "cand", [P, TT, PH, TOP * TOP])
            bv = sb(q0, "bv", [P, TT, PH, TOP])
            bi = sb(q0, "bi", [P, TT, PH, TOP], U32)
            ba = sb(q0, "ba", [P, 2, TT, PH * TOP], U32)
            baf = sb(q0, "baf", [P, 2, TT, PH * TOP])
            eq = sb(q0, "eq", [P, TT, PH * TOP, TOP])
            hk = sb(q0, "hk", [P, 3, TT, PH * TOP])
            gsum = sb(q0, "gsum", [P, 2, TT, PH])
        g = sb(ctx, "g", [P, PK, T])
        hkT = sb(ctx, "hkT", [P, 3, T])
        iota = ident
        gel = sb(ctx, "gel", [P, 2, T])
        with ExitStack() as q2:
            oha = sb(q2, "oha", [P, 2, P])
            ohb = sb(q2, "ohb", [P, 2, P])
        with ExitStack() as q3:
            gback = sb(q3, "gback", [P, 2, T])
        v_lo = [wlo[:, 0, :], wlo[:, 1, :]] + [t[:, CPB:2 * CPB, :].rearrange("p k t -> p (k t)")
                                                for t in (t1hi, t1lo)]
        x2_back = [t[:, KC // 2:KC, :].rearrange("p k t -> p (k t)").bitcast(F32) for t in (t1hi, t1lo)]
        PS = ctx.enter_context(nc.psum_tensor("PS", [P, 8, BLK], F32))

        pre, fab, fexp, fln, fmin = (gt[:, i, :, :] for i in range(5))
        logf, a_in, bsum = gt[:, 5, :, 0:8], gt[:, 5, :, 8:16], gt[:, 6, :, 0:8]
        mt, expnm = gt[:, 6, :, 8:16], gt[:, 7, :, 0:8]
        mfin = mrow[:, 2, :]

        raw_landed = [sem(f"raw_landed{i}") for i in range(RAW)]
        hi_made, lo_made, unit_used = sem("hi_made"), sem("lo_made"), sem("unit_used")
        block_out = sem("block_out")
        consts, eps_set, iota_set = sem("consts"), sem("eps_set"), sem("iota_set")
        x_in = [sem("x_in0"), sem("x_in1")]
        w_small, wif_in, subk_in = sem("w_small"), sem("wif_in"), sem("subk_in")
        gate_sb, conv_first = sem("gate_sb"), sem("conv_first")
        gate_stored = [sem("gate_stored0"), sem("gate_stored1")]
        o_in, ga_in, gm_in, xr_in = sem("o_in"), sem("ga_in"), sem("gm_in"), sem("xr_in")
        x2_stored, x2_in, out_stored = sem("x2_stored"), sem("x2_in"), sem("out_stored")
        n_sq, n_root, n_rs, n_scaled = sem("n_sq"), sem("n_root"), sem("n_rs"), sem("n_scaled")
        turned, t_hi, t_lo = sem("turned"), sem("t_hi"), sem("t_lo")
        x2_sum = sem("x2_sum")
        wg_hi, wg_lo, if_mm, if_sb = sem("wg_hi"), sem("wg_lo"), sem("if_mm"), sem("if_sb")
        gate_act, f_min, logf_s, b_mm, b_sb, a_s = (sem("gate_act"), sem("f_min"), sem("logf_s"), sem("b_mm"),
                                                    sem("b_sb"), sem("a_s"))
        at_mm, m_step, mt_mm, mt_s, expnm_s = sem("at_mm"), sem("m_step"), sem("mt_mm"), sem("mt_s"), sem("expnm_s")
        qk_turned, conv_step, conv_done, sig_done, silu_done = (
            sem("qk_turned"), sem("conv_step"), sem("conv_done"), sem("sig_done"), sem("silu_done"))
        q_sq, q_sum, q_root, q_rs, q_scaled = sem("q_sq"), sem("q_sum"), sem("q_root"), sem("q_rs"), sem("q_scaled")
        k_zero, q_turned, q_out, vb2_s = sem("k_zero"), sem("q_turned"), sem("q_out"), sem("vb2_s")
        st_peak, st_sum, st_rec = sem("st_peak"), sem("st_sum"), sem("st_rec")
        logits_s, st_step, st_max, prob_exp, prob_norm = (
            sem("logits_s"), sem("st_step"), sem("st_max"), sem("prob_exp"), sem("prob_norm"))
        prob_turned, probT_sb, av_mm, av_hi, av_lo = (
            sem("prob_turned"), sem("probT_sb"), sem("av_mm"), sem("av_hi"), sem("av_lo"))
        ms_mm, ms_arg, ms_exp, ms_p, mn_mm, mn_step, h_out, h_sq = (
            sem("ms_mm"), sem("ms_arg"), sem("ms_exp"), sem("ms_p"), sem("mn_mm"), sem("mn_step"),
            sem("h_out"), sem("h_sq"))
        h_root, h_rs, h_gated, y_add = (sem("h_root"), sem("h_rs"), sem("h_gated"), sem("y_add"))
        qp_turned, qT_sb, score_mm, score_sb = sem("qp_turned"), sem("qT_sb"), sem("score_mm"), sem("score_sb")
        route, best_sub, best_exp, hk_turned, hkT_sb = (
            sem("route"), sem("best_sub"), sem("best_exp"), sem("hk_turned"), sem("hkT_sb"))
        hk_ready = sem("hk_ready")
        onehots, g_mm, g_out = sem("onehots"), sem("g_mm"), sem("g_out")
        gelu_done, w_made = sem("gelu_done"), sem("w_made")
        gel_stored = [sem("gel_stored0"), sem("gel_stored1")]
        gel_back = [sem("gel_back0"), sem("gel_back1")]
        wch_hi, wch_lo = sem("wch_hi"), sem("wch_lo")
        y_out = sem("y_out")
        block = ctx.enter_context(nc.Block())

        def load_unit(sp, u, k, first=False):
            if not first:
                sp.wait_ge(lo_made, u - RAW + 1)
            sp.dma_start(raw[:, k % RAW, :], units[bass.ds(u, 1), :, :].rearrange("a p n -> p (a n)")
                         ).then_inc(raw_landed[k % RAW], 16)

        def hi_unit(act, u, k, landed):
            act.wait_ge(raw_landed[k % RAW], landed)
            if not (isinstance(u, int) and u < HI):
                act.wait_ge(unit_used, u - HI + 1)
            act.activation(whi[:, k % HI, :], raw[:, k % RAW, :], ACT.Copy).then_inc(hi_made, 1)

        def lo_unit(dve, u, k):
            dve.wait_ge(hi_made, u + 1)
            if not (isinstance(u, int) and u < LO):
                dve.wait_ge(unit_used, u - LO + 1)
            dve.tensor_tensor(wlo[:, k % LO, :], raw[:, k % RAW, :], whi[:, k % HI, :].bitcast(F32),
                              ALU.subtract).then_inc(lo_made, 1)

        def hi_fix(act, u):
            hi_unit(act, u, u, (u // RAW + 1) * 16)

        def hi_block(act, b, evacuate=None):
            for k in range(BU):
                hi_unit(act, b * BU + k, k, b * (BU // RAW * 16) + (k // RAW + 1) * 16)
                if k == HI - 1 and evacuate is not None:
                    evacuate()

        def lo_block(dve, b):
            for k in range(BU):
                lo_unit(dve, b * BU + k, k)

        def mm_block(pe, b, odd, thi, tlo, after=None, ready=None):
            if not (isinstance(b, int) and b < 2):
                pe.wait_ge(block_out, b - 1)
            for k in range(BU):
                pe.wait_ge(lo_made, b * BU + k + 1)
                if ready is not None:
                    pe.wait_ge(t_lo, ready + 2 * k + 2)
                for kk in range(2):
                    kc = 2 * k + kk
                    vh = whi[:, k % HI, kk * BLK:(kk + 1) * BLK]
                    vl = wlo[:, k % LO, kk * BLK:(kk + 1) * BLK]
                    for tt in range(TT):
                        o = PS[:, 2 * odd + tt, :]
                        sh, sl = thi[:, kc, tt * P:(tt + 1) * P], tlo[:, kc, tt * P:(tt + 1) * P]
                        pe.matmul(o, sh, vh, start=(kc == 0), stop=False)
                        pe.matmul(o, sh, vl, start=False, stop=False)
                        mm = pe.matmul(o, sl, vh, start=False, stop=(kc == KC - 1))
                mm.then_inc(unit_used, 1)
                if after is not None:
                    after(k)

        def turn(pe, n, kc, src):
            if n or kc >= 4:
                pe.wait_ge(t_lo, KC * n + kc - 3)
            for tt in range(TT):
                mm = pe.transpose(PS[:, 4 + kc % 4, tt * P:(tt + 1) * P], src[:, tt, kc * P:(kc + 1) * P], ident[:])
            mm.then_inc(turned, 1)

        def turn_hi(act, n, kc, thi, w):
            act.wait_ge(turned, KC * n + kc + 1)
            act.activation(thi[:, kc, :], PS[:, 4 + kc % 4, 0:T], ACT.Copy,
                           scale=(1.0 if w is None else w[:, kc:kc + 1])).then_inc(t_hi, 1)

        def turn_lo(dve, n, kc, thi, tlo, w):
            dve.wait_ge(t_hi, KC * n + kc + 1)
            dve.scalar_tensor_tensor(tlo[:, kc, :], PS[:, 4 + kc % 4, 0:T],
                                     1.0 if w is None else w[:, kc:kc + 1],
                                     thi[:, kc, :].bitcast(F32), ALU.mult, ALU.subtract).then_inc(t_lo, 1)

        def norm_root(act, m):
            act.activation(sd, ss, ACT.Sqrt, scale=1.0 / D, bias=eps_t).then_inc(n_root, 1)

        def norm_rs(dve, m):
            dve.wait_ge(n_root, m + 1)
            dve.reciprocal(rs, sd).then_inc(n_rs, 1)
            dve.wait_ge(n_rs, m + 1)

        def norm_scale(dve, xin, out, q):
            for tt in range(TT):
                dve.tensor_scalar(out[:, tt, q * BLK:(q + 1) * BLK], xin[:, tt, q * BLK:(q + 1) * BLK],
                                  rs[:, tt:tt + 1], None, ALU.mult).then_inc(n_scaled, 1)

        def norm_tiles(k):
            return range(4) if k == -1 else range(2 * k + 4, 2 * k + 6) if 0 <= k < KC // 2 - 2 else ()

        def norm_turn(pe, m, n, src, k):
            for kc in norm_tiles(k):
                pe.wait_ge(n_scaled, TT * (4 * m + kc // 4 + 1))
                turn(pe, n, kc, src)

        def norm_hi(act, n, thi, w, k):
            for kc in norm_tiles(k):
                turn_hi(act, n, kc, thi, w)

        def norm_lo(dve, n, thi, tlo, w, k):
            for kc in (norm_tiles(-1) if k == -1 else norm_tiles(k - 1) if k > 0 else ()):
                turn_lo(dve, n, kc, thi, tlo, w)

        def window(c):
            return {0: [(0, 0, CH)], 1: [(0, 0, P)], 2: [(0, P, P + CH), (CH, CH, P)], 3: [(0, CH * 2, T)]}[c]

        def keys_of(c):
            return CH if c == 0 else P

        def y_tile(t):
            b, k = B_FIX + t // BU, t % BU
            return 4 * (b - B_PM - 1) + k - 1 if B_PM < b <= B_WO and 1 <= k <= 4 else None

        def mden(b):
            return PS[:, 5, 3 * P + TT * b:3 * P + TT * (b + 1)]

        @block.sync
        def _(sp):
            for tt in range(TT):
                sp.dma_start(R2[:, tt, :], x_d[:, tt, :]).then_inc(x_in[tt], 16)
            for u in range(RAW):
                load_unit(sp, u, u, first=True)
            with sp.Fori(1, U_U // RAW) as i:
                for k in range(RAW):
                    load_unit(sp, i * RAW + k, k)

            def store_gelu(c, k):
                sp.wait_ge(gelu_done, c + 1)
                sp.dma_start(gel_d[bass.ds(c, 1), :, :].rearrange("a p t -> p (a t)"), gel[:, k % 2, :]
                             ).then_inc(gel_stored[k % 2], 16)

            def u_body(i, first):
                for k in range(CPB):
                    for j in range(CU):
                        n = CU * k + j
                        load_unit(sp, i * (CPB * CU) + (U_U + n), n)
                    if not first:
                        store_gelu(i * CPB - CPB + k, k)

            u_body(0, True)
            with sp.Fori(1, PK // CPB) as i:
                u_body(i, False)

            def load_gelu(c, k):
                if isinstance(c, int) and c < CPB + 1:
                    sp.wait_ge(gel_stored[k % 2], (c // 2 + 1) * 16)
                if isinstance(c, int) and c < 2:
                    sp.wait_ge(g_mm, T)
                else:
                    sp.wait_ge(w_made, c - 1)
                sp.dma_start(gback[:, k % 2, :], gel_d[bass.ds(c, 1), :, :].rearrange("a p t -> p (a t)")
                             ).then_inc(gel_back[k % 2], 16)

            def v_body(i, first, last):
                for k in range(CPB):
                    for j in range(CU):
                        n = CU * k + j
                        load_unit(sp, i * (CPB * CU) + (U_V + n), n)
                    if first and k < CPB:
                        store_gelu(PK - CPB + k, k)
                    if not (last and k == CPB - 1):
                        load_gelu(i * CPB + (k + 1), k + 1)

            load_gelu(0, 0)
            v_body(0, True, False)
            for st in gel_stored:
                sp.wait_ge(st, PK // 2 * 16)
            with sp.Fori(1, PK // CPB - 1) as i:
                v_body(i, False, False)
            v_body(PK // CPB - 1, False, True)

        @block.gpsimd
        def _(pool):
            for dst, src in ((n1, norm1), (n2, norm2), (cw, conv_w), (ifb, if_bias), (mw, mnorm), (qkw, qk_w),
                             (sink, sinks)):
                pool.dma_start(dst[:], src).then_inc(w_small, 16)
            pool.dma_start(wg[:], w_if).then_inc(wif_in, 16)
            pool.memset(small[:, 0:8], EPS).then_inc(eps_set, 1)
            pool.memset(ones[:], 1.0).then_inc(consts, 1)
            pool.memset(ident[:], 0.0).then_inc(consts, 1)
            pool.memset(tri[:], 1.0).then_inc(consts, 1)
            pool.memset(mask[:], 0.0).then_inc(consts, 1)
            pool.iota(iota16, pattern=[[1, TOP]], base=0, channel_multiplier=0,
                      allow_small_or_imprecise_dtypes=True).then_inc(iota_set, 1)
            pool.wait_ge(consts, 4)
            pool.affine_select(out=ident[:], in_=ident[:], compare_op=ALU.not_equal, fill=1.0, base=0,
                               pattern=[[-1, P]], channel_multiplier=1).then_inc(consts, 1)
            pool.affine_select(out=tri[:], in_=tri[:], compare_op=ALU.is_ge, fill=0.0, base=0,
                               pattern=[[1, T]], channel_multiplier=-1).then_inc(consts, 1)
            pool.affine_select(out=mask[:], in_=mask[:], compare_op=ALU.is_ge, fill=NEG, base=0,
                               pattern=[[1, T]], channel_multiplier=-1).then_inc(consts, 1)
            def gates_away(first, last):
                for n in range(first, last):
                    for tt in range(TT):
                        if tt == 0:
                            pool.wait_ge(gate_sb, n + 1)
                        else:
                            pool.wait_ge(block_out, B_FIX + n + 1)
                        pool.dma_start(gates_d[n, :, tt * BLK:(tt + 1) * BLK], gate_out[:, tt, :]
                                       ).then_inc(gate_stored[tt], 16)

            def gates_back(dst, first, s):
                for st in gate_stored:
                    pool.wait_ge(st, 16 * (first + B_MAT))
                for n in range(B_MAT):
                    pool.dma_start(dst[:, :, n * BLK:(n + 1) * BLK],
                                   gates_d[first + n].rearrange("p (a n) -> p a n", a=TT)).then_inc(s, 16)

            gates_away(0, 2 * B_MAT)
            pool.wait_ge(av_lo, N_ITEM)
            gates_back(R0, B_MAT, ga_in)
            gates_away(2 * B_MAT, 2 * B_MAT + 1)
            pool.wait_ge(mn_mm, MH)
            gates_back(o_sb, 0, o_in)
            gates_away(2 * B_MAT + 1, B_GATE)
            gates_back(R1, 2 * B_MAT, gm_in)
            pool.wait_ge(turned, 2 * KC)
            pool.dma_start(R2, x_d).then_inc(xr_in, 16)
            pool.wait_ge(block_out, B_WO + B_MAT)
            pool.dma_start(x2_d, R2).then_inc(x2_stored, 16)
            pool.wait_ge(x2_stored, 16)
            pool.wait_ge(t_lo, 4 * KC)
            pool.dma_start(subk[:], subk_d).then_inc(subk_in, 16)
            pool.wait_ge(hk_turned, 3)
            pool.iota(iota[:], pattern=[[1, P]], base=0, channel_multiplier=0,
                      allow_small_or_imprecise_dtypes=True).then_inc(iota_set, 1)
            pool.wait_ge(unit_used, U_V)
            for tt in range(TT):
                pool.dma_start(x2_back[tt], x2_d[:, tt, :]).then_inc(x2_in, 16)
            for tt in range(TT):
                pool.wait_ge(y_out, tt + 1)
                pool.dma_start(out_d[:, tt, :], g[:, 8 * tt:8 * tt + 8, :].rearrange("p k t -> p (k t)")
                               ).then_inc(out_stored, 16)
            pool.wait_ge(out_stored, 16 * TT)

        @block.scalar
        def _(act):
            act.wait_ge(eps_set, 1)
            for tt in range(TT):
                act.wait_ge(x_in[tt], 16)
                act.activation(sqj[tt], R2[:, tt, :], ACT.Square, accum_out=ss[:, tt:tt + 1]).then_inc(n_sq, 1)
            act.wait_ge(n_sq, TT)
            norm_root(act, 0)
            act.wait_ge(w_small, 7 * 16)
            for k in range(-1, BU):
                if k == -1:
                    for u in range(HI - 1):
                        hi_fix(act, u)
                elif k + HI - 1 < BU:
                    hi_fix(act, k + HI - 1)
                norm_hi(act, 0, t1hi, n1, k)
            act.wait_ge(wif_in, 16)
            act.activation(wghi[:], wg[:], ACT.Copy).then_inc(wg_hi, 1)

            def out_kv():
                act.activation(kv[:], PS[:, 0:TT, :], ACT.Copy).then_inc(block_out, 1)

            def out_big(b, odd):
                act.activation(big[:, :, bass.ds((b - 1) * BLK, BLK)], PS[:, 2 * odd:2 * odd + TT, :], ACT.Copy
                               ).then_inc(block_out, 1)

            def out_gate(b):
                n = b - B_FIX
                for tt in range(TT):
                    if n:
                        act.wait_ge(gate_stored[tt], 16 * n)
                    act.activation(gate_out[:, tt, :], PS[:, 2 * (b % 2) + tt, :], ACT.Sigmoid
                                   ).then_inc(gate_sb if tt == 0 else block_out, 1)

            hi_block(act, 1, out_kv)
            with act.Fori(1, B_BIG // 2) as i:
                hi_block(act, i * 2, lambda: out_big(i * 2 - 1, 1))
                hi_block(act, i * 2 + 1, lambda: out_big(i * 2, 0))
            hi_block(act, B_BIG, lambda: out_big(B_BIG - 1, 1))

            def tick(t):
                if t % BU == 0 and t <= tick_of(B_IN):
                    b = B_FIX - 1 + t // BU
                    out_big(b, b % 2) if b < B_FIX else out_gate(b)

                if t == K_GATES + 2:
                    act.wait_ge(consts, 7)
                    act.wait_ge(if_sb, 1)
                    act.activation(fab, pre, ACT.Abs).then_inc(gate_act, 1)
                    act.wait_ge(gate_act, 1)
                    act.activation(fexp, fab, ACT.Exp, scale=-1.0).then_inc(gate_act, 1)
                    act.wait_ge(gate_act, 2)
                    act.activation(fln, fexp, ACT.Ln, bias=ones[:, 0:1]).then_inc(gate_act, 1)
                if t == K_GATES + 10:
                    act.wait_ge(mt_s, 1)
                    act.activation(expnm, mt, ACT.Exp, scale=-1.0).then_inc(expnm_s, 1)

                n = t - K_CONV
                if n % 2 == 0 and n // 2 < KC:
                    n //= 2
                    act.wait_ge(qk_turned, n + 1)
                    act.activation(bt[:, n, :], PS[:, 4 + n % 2, 0:T], ACT.Copy, scale=cw[:, n, 3:4]
                                   ).then_inc(conv_first, 1)
                n = t - K_CONV - 8
                if n % 8 == 0 and 0 <= n // 8 < 4:
                    n //= 8
                    act.wait_ge(conv_done, 4 * n + 4)
                    if n >= 2:
                        act.wait_ge(silu_done, n - 1)
                    act.activation(stage[:, n % 2, :], bt[:, 4 * n:4 * n + 4, :].rearrange("p k t -> p (k t)"),
                                   ACT.Sigmoid).then_inc(sig_done, 1)

                m = t - K_RMS
                if 0 <= m < 2 * TT:
                    if m == 0:
                        act.wait_ge(block_out, B_FIX)
                    else:
                        act.wait_ge(q_sum, m)
                    act.activation(qsq, R2[:, m // 2, m % 2 * UW:(m % 2 + 1) * UW], ACT.Square).then_inc(q_sq, 1)
                if m == 2 * TT:
                    act.wait_ge(if_sb, 1)
                    act.activation(ksq, kv[:, :, 0:T], ACT.Square).then_inc(q_sq, 1)
                if m == 2 * TT + 1:
                    act.wait_ge(q_sum, 2 * TT + 1)
                    act.activation(qs[:, 1, :, :], qs[:, 0, :, :], ACT.Sqrt, scale=1.0 / DH, bias=eps_t
                                   ).then_inc(q_root, 1)

                s = t - K_ATT
                if s == 0:
                    act.wait_ge(silu_done, 4)
                if 2 <= s < N_ITEM + 2:
                    i = s - 2
                    gq, c = i // NCH, i % NCH
                    act.wait_ge(av_mm, i + 1)
                    act.activation(t2hi[:, PAIRS * gq:PAIRS * (gq + 1), c * CH:(c + 1) * CH],
                                   PS[:, 7, 0:T].rearrange("p (j l) -> p j l", j=PAIRS), ACT.Copy
                                   ).then_inc(av_hi, 1)
                if 1 <= s <= N_ITEM:
                    i, b = s - 1, (s - 1) % 2
                    act.wait_ge(prob_turned, i + 1)
                    if i >= 2:
                        act.wait_ge(av_mm, i - 1)
                    act.activation(probT[:, b], PS[:, 6, :].rearrange("p (j n) -> p j n", j=PAIRS), ACT.Copy
                                   ).then_inc(probT_sb, 1)
                if 0 <= s < N_ITEM:
                    b, w = s % 2, keys_of(s % NCH)
                    act.wait_ge(st_max, s + 1)
                    if s >= 2:
                        act.wait_ge(prob_turned, s - 1)
                    for j in range(PAIRS):
                        act.activation(prob[:, b, j, 0:w], PS[:, 4 + b, j * P:j * P + w], ACT.Exp,
                                       bias=ast[:, b, 1, j:j + 1], accum_out=ast[:, b, 3, j:j + 1])
                    act.activation(ast[:, b, 4, :], ast[:, b, 2, :], ACT.Exp).then_inc(prob_exp, 1)

                s = t - K_MLSTM
                if s % 2 == 0 and 0 <= s <= 2 * MH:
                    h = s // 2 - 1
                    if h >= 0:
                        act.wait_ge(h_out, h + 1)
                        if h >= 2:
                            act.wait_ge(h_sq, 2 * (h - 1))
                        for tt in range(TT):
                            act.activation(hsq[:, (2 * h + tt) % 4, :], R2[:, tt, h * MV:(h + 1) * MV], ACT.Square,
                                           accum_out=hs[:, 0, tt, h:h + 1]).then_inc(h_sq, 1)
                    h, b = s // 2, s // 2 % 2
                    if h < MH:
                        act.wait_ge(ms_arg, h + 1)
                        act.activation(ee[:, b, 0:T], ee[:, b, 0:T], ACT.Exp, bias=a_in[:, 0, h:h + 1])
                        act.activation(ee[:, b, T:3 * P], ee[:, b, T:3 * P], ACT.Exp, bias=a_in[:, 1, h:h + 1]
                                       ).then_inc(ms_exp, 1)
                if t == K_HNORM:
                    act.wait_ge(h_sq, 2 * MH)
                    act.activation(hs[:, 1], hs[:, 0], ACT.Sqrt, scale=1.0 / MV, bias=eps_t).then_inc(h_root, 1)

                if 0 <= t - K_HM < KC:
                    turn_hi(act, 1, t - K_HM, t1hi, mw)
                if y_tile(t) is not None:
                    turn_hi(act, 2, y_tile(t), t2hi, None)

                n = (t - 1 - tick_of(B_WO + 1)) // BU
                if t == K_X2 or (t % BU == 1 and 0 <= n < B_MAT - 1):
                    n = B_MAT - 1 if t == K_X2 else n
                    act.wait_ge(block_out, B_WO + n + 1)
                    for tt in range(TT):
                        act.activation(x2sq[TT * n + tt], R2[:, tt, n * BLK:(n + 1) * BLK], ACT.Square,
                                       accum_out=ss_blk[:, tt, n:n + 1]).then_inc(n_sq, 1)
                if t == K_X2:
                    act.wait_ge(x2_sum, 1)
                    norm_root(act, 1)
                norm_hi(act, 3, t1hi, n2, t - K_X2 - 1) if t >= K_X2 else None

            for u in range(B_FIX * BU, B_END * BU):
                hi_fix(act, u)
                if u - B_FIX * BU >= HI - 1:
                    tick(u - B_FIX * BU - (HI - 1))

            def qT_copy(n):
                act.wait_ge(qp_turned, n + 1)
                act.activation(qT[:, n, :], PS[:, 4 + n % 4, 0:T], ACT.Copy).then_inc(qT_sb, 1)

            def score_copy(n):
                act.wait_ge(score_mm, n + 1)
                act.activation(sc[:, :, 2 * n:2 * n + 2, :].rearrange("p a c k -> p c a k"),
                               PS[:, 4 + n % 4, :].rearrange("p (c a k) -> p c a k", c=2, a=TT), ACT.Copy
                               ).then_inc(score_sb, 1)

            def gelu_chunk(c, k):
                if not (isinstance(c, int) and c < 2):
                    act.wait_ge(gel_stored[k % 2], (c // 2) * 16 if isinstance(c, int) else c * 8 - (k % 2) * 8)
                act.activation(gel[:, k % 2, :], PS[:, k % 4, 0:T], ACT.Gelu).then_inc(gelu_done, 1)

            def g_copy(c, k):
                act.wait_ge(g_mm, c * TPC - (C_G - 1) * TPC)
                act.activation(g[:, :, bass.ds(c * TPC - C_G * TPC, TPC)].rearrange("p k t -> p t k"),
                               PS[:, 4 + k % 4, :].rearrange("p (t k) -> p t k", t=TPC), ACT.Copy).then_inc(g_out, 1)

            def u_hi(i, n):
                hi_unit(act, i * (CPB * CU) + (U_U + n), n,
                        i * (CPB * CU // RAW * 16) + (U_U // RAW + n // RAW + 1) * 16)

            def u_body(i, first=False, build=(False, False)):
                for k in range(CPB):
                    for j in range(CU):
                        u_hi(i, CU * k + j)
                    if not first or k >= 2:
                        gelu_chunk(i * CPB + (k - 2), k - 2 + CPB)
                    if build[0] if k >= 2 else build[1]:
                        g_copy(i * CPB + (k - 2), k - 2 + CPB)

            n_unit = CPB * CU
            for n in range(2 * n_unit):
                i, k = n // n_unit, n % n_unit // CU
                u_hi(i, n % n_unit)
                if n % CU == CU - 1 and CPB * i + k >= 2:
                    gelu_chunk(i * CPB + k - 2, k - 2 + CPB)
                if 3 <= n < 3 + n_unit:
                    qT_copy(2 * (n - 3))
                    qT_copy(2 * (n - 3) + 1)
                if n >= 3 + n_unit:
                    score_copy(n - 3 - n_unit)
            for n in range(PH - 3, PH):
                u_hi(2, n - (PH - 3))
                score_copy(n)
            u_hi(2, 3)
            gelu_chunk(2 * CPB - 2, CPB - 2)
            gelu_chunk(2 * CPB - 1, CPB - 1)
            for k in range(2, CPB):
                for j in range(CU):
                    u_hi(2, CU * k + j)
                gelu_chunk(2 * CPB + k - 2, k - 2)
            with act.Fori(3, EXP_BODY) as i:
                u_body(i)
            act.wait_ge(best_sub, 1)
            act.activation(bv[:], bv[:], ACT.Exp).then_inc(best_exp, 1)
            with act.Fori(EXP_BODY, C_G // CPB) as i:
                u_body(i)
            u_body(C_G // CPB, build=(True, False))
            with act.Fori(C_G // CPB + 1, (C_G + T // TPC) // CPB) as i:
                u_body(i, build=(True, True))
            for i in range((C_G + T // TPC) // CPB, PK // CPB):
                u_body(i, build=(False, i == (C_G + T // TPC) // CPB))
            for c in (PK - 2, PK - 1):
                act.wait_ge(unit_used, U_U + CU * (c + 1))
                gelu_chunk(c, c)

            def w_hi(c, k):
                act.wait_ge(w_made, c + 1)
                if isinstance(c, int) and c < CPB:
                    act.wait_ge(unit_used, U_V)
                else:
                    act.wait_ge(unit_used, c * CU + (U_V - CU * (CPB - 1)))
                act.activation(t1hi[:, k % CPB, :], g[:, bass.ds(c, 1), :].rearrange("p a t -> p (a t)"), ACT.Copy
                               ).then_inc(wch_hi, 1)

            def v_body(i, last=False):
                for k in range(CPB):
                    for j in range(CU):
                        n = CU * k + j
                        hi_unit(act, i * (CPB * CU) + (U_V + n), n,
                                i * (CPB * CU // RAW * 16) + (U_V // RAW + n // RAW + 1) * 16)
                    if not (last and k == CPB - 1):
                        w_hi(i * CPB + (k + 1), k + 1)

            w_hi(0, 0)
            v_body(0)
            with act.Fori(1, PK // CPB - 1) as i:
                v_body(i)
            v_body(PK // CPB - 1, True)

        @block.tensor
        def _(pe):
            pe.wait_ge(consts, 7)
            norm_turn(pe, 0, 0, R2, -1)
            mm_block(pe, 0, 0, t1hi, t1lo, after=lambda k: norm_turn(pe, 0, 0, R2, k), ready=0)
            mm_block(pe, 1, 1, t1hi, t1lo)
            with pe.Fori(1, B_BIG // 2) as i:
                mm_block(pe, i * 2, 0, t1hi, t1lo)
                mm_block(pe, i * 2 + 1, 1, t1hi, t1lo)
            mm_block(pe, B_BIG, 0, t1hi, t1lo)

            def tick(t):
                tt = t - K_GATES
                if 0 <= tt < TT:
                    pe.wait_ge(wg_lo, 1)
                    for kc in range(KC):
                        sh, sl = t1hi[:, kc, tt * P:(tt + 1) * P], t1lo[:, kc, tt * P:(tt + 1) * P]
                        o = PS[:, 6, tt * 16:(tt + 1) * 16]
                        pe.matmul(o, sh, wghi[:, kc, :], start=(kc == 0), stop=False)
                        pe.matmul(o, sh, wglo[:, kc, :], start=False, stop=False)
                        mm = pe.matmul(o, sl, wghi[:, kc, :], start=False, stop=(kc == KC - 1))
                    if tt == TT - 1:
                        mm.then_inc(if_mm, 1)
                if t == K_GATES + 3:
                    pe.wait_ge(logf_s, 1)
                    pe.matmul(PS[:, 7, 0:MH], tri[:, 0:P], logf[:, 0, :], start=True, stop=True)
                    pe.matmul(PS[:, 7, MH:2 * MH], tri[:, P:T], logf[:, 0, :], start=True, stop=False)
                    pe.matmul(PS[:, 7, MH:2 * MH], tri[:, 0:P], logf[:, 1, :], start=False, stop=True
                              ).then_inc(b_mm, 1)
                if t == K_GATES + 4:
                    pe.wait_ge(a_s, 1)
                    for tt in range(TT):
                        mm = pe.matmul(PS[0:MH, 6, tt * P:(tt + 1) * P], a_in[:, tt, :], ident[:],
                                       start=True, stop=True)
                    mm.then_inc(at_mm, 1)
                if t == K_GATES + 9:
                    pe.wait_ge(m_step, 10)
                    for tt in range(TT):
                        mm = pe.matmul(PS[:, 7, tt * MH:(tt + 1) * MH], mfin[:, tt * P:(tt + 1) * P],
                                       ident[0:MH, 0:MH], start=True, stop=True)
                    mm.then_inc(mt_mm, 1)

                n = t - K_CONV
                if n % 2 == 0 and n // 2 < KC:
                    n //= 2
                    if n >= 2:
                        pe.wait_ge(conv_done, n - 1)
                    for tt in range(TT):
                        mm = pe.transpose(PS[:, 4 + n % 2, tt * P:(tt + 1) * P], R0[:, tt, n * P:(n + 1) * P], ident[:])
                    mm.then_inc(qk_turned, 1)

                for n in range(2 * (t - K_QK), 2 * (t - K_QK) + 2):
                    if not 0 <= n < KC + KVH:
                        continue
                    if n < 2:
                        pe.wait_ge(conv_done, KC - 1 + n)
                    elif n < 4:
                        pe.wait_ge(mt_s, 1)
                    else:
                        pe.wait_ge(q_out, n - 3)
                    if n == 0:
                        pe.wait_ge(q_scaled, 4 * TT)
                    for tt in range(TT):
                        src = (R2[:, tt, n * P:(n + 1) * P] if n < KC else
                               kd[:, tt, n - KC, :, :].rearrange("p r d -> p (r d)"))
                        mm = pe.transpose(PS[:, 4 + n % 4, tt * P:(tt + 1) * P], src, ident[:])
                    mm.then_inc(q_turned, 1)

                s = t - K_ATT
                if s == 0:
                    pe.wait_ge(q_out, KC + KVH)
                    pe.wait_ge(vb2_s, 1)
                if 2 <= s < N_ITEM + 2:
                    i, b = s - 2, s % 2
                    gq, c = i // NCH, i % NCH
                    pe.wait_ge(probT_sb, i + 1)
                    if i >= 1:
                        pe.wait_ge(av_lo, i)
                    cols = slice(T + gq * DH, T + (gq + 1) * DH)
                    v = (kv[:, 0, cols], kv[:, 0, cols], vb2[:, gq * DH:(gq + 1) * DH], kv[:, 1, cols])[c]
                    for par in range(2):
                        mm = pe.matmul(PS[par * DH:(par + 1) * DH, 7, 0:T], v,
                                       probT[:, b, :, par * CH:(par + 1) * CH], start=True, stop=True)
                    mm.then_inc(av_mm, 1)
                if 0 <= s < N_ITEM:
                    b, gq, c = s % 2, s // NCH, s % NCH
                    if s >= 2:
                        pe.wait_ge(prob_exp, s - 1)
                    for j in range(PAIRS):
                        qj = qT_of(PAIRS * gq + j)[:, c * CH:(c + 1) * CH]
                        for par, kt in ((0, kte), (1, kto)):
                            for at, k0, k1 in window(c):
                                mm = pe.matmul(PS[par * CH:(par + 1) * CH, 4 + b, j * P + at:j * P + at + k1 - k0],
                                               qj, kt[:, gq, k0:k1], start=True, stop=True)
                    mm.then_inc(logits_s, 1)
                if 1 <= s <= N_ITEM:
                    i, b = s - 1, (s - 1) % 2
                    pe.wait_ge(prob_norm, i + 1)
                    if i >= 1:
                        pe.wait_ge(probT_sb, i)
                    for j in range(PAIRS):
                        mm = pe.transpose(PS[:, 6, j * P:(j + 1) * P], prob[:, b, j, :], ident[:])
                    mm.then_inc(prob_turned, 1)

                s = t - K_MLSTM
                if s == 0:
                    pe.wait_ge(silu_done, 4)
                    pe.wait_ge(av_lo, N_ITEM)
                h, b = s // 2, s // 2 % 2
                if s % 2 == 0 and 0 <= h < MH:
                    if h >= 1:
                        pe.wait_ge(ms_p, h)
                        pe.wait_ge(mn_step, 4 * h - 3)
                    pe.matmul(PS[:, 4, 0:T], ident[0:MH, h:h + 1].to_broadcast([MH, P]), mfin,
                              start=True, stop=True)
                    pe.matmul(PS[:, 5, 0:T], bt[:, MH + h, 0:P], bt[:, h, :], start=True, stop=True)
                    pe.matmul(PS[:, 5, T:3 * P], bt[:, MH + h, P:T], bt[:, h, P:T], start=True, stop=True
                              ).then_inc(ms_mm, 1)
                if s % 2 == 1 and 0 <= h < MH:
                    pe.wait_ge(ms_p, h + 1)
                    if h >= 2:
                        pe.wait_ge(h_out, h - 1)
                    v = [R1[:, tt, h * MV:(h + 1) * MV] for tt in range(TT)]
                    for rhs, at in ((v, [PS[:, 6 + b, tt * MV:(tt + 1) * MV] for tt in range(TT)]),
                                    ([ones[:, 0:1]] * TT, [mden(b)[:, tt:tt + 1] for tt in range(TT)])):
                        pe.matmul(at[0], pp[:, b, 0:P], rhs[0], start=True, stop=True)
                        pe.matmul(at[1], pp[:, b, P:T], rhs[0], start=True, stop=False)
                        mm = pe.matmul(at[1], pp[:, b, T:3 * P], rhs[1], start=False, stop=True)
                    mm.then_inc(mn_mm, 1)

                if 0 <= t - K_HM < KC:
                    if t == K_HM:
                        pe.wait_ge(h_gated, 2 * TT)
                    turn(pe, 1, t - K_HM, R2)
                if y_tile(t) is not None:
                    pe.wait_ge(y_add, y_tile(t) // 4 + 1)
                    turn(pe, 2, y_tile(t), R0)
                if t >= K_X2:
                    norm_turn(pe, 1, 3, R0, t - K_X2 - 1)

            for b in range(B_FIX, B_END):
                if b == B_PM:
                    pe.wait_ge(t_lo, 2 * KC)
                thi, tlo = (t2hi, t2lo) if B_PA <= b < B_PM or B_WO <= b < B_PQ else (t1hi, t1lo)
                mm_block(pe, b, b % 2, thi, tlo, after=lambda k: tick(tick_of(b, k)),
                         ready={B_WO: 2 * KC, B_PQ: 3 * KC}.get(b))

            def turn_query(n):
                if n >= 4:
                    pe.wait_ge(qT_sb, n - 3)
                for tt in range(TT):
                    mm = pe.transpose(PS[:, 4 + n % 4, tt * P:(tt + 1) * P], qp[:, tt, n * P:(n + 1) * P], ident[:])
                mm.then_inc(qp_turned, 1)

            def scores(n):
                if n == 0:
                    pe.wait_ge(subk_in, 16)
                pe.wait_ge(qT_sb, 2 * PH)
                if n >= 4:
                    pe.wait_ge(score_sb, n - 3)
                for c in range(2):
                    for tt in range(TT):
                        at = (c * TT + tt) * PK
                        mm = pe.matmul(PS[:, 4 + n % 4, at:at + PK], qT[:, 2 * n + c, tt * P:(tt + 1) * P],
                                       subk[:, c, :], start=True, stop=True)
                mm.then_inc(score_mm, 1)

            def g_token(i, k, m):
                t = i * (CPB * TPC) + (k * TPC + m - C_G * TPC)
                pe.wait_ge(onehots, t + 1)
                pe.matmul(PS[:, 4 + k, m * PK:(m + 1) * PK], oha[:, m % 2, :], ohb[:, m % 2, :],
                          start=True, stop=True).then_inc(g_mm, 1)

            def u_unit(i, n, build=False):
                k, j = n // CU, n % CU
                pe.wait_ge(lo_made, i * (CPB * CU) + (U_U + n + 1))
                for kk in range(UW // P):
                    kc = j * (UW // P) + kk
                    wh = whi[:, n % HI, kk * P:(kk + 1) * P]
                    wl = wlo[:, n % LO, kk * P:(kk + 1) * P]
                    o = PS[:, k % 4, 0:T]
                    pe.matmul(o, wh, t1hi[:, kc, :], start=(kc == 0), stop=False)
                    pe.matmul(o, wh, t1lo[:, kc, :], start=False, stop=False)
                    mm = pe.matmul(o, wl, t1hi[:, kc, :], start=False, stop=(kc == KC - 1))
                    if kk == UW // P - 1:
                        mm.then_inc(unit_used, 1)
                    if build and kk % (UW // P // 2) == UW // P // 2 - 1:
                        g_token(i, k, j * 2 + kk // (UW // P // 2))

            def u_body(i, first=False, build=False, g_waits=False, turn_hk=False):
                for k in range(CPB):
                    if not first:
                        pe.wait_ge(gelu_done, i * CPB + (k - 3))
                    if g_waits:
                        pe.wait_ge(g_out, i * CPB + (k - C_G - 3))
                    if turn_hk and k == CPB - 1:
                        pe.wait_ge(hk_ready, 1)
                        for n in range(3):
                            for tt in range(TT):
                                mm = pe.transpose(PS[:, 4 + n, tt * P:(tt + 1) * P], hk[:, n, tt, :], ident[:])
                            mm.then_inc(hk_turned, 1)
                    for j in range(CU):
                        u_unit(i, CU * k + j, build)

            pe.wait_ge(block_out, B_END)
            n_unit = CPB * CU
            for n in range(2 * n_unit):
                i, k = n // n_unit, n % n_unit // CU
                if i and n % CU == 0:
                    pe.wait_ge(gelu_done, k + 1)
                u_unit(i, n % n_unit)
                if i == 0:
                    turn_query(2 * n)
                    turn_query(2 * n + 1)
                else:
                    scores(n - n_unit)
            with pe.Fori(2, C_G // CPB - 1) as i:
                u_body(i)
            u_body(C_G // CPB - 1, turn_hk=True)
            pe.wait_ge(hkT_sb, 3)
            u_body(C_G // CPB, build=True)
            with pe.Fori(C_G // CPB + 1, (C_G + T // TPC) // CPB) as i:
                u_body(i, build=True, g_waits=True)
            for i in range((C_G + T // TPC) // CPB, PK // CPB):
                u_body(i)

            pe.wait_ge(gelu_done, PK)
            pe.wait_ge(g_out, T // TPC)

            def v_body(i, first, last):
                for k in range(CPB):
                    pe.wait_ge(wch_lo, i * CPB + (k + 1))
                    for j in range(CU):
                        n = CU * k + j
                        pe.wait_ge(lo_made, i * (CPB * CU) + (U_V + n + 1))
                        for tt in range(TT):
                            sh, sl = t1hi[:, k, tt * P:(tt + 1) * P], t1lo[:, k, tt * P:(tt + 1) * P]
                            for half in range(2):
                                o = PS[:, 4 * tt + 2 * j + half, :]
                                vh = whi[:, n % HI, half * BLK:(half + 1) * BLK]
                                vl = v_lo[n % len(v_lo)][:, half * BLK:(half + 1) * BLK]
                                pe.matmul(o, sh, vh, start=(first and k == 0), stop=False)
                                pe.matmul(o, sh, vl, start=False, stop=False)
                                mm = pe.matmul(o, sl, vh, start=False, stop=(last and k == CPB - 1))
                        mm.then_inc(unit_used, 1)

            v_body(0, True, False)
            with pe.Fori(1, PK // CPB - 1) as i:
                v_body(i, False, False)
            v_body(PK // CPB - 1, False, True)

        @block.vector
        def _(dve):
            for tt in range(TT):
                dve.wait_ge(x_in[tt], 16)
            norm_rs(dve, 0)
            norm_scale(dve, R2, R2, 0)
            norm_scale(dve, R2, R2, 1)
            dve.wait_ge(w_small, 7 * 16)
            lo_unit(dve, 0, 0)
            norm_lo(dve, 0, t1hi, t1lo, n1, -1)
            norm_scale(dve, R2, R2, 2)
            for k in range(BU):
                if k + 1 < BU:
                    lo_unit(dve, k + 1, k + 1)
                norm_lo(dve, 0, t1hi, t1lo, n1, k)
                if k == 0:
                    norm_scale(dve, R2, R2, 3)
            dve.wait_ge(wg_hi, 1)
            dve.tensor_tensor(wglo[:], wg[:], wghi[:].bitcast(F32), ALU.subtract).then_inc(wg_lo, 1)
            with dve.Fori(1, B_FIX) as b:
                lo_block(dve, b)

            def cols(b):
                n = (b - B_IN) % B_MAT
                return slice(n * BLK, (n + 1) * BLK)

            def out_block(b):
                dve.wait_ge(unit_used, (b + 1) * BU)
                banks = PS[:, 2 * (b % 2):2 * (b % 2) + TT, :]
                if b < B_PM:
                    if b == B_PA:
                        dve.wait_ge(ga_in, 16 * B_MAT)
                    dve.tensor_tensor(R0[:, :, cols(b)], banks, R0[:, :, cols(b)], ALU.mult).then_inc(block_out, 1)
                elif b < B_WO:
                    if b == B_PM:
                        dve.wait_ge(gm_in, 16 * B_MAT)
                    dve.tensor_tensor(R1[:, :, cols(b)], banks, R1[:, :, cols(b)], ALU.mult).then_inc(block_out, 1)
                    dve.wait_ge(block_out, b + 1)
                    dve.tensor_tensor(R0[:, :, cols(b)], R0[:, :, cols(b)], R1[:, :, cols(b)], ALU.add
                                      ).then_inc(y_add, 1)
                elif b < B_PQ:
                    if b == B_WO:
                        dve.wait_ge(xr_in, 16)
                    dve.tensor_tensor(R2[:, :, cols(b)], banks, R2[:, :, cols(b)], ALU.add).then_inc(block_out, 1)
                else:
                    dve.tensor_copy(qp[:, :, cols(b)], banks).then_inc(block_out, 1)

            def tick(t):
                b = B_FIX + t // BU - 1
                if t % BU == 0 and b >= B_IN and b != B_PQ - 1:
                    out_block(b)

                if t == K_GATES + 2:
                    dve.wait_ge(if_mm, 1)
                    dve.tensor_tensor(pre, PS[:, 6, 0:TT * 16].rearrange("p (a n) -> p a n", a=TT),
                                      ifb[:].unsqueeze(1).to_broadcast([P, TT, 16]), ALU.add).then_inc(if_sb, 1)
                    dve.wait_ge(if_sb, 1)
                    dve.tensor_scalar(fmin, pre, 0.0, None, ALU.min).then_inc(f_min, 1)
                if t == K_GATES + 3:
                    dve.wait_ge(f_min, 1)
                    dve.wait_ge(gate_act, 3)
                    dve.tensor_tensor(logf, fmin[:, :, 8:16], fln[:, :, 8:16], ALU.subtract).then_inc(logf_s, 1)
                if t == K_GATES + 4:
                    dve.wait_ge(b_mm, 1)
                    dve.tensor_copy(bsum, PS[:, 7, 0:TT * MH].rearrange("p (a n) -> p a n", a=TT)
                                    ).then_inc(b_sb, 1)
                    dve.wait_ge(b_sb, 1)
                    dve.tensor_tensor(a_in, pre[:, :, 0:8], bsum, ALU.subtract).then_inc(a_s, 1)
                if t == K_GATES + 5:
                    dve.wait_ge(at_mm, 1)
                    dve.tensor_copy(mrow[:, 0, :], PS[0:MH, 6, 0:T]).then_inc(m_step, 1)
                if 0 <= t - K_GATES - 5 < 4:
                    for n in range(2 * (t - K_GATES - 5), 2 * (t - K_GATES - 5) + 2):
                        w, src, dst = 1 << n, mrow[:, n % 2, :], mrow[:, (n + 1) % 2, :]
                        dve.wait_ge(m_step, n + 1)
                        dve.tensor_copy(dst[:, 0:w], src[:, 0:w])
                        dve.tensor_tensor(dst[:, w:T], src[:, w:T], src[:, 0:T - w], ALU.max).then_inc(m_step, 1)
                if t == K_GATES + 9:
                    dve.wait_ge(m_step, 9)
                    dve.tensor_scalar(mfin, mrow[:, 0, :], 0.0, None, ALU.max).then_inc(m_step, 1)
                if t == K_GATES + 10:
                    dve.wait_ge(mt_mm, 1)
                    dve.tensor_tensor(mt, PS[:, 7, 0:TT * MH].rearrange("p (a n) -> p a n", a=TT), bsum, ALU.add
                                      ).then_inc(mt_s, 1)

                for at, backs in ((1, (1,)), (2, (2, 3))):
                    n = t - K_CONV - at
                    if n % 2 or not 0 <= n // 2 < KC:
                        continue
                    n //= 2
                    x, y = PS[:, 4 + n % 2, 0:T], bt[:, n, :]
                    for back in backs:
                        if back == 1:
                            dve.wait_ge(conv_first, n + 1)
                        else:
                            dve.wait_ge(conv_step, 2 * n + back - 1)
                        dve.scalar_tensor_tensor(y[:, back:T], x[:, 0:T - back], cw[:, n, 3 - back:4 - back],
                                                 y[:, back:T], ALU.mult, ALU.add
                                                 ).then_inc(conv_step if back < 3 else conv_done, 1)
                n = t - K_CONV - 9
                if n % 8 == 0 and 0 <= n // 8 < 4:
                    n //= 8
                    dve.wait_ge(sig_done, n + 1)
                    y = bt[:, 4 * n:4 * n + 4, :].rearrange("p k t -> p (k t)")
                    dve.tensor_tensor(y, y, stage[:, n % 2, :], ALU.mult).then_inc(silu_done, 1)

                m = t - K_RMS - 1
                if 0 <= m < 2 * TT:
                    dve.wait_ge(q_sq, m + 1)
                    dve.tensor_reduce(qs[:, 0, m // 2, m % 2 * 16:(m % 2 + 1) * 16],
                                      qsq.rearrange("p (h d) -> p h d", d=DH), AX.X, ALU.add).then_inc(q_sum, 1)
                if m == 2 * TT:
                    dve.wait_ge(q_sq, 2 * TT + 1)
                    dve.tensor_reduce(qs[:, 0, :, AH:AH + KVH], ksq.rearrange("p a (h d) -> p a h d", d=DH), AX.X,
                                      ALU.add).then_inc(q_sum, 1)
                if m == 2 * TT + 1:
                    dve.wait_ge(q_sum, 2 * TT + 1)
                    dve.memset(kte[DH:P, :, :], 0.0).then_inc(k_zero, 1)
                    dve.memset(kto[0:DH, :, :], 0.0).then_inc(k_zero, 1)
                if m == 2 * TT + 2:
                    dve.tensor_copy(vb2[0:CH, :], kv[0:CH, 1, T:2 * T]).then_inc(k_zero, 1)
                    dve.tensor_copy(vb2[CH:P, :], kv[CH:P, 0, T:2 * T]).then_inc(k_zero, 1)
                    dve.wait_ge(q_root, 1)
                    dve.reciprocal(qs[:, 2], qs[:, 1]).then_inc(q_rs, 1)
                m -= 2 * TT + 4
                if 0 <= m < 2 * TT:
                    tt, half = m // 2, m % 2
                    dve.wait_ge(q_rs, 1)
                    q = R2[:, tt, half * UW:(half + 1) * UW].rearrange("p (h d) -> p h d", d=DH)
                    dve.tensor_tensor(q, q, qs[:, 2, tt, half * 16:(half + 1) * 16].unsqueeze(2)
                                      .to_broadcast([P, 16, DH]), ALU.mult).then_inc(q_scaled, 1)
                m -= 2 * TT
                if 0 <= m < TT:
                    for r in range(2):
                        dve.tensor_tensor(kd[:, m, :, r, :], kv[:, m, 0:T].rearrange("p (h d) -> p h d", d=DH),
                                          qs[:, 2, m, AH:AH + KVH].unsqueeze(2).to_broadcast([P, KVH, DH]), ALU.mult
                                          ).then_inc(q_scaled, 1)
                for n in range(2 * (t - K_QK - 1), 2 * (t - K_QK - 1) + 2):
                    if not 0 <= n < KC + KVH:
                        continue
                    dve.wait_ge(q_turned, n + 1)
                    x = PS[:, 4 + n % 4, 0:T]
                    if n < KC:
                        dve.tensor_scalar(qT_of(n), x, qkw[:, 0:1], float(DH) ** -0.5, ALU.mult, ALU.mult
                                          ).then_inc(q_out, 1)
                    else:
                        if n == KC:
                            dve.wait_ge(k_zero, 4)
                        dve.tensor_scalar(kte[0:DH, n - KC, :], x[0:DH], qkw[0:DH, 1:2], None, ALU.mult)
                        dve.tensor_scalar(kto[DH:P, n - KC, :], x[DH:P], qkw[DH:P, 1:2], None, ALU.mult
                                          ).then_inc(q_out, 1)
                if t == K_QK + 4:
                    dve.wait_ge(silu_done, 4)
                    dve.memset(stage[:, 0, :], 0.0).then_inc(vb2_s, 1)

                s = t - K_ATT
                if 1 <= s <= N_ITEM:
                    i, b, w = s - 1, (s - 1) % 2, keys_of((s - 1) % NCH)
                    dve.wait_ge(prob_exp, i + 1)
                    if w < P:
                        dve.memset(prob[:, b, :, w:P], 0.0)
                    dve.tensor_tensor(ast[:, b, 5, :], ast[:, b, 3, :], ast[:, b, 4, :], ALU.add).then_inc(st_sum, 1)
                    dve.wait_ge(st_sum, i + 1)
                    dve.reciprocal(ast[:, b, 6, :], ast[:, b, 5, :]).then_inc(st_rec, 1)
                    dve.wait_ge(st_rec, i + 1)
                    dve.tensor_tensor(prob[:, b, :, 0:w], prob[:, b, :, 0:w],
                                      ast[:, b, 6, :].unsqueeze(2).to_broadcast([P, PAIRS, w]), ALU.mult
                                      ).then_inc(prob_norm, 1)
                if 2 <= s < N_ITEM + 2:
                    i = s - 2
                    gq, c = i // NCH, i % NCH
                    dve.wait_ge(av_hi, i + 1)
                    at = (slice(None), slice(PAIRS * gq, PAIRS * (gq + 1)), slice(c * CH, (c + 1) * CH))
                    dve.tensor_tensor(t2lo[at], PS[:, 7, 0:T].rearrange("p (j l) -> p j l", j=PAIRS),
                                      t2hi[at].bitcast(F32), ALU.subtract).then_inc(av_lo, 1)
                if 0 <= s < N_ITEM:
                    b, gq, w = s % 2, s // NCH, keys_of(s % NCH)
                    sk = sink[:, PAIRS * gq:PAIRS * (gq + 1)]
                    dve.wait_ge(logits_s, s + 1)
                    dve.tensor_reduce(ast[:, b, 0, :], PS[:, 4 + b, :].rearrange("p (j n) -> p j n", j=PAIRS)[:, :, 0:w],
                                      AX.X, ALU.max).then_inc(st_step, 1)
                    dve.wait_ge(st_step, s + 1)
                    dve.tensor_tensor(ast[:, b, 0, :], ast[:, b, 0, :], sk, ALU.max).then_inc(st_peak, 1)
                    dve.wait_ge(st_peak, s + 1)
                    dve.tensor_scalar(ast[:, b, 1, :], ast[:, b, 0, :], -1.0, None, ALU.mult)
                    dve.tensor_tensor(ast[:, b, 2, :], sk, ast[:, b, 0, :], ALU.subtract).then_inc(st_max, 1)

                s = t - K_MLSTM
                if s % 2 == 0 and 0 < s <= 2 * MH:
                    h, b = s // 2 - 1, (s // 2 - 1) % 2
                    if h == 0:
                        dve.wait_ge(expnm_s, 1)
                    dve.wait_ge(mn_mm, h + 1)
                    den = hd[:, b, 0, :]
                    dve.tensor_copy(den, mden(b)).then_inc(mn_step, 1)
                    dve.wait_ge(mn_step, 4 * h + 1)
                    dve.scalar_tensor_tensor(den, den, -1.0, den, ALU.mult, ALU.max).then_inc(mn_step, 1)
                    dve.wait_ge(mn_step, 4 * h + 2)
                    dve.tensor_tensor(den, den, expnm[:, :, h], ALU.max).then_inc(mn_step, 1)
                    dve.wait_ge(mn_step, 4 * h + 3)
                    dve.reciprocal(hd[:, b, 1, :], den).then_inc(mn_step, 1)
                    dve.wait_ge(mn_step, 4 * h + 4)
                    for tt in range(TT):
                        mm = dve.tensor_scalar(R2[:, tt, h * MV:(h + 1) * MV], PS[:, 6 + b, tt * MV:(tt + 1) * MV],
                                               hd[:, b, 1, tt:tt + 1], None, ALU.mult)
                    mm.then_inc(h_out, 1)
                h, b = s // 2, s // 2 % 2
                if s % 2 == 0 and 0 <= h < MH:
                    dve.wait_ge(ms_mm, h + 1)
                    if h >= 2:
                        dve.wait_ge(ms_p, h - 1)
                    dve.scalar_tensor_tensor(ee[:, b, 0:T], PS[:, 4, 0:T], -1.0, mask[:], ALU.mult,
                                             ALU.add)
                    dve.scalar_tensor_tensor(ee[:, b, T:3 * P], PS[:, 4, P:T], -1.0, mask[:, 0:P],
                                             ALU.mult, ALU.add).then_inc(ms_arg, 1)
                if s % 2 == 1 and 0 <= h < MH:
                    dve.wait_ge(ms_exp, h + 1)
                    if h >= 2:
                        dve.wait_ge(mn_mm, h - 1)
                    dve.scalar_tensor_tensor(pp[:, b, :], PS[:, 5, 0:3 * P], float(P) ** -0.5, ee[:, b, :],
                                             ALU.mult, ALU.mult).then_inc(ms_p, 1)

                if t == K_HNORM + 1:
                    dve.wait_ge(h_root, 1)
                    dve.reciprocal(hs[:, 2], hs[:, 1]).then_inc(h_rs, 1)
                m = t - K_GATED
                if 0 <= m < 2 * TT:
                    if m == 0:
                        dve.wait_ge(h_rs, 1)
                        dve.wait_ge(o_in, 16 * B_MAT)
                    tt = m // 2
                    for h in range(m % 2 * MH // 2, (m % 2 + 1) * MH // 2):
                        at = slice(h * MV, (h + 1) * MV)
                        mm = dve.scalar_tensor_tensor(R2[:, tt, at], R2[:, tt, at], hs[:, 2, tt, h:h + 1],
                                                      o_sb[:, tt, at], ALU.mult, ALU.mult)
                    mm.then_inc(h_gated, 1)

                if 0 <= t - K_HM - 1 < KC:
                    turn_lo(dve, 1, t - K_HM - 1, t1hi, t1lo, mw)
                if y_tile(t - 1) is not None:
                    turn_lo(dve, 2, y_tile(t - 1), t2hi, t2lo, None)
                if t == K_X2:
                    out_block(B_PQ - 1)
                    dve.wait_ge(n_sq, TT + TT * B_MAT)
                    dve.tensor_reduce(ss, ss_blk, AX.X, ALU.add).then_inc(x2_sum, 1)
                    norm_rs(dve, 1)
                    norm_scale(dve, R2, R0, 0)
                    norm_scale(dve, R2, R0, 1)
                if t >= K_X2:
                    norm_lo(dve, 3, t1hi, t1lo, n2, t - K_X2 - 1)
                if 0 <= t - K_X2 < 2:
                    norm_scale(dve, R2, R0, 2 + t - K_X2)

            for u in range(B_FIX * BU, B_END * BU):
                lo_unit(dve, u, u)
                if u > B_FIX * BU:
                    tick(u - B_FIX * BU - 1)
            out_block(B_END - 1)

            done = [0]

            def step(ins):
                done[0] += 1
                ins.then_inc(route, 1)
                dve.wait_ge(route, done[0])

            def top16(rows):
                for v, tv_, _ in rows:
                    ins = dve.max(tv_[:, 0:8], v)
                step(ins)
                yield
                for v, tv_, ti_ in rows:
                    ins = dve.max_index(ti_[:, 0:8], tv_[:, 0:8], v)
                step(ins)
                yield
                for v, tv_, _ in rows:
                    ins = dve.match_replace(v, tv_[:, 0:8], v, NEG)
                step(ins)
                yield
                for v, tv_, _ in rows:
                    ins = dve.max(tv_[:, 8:16], v)
                step(ins)
                yield
                for v, tv_, ti_ in rows:
                    ins = dve.max_index(ti_[:, 8:16], tv_[:, 8:16], v)
                step(ins)
                yield

            def routing():
                for n in range(PH):
                    dve.wait_ge(score_sb, n + 1)
                    yield from top16([(sc[:, tt, 2 * n + c, :], tv[:, tt, 2 * n + c, :], ti[:, tt, 2 * n + c, :])
                                      for tt in range(TT) for c in range(2)])
                step(dve.tensor_copy(tif[:], ti[:]))
                yield
                for tt in range(TT):
                    v = tv[:, tt, :, :].rearrange("p (h c) k -> p h c k", c=2)
                    step(dve.tensor_tensor(cand[:, tt].rearrange("p h (a b) -> p h a b", a=TOP),
                                           v[:, :, 0, :].unsqueeze(3).to_broadcast([P, PH, TOP, TOP]),
                                           v[:, :, 1, :].unsqueeze(2).to_broadcast([P, PH, TOP, TOP]), ALU.add))
                    yield
                for tt in range(TT):
                    for h0 in range(0, PH, 4):
                        yield from top16([(cand[:, tt, h, :], bv[:, tt, h, :], bi[:, tt, h, :])
                                          for h in range(h0, h0 + 4)])
                step(dve.tensor_copy(gsum[:, 0], bv[:, :, :, 0]))
                dve.tensor_tensor(bv[:], bv[:], gsum[:, 0].unsqueeze(3).to_broadcast([P, TT, PH, TOP]), ALU.subtract
                                  ).then_inc(best_sub, 1)
                yield
                flat = bi[:].rearrange("p a h k -> p a (h k)")
                dve.tensor_scalar(ba[:, 0], flat, 4, None, ALU.logical_shift_right)
                step(dve.tensor_scalar(ba[:, 1], flat, TOP - 1, None, ALU.bitwise_and))
                step(dve.tensor_copy(baf[:], ba[:]))
                yield
                half = PH * TOP // 2
                parts = [(tt, slice(m * half, (m + 1) * half), slice(m * PH // 2, (m + 1) * PH // 2))
                         for tt in range(TT) for m in range(2)]
                for c in range(2):
                    for tt, hks, _ in parts:
                        step(dve.tensor_tensor(eq[:, tt, hks], baf[:, c, tt, hks].unsqueeze(2)
                                               .to_broadcast([P, half, TOP]),
                                               iota16.unsqueeze(1).to_broadcast([P, half, TOP]), ALU.is_equal))
                        yield
                    for tt, hks, hh in parts:
                        e = eq[:, tt, hks].rearrange("p (h k) a -> p h k a", k=TOP)
                        side = tif[:, tt].rearrange("p (h c) k -> p h c k", c=2)[:, hh, c, :]
                        step(dve.tensor_tensor(e, e, side.unsqueeze(2).to_broadcast([P, PH // 2, TOP, TOP]), ALU.mult))
                        yield
                    for tt, hks, _ in parts:
                        step(dve.tensor_reduce(hk[:, c, tt, hks], eq[:, tt, hks], AX.X, ALU.add))
                        yield
                dve.wait_ge(best_exp, 1)
                step(dve.tensor_reduce(gsum[:, 0], bv[:], AX.X, ALU.add))
                step(dve.reciprocal(gsum[:, 1], gsum[:, 0]))
                dve.tensor_tensor(hk[:, 2].rearrange("p a (h k) -> p a h k", h=PH), bv[:],
                                  gsum[:, 1].unsqueeze(3).to_broadcast([P, TT, PH, TOP]), ALU.mult
                                  ).then_inc(hk_ready, 1)
                yield

            def u_lo(i, n):
                lo_unit(dve, i * (CPB * CU) + (U_U + n), n)

            dve.wait_ge(iota_set, 1)
            steps = routing()
            first_step = 2 * CPB * CU + 2
            for u in range(C_G * CU - CU):
                u_lo(0, u)
                if u >= first_step:
                    next(steps, None)
            assert next(steps, "over") == "over"
            for n in range(3):
                if n < CU:
                    u_lo(0, C_G * CU - CU + n)
                dve.wait_ge(hk_turned, n + 1)
                dve.tensor_copy(hkT[:, n, :], PS[:, 4 + n, 0:T]).then_inc(hkT_sb, 1)

            dve.wait_ge(hkT_sb, 3)
            dve.wait_ge(iota_set, 2)

            def onehot(t, k, first=False):
                if not first:
                    dve.wait_ge(g_mm, t - 1)
                at = bass.ds(t, 1)
                dve.tensor_scalar(oha[:, k, :], iota[:], hkT[:, 0, at], hkT[:, 2, at], ALU.is_equal, ALU.mult)
                dve.tensor_scalar(ohb[:, k, :], iota[:], hkT[:, 1, at], None, ALU.is_equal).then_inc(onehots, 1)

            def onehot_body(i, first=False):
                for n in range(CPB * CU):
                    lo_unit(dve, i * (CPB * CU) + (U_U + C_G * CU + n), n)
                    for k in range(2):
                        onehot(i * (CPB * CU * 2) + (2 * n + k), k, first and n == 0)

            onehot_body(0, True)
            with dve.Fori(1, T // TPC // CPB) as i:
                onehot_body(i)
            for u in range(C_G * CU + T // TPC * CU, PK * CU):
                u_lo(0, u)

            def w_chunk(c, k, back):
                dve.wait_ge(gel_back[k % 2], back)
                gc = g[:, bass.ds(c, 1), :].rearrange("p a t -> p (a t)")
                dve.tensor_tensor(gc, gback[:, k % 2, :], gc, ALU.mult).then_inc(w_made, 1)

            def w_lo(c, k):
                dve.wait_ge(wch_hi, c + 1)
                dve.tensor_tensor(t1lo[:, k % CPB, :], g[:, bass.ds(c, 1), :].rearrange("p a t -> p (a t)"),
                                  t1hi[:, k % CPB, :].bitcast(F32), ALU.subtract).then_inc(wch_lo, 1)

            def v_lo_unit(i, n):
                u = i * (CPB * CU) + (U_V + n)
                dve.wait_ge(hi_made, u + 1)
                if isinstance(u, int) and u < U_V + LO:
                    dve.wait_ge(unit_used, u - LO + 1)
                elif isinstance(u, int) and u < U_V + len(v_lo):
                    dve.wait_ge(unit_used, U_V)
                else:
                    dve.wait_ge(unit_used, u - len(v_lo) + 1)
                dve.tensor_tensor(v_lo[n % len(v_lo)], raw[:, n % RAW, :], whi[:, n % HI, :].bitcast(F32),
                                  ALU.subtract).then_inc(lo_made, 1)

            def v_body(i, last=False):
                for k in range(CPB):
                    for j in range(CU):
                        v_lo_unit(i, CU * k + j)
                        if j == 0 and not (last and k >= CPB - 2):
                            w_chunk(i * CPB + (k + 2), k, i * 32 + (k // 2 + 2) * 16)
                        if j == 1 and not (last and k == CPB - 1):
                            w_lo(i * CPB + (k + 1), k + 1)

            dve.wait_ge(g_out, T // TPC)
            w_chunk(0, 0, 16)
            w_chunk(1, 1, 16)
            w_lo(0, 0)
            v_body(0)
            with dve.Fori(1, PK // CPB - 1) as i:
                v_body(i)
            v_body(PK // CPB - 1, True)

            dve.wait_ge(unit_used, UNITS)
            dve.wait_ge(x2_in, 16 * TT)
            for tt in range(TT):
                dve.tensor_tensor(g[:, 8 * tt:8 * tt + 8, :].rearrange("p k t -> p (k t)"),
                                  PS[:, 4 * tt:4 * tt + 4, :].rearrange("p b n -> p (b n)"), x2_back[tt], ALU.add
                                  ).then_inc(y_out, 1)


def lay_out(inputs):
    a = {k: np.asarray(v) for k, v in inputs.items()}
    w = a["w_in"][0]
    cut = np.cumsum([0, 1024, 1024, 2048, 2048, 8, 8, 2048, 256, 256, 2048, 2048])
    qm, km, vm, om, im, fm, qa, ka, va, gm, ga = (w[:, cut[i]:cut[i + 1]] for i in range(11))

    def blocks(m):
        n = m.shape[1] // BLK
        return m.reshape(BU, 2, P, n, BLK).transpose(3, 0, 2, 1, 4).reshape(n * BU, P, UW)

    u = a["expert_u"][0].reshape(PK, PK, CU, UW // P, P)
    u = u.transpose(1, 2, 4, 3, 0).reshape(PK * CU, P, UW)
    v = a["expert_v"][0].reshape(PK, PK, CU, UW).transpose(1, 2, 0, 3).reshape(PK * CU, P, UW)
    units = np.concatenate([blocks(m) for m in (ka_va(ka, va), qm, km, vm, qa, om, ga, gm, a["w_proj_a"][0],
                                                a["w_proj_m"][0], a["w_out"][0], a["w_peer_q"][0])] + [u, v])

    def column(x):
        return np.ascontiguousarray(x.reshape(KC, P).T)

    def rep(x, n):
        return np.ascontiguousarray(np.broadcast_to(x, (n,) + x.shape))

    x = a["x"][0].reshape(TT, P, D).transpose(1, 0, 2)
    wi = np.concatenate([im, fm], axis=1).reshape(KC, P, 16).transpose(1, 0, 2)
    sinks = np.repeat(a["sinks"][0].reshape(KC, 2).T, CH, axis=0)
    qk = np.stack([np.tile(a["q_norm_w"][0], 2), np.tile(a["k_norm_w"][0], 2)], axis=1)
    return {
        "units": units,
        "w_if": wi,
        "x": x,
        "norm1": column(a["norm1_w"][0]),
        "norm2": column(a["norm2_w"][0]),
        "conv_w": a["conv_w"][0].reshape(4, KC, P).transpose(2, 1, 0),
        "if_bias": rep(np.concatenate([a["b_igate"][0], a["b_fgate"][0]]), P),
        "mnorm": column(np.tile(a["mlstm_norm_w"][0], MH)),
        "qk_w": qk,
        "sinks": sinks,
        "subk": a["sub_keys"][0].transpose(2, 0, 1),
    }


def ka_va(ka, va):
    return np.concatenate([ka, va], axis=1)


def kernel(**inputs):
    import concourse.bacc as _bacc
    from concourse.bass_utils import run_bass_kernel_spmd as _run

    nc = _bacc.Bacc("TRN2", target_bir_lowering=False, num_devices=1)
    arrays, args = {}, []
    for name, v in lay_out(inputs).items():
        v = np.ascontiguousarray(v)
        arrays[f"in_{name}"] = v
        args.append(nc.dram_tensor(f"in_{name}", v.shape, F32, kind="ExternalInput").ap())
    out = nc.dram_tensor("out", (P, TT, D), F32, kind="ExternalOutput").ap()
    gates = nc.dram_tensor("gates_spill", (B_GATE, P, TT * BLK), F32, kind="Internal").ap()
    x2 = nc.dram_tensor("x2_spill", (P, TT, D), F32, kind="Internal").ap()
    gel = nc.dram_tensor("gelu_spill", (PK, P, T), F32, kind="Internal").ap()
    block_program(nc, *args, out, gates, x2, gel)
    r = _run(nc, [arrays], core_ids=[0])
    return np.ascontiguousarray(r.results[0]["out"].transpose(1, 0, 2)).reshape(1, T, D)
```

```python
from contextlib import ExitStack

import numpy as np
import concourse.bass as bass
from concourse import mybir

F32 = mybir.dt.float32
R32 = mybir.dt.float32r
U32 = mybir.dt.uint32
ALU = mybir.AluOpType
ACT = mybir.ActivationFunctionType
AX = mybir.AxisListType

P = 128
T = 256
D = 2048
TT = T // P
KC = D // P
EPS = 1e-6
BLK = 512
UW = 1024
BU = D * BLK // P // UW
RAW, HI, LO = 4, 4, 2

MH, MV = 8, 256
AH, KVH, DH, CH = 32, 4, 64, 64
NCH = T // CH
PAIRS = AH // KVH // 2
PH, PK, TOP = 8, 128, 16

B_BIG = 12
B_GATE = 12
B_IN = 1 + B_BIG + B_GATE
B_MAT = D // BLK
B_PA, B_PM, B_WO, B_PQ = (B_IN + B_MAT * i for i in range(4))
B_END = B_PQ + B_MAT
U_U = B_END * BU
CU = P * D // P // UW
CPB = 4
U_V = U_U + PK * CU
EXP_BODY = 12
UNITS = U_V + PK * CU
A_BANK = (2, 0, 1, 3)
C_G = 60
TPC = 4
NEG = -1.0e30

B_FIX = 1 + B_BIG
K_GATES, K_CONV, K_QK, K_ATT, K_MLSTM = 0, 0, 32, 43, 62
K_HNORM = K_MLSTM + 2 * MH + 1
K_GATED = K_HNORM + 7
K_SQ, K_KSQ = (12, 14, 18, 20), 22
K_KZERO, K_SCALE, K_KD = 27, (29, 31, 34, 35), (36, 37)
N_ITEM = KVH * NCH


def tick_of(b, k=0):
    return (b - B_FIX) * BU + k


K_HM = tick_of(B_PA)
K_X2 = tick_of(B_PQ) - 1


def block_program(nc, units, w_if, x_d, norm1, norm2, conv_w, if_bias, mnorm, qk_w, sinks, subk_d,
                  out_d, gates_d, x2_d, gel_d):
    with ExitStack() as ctx:
        def sem(name):
            return ctx.enter_context(nc.semaphore(name))

        def sb(stack, name, shape, dt=F32):
            return stack.enter_context(nc.sbuf_tensor(name, shape, dt))

        raw = sb(ctx, "raw", [P, RAW, UW])
        whi = sb(ctx, "whi", [P, HI, UW], R32)
        wlo = sb(ctx, "wlo", [P, LO, UW], R32)
        t1 = sb(ctx, "t1", [P, KC, 2, T], R32)
        t1hi, t1lo = t1[:, :, 0, :], t1[:, :, 1, :]
        ident = sb(ctx, "ident", [P, P])
        small = sb(ctx, "small", [P, 8 + TOP + 8])
        eps_t, ss, sd, rs = small[:, 0:1], small[:, 2:4], small[:, 4:6], small[:, 6:8]
        iota16 = small[:, 8:8 + TOP]
        ss_blk = small[:, 8 + TOP:].rearrange("p (a b) -> p a b", a=TT)

        with ExitStack() as p1:
            t2hi = sb(p1, "t2hi", [P, KC, T], R32)
            t2lo = sb(p1, "t2lo", [P, KC, T], R32)
            big = sb(p1, "big", [P, TT, B_BIG * BLK])
            kv = sb(p1, "kv", [P, TT, BLK])
            bt = sb(p1, "bt", [P, KC, T])
            stage = sb(p1, "stage", [P, 2, TT * BLK])
            stage4 = sb(p1, "stage4", [P, 2, TT * BLK])
            n1 = sb(p1, "n1", [P, KC])
            n2 = sb(p1, "n2", [P, KC])
            cw = sb(p1, "cw", [P, KC, 4])
            ifb = sb(p1, "ifb", [P, 16])
            mw = sb(p1, "mw", [P, KC])
            qkw = sb(p1, "qkw", [P, 2])
            sink = sb(p1, "sink", [P, KC])
            gt = sb(p1, "gt", [P, 8, TT, 16])
            qs = sb(p1, "qs", [P, 3, TT, 36])
            ast = sb(p1, "ast", [P, 2, 7, PAIRS])
            hs = sb(p1, "hs", [P, 3, TT, MH])
            hd = sb(p1, "hd", [P, 2, 2, TT])
            ones = sb(p1, "ones", [P, 2])
            mrow = sb(p1, "mrow", [MH, 3, T])
            tri = sb(p1, "tri", [P, T])
            mask = sb(p1, "mask", [P, T])
            with ExitStack() as pa:
                kte = sb(pa, "kte", [P, KVH, T])
                kto = sb(pa, "kto", [P, KVH, T])
                vb2 = sb(pa, "vb2", [P, KVH * DH])
            with ExitStack() as pm:
                wg = sb(pm, "wg", [P, KC, 16])
                wghi = sb(pm, "wghi", [P, KC, 16], R32)
                wglo = sb(pm, "wglo", [P, KC, 16], R32)
        sqj = [s[:].rearrange("p a b -> p (a b)") for s in (stage, stage4)]
        x2sq = [j[:, n * BLK:(n + 1) * BLK] for j in sqj for n in range(4)]
        qsq = stage4[:, 0, :]
        kd = stage4[:, 0, :].rearrange("p (t g r d) -> p t g r d", t=TT, g=KVH, r=2)
        hsq = stage4[:, 0, :].rearrange("p (s n) -> p s n", n=MV)
        gate_out = stage4[:, 1, :].rearrange("p (a n) -> p a n", a=TT)
        gate_rows = stage[0:16, 0, 0:T]
        ksq = kto[:, 0:2, :]
        prob = stage[:, 0, :].rearrange("p (b j n) -> p b j n", b=2, j=PAIRS)
        probT = stage[:, 1, :].rearrange("p (b j n) -> p b j n", b=2, j=PAIRS)
        ee = stage[:, 0, 0:6 * P].rearrange("p (b n) -> p b n", b=2)
        pp = stage[:, 1, 0:6 * P].rearrange("p (b n) -> p b n", b=2)
        R0, R1, R2 = (big[:, :, i * D:(i + 1) * D] for i in range(3))
        o_sb = bt[:].rearrange("p k t -> p (k t)").rearrange("p (a n) -> p a n", a=TT)

        def qT_of(kc):
            return big[:, kc // 8, kc % 8 * T:(kc % 8 + 1) * T]

        with ExitStack() as q0:
            qp = sb(q0, "qp", [P, TT, D])
            qT = sb(q0, "qT", [P, 2 * PH, T])
            sc = sb(q0, "sc", [P, TT, 2 * PH, PK])
            subk = sb(q0, "subk", [P, 2, PK])
            tv = sb(q0, "tv", [P, TT, 2 * PH, TOP])
            ti = sb(q0, "ti", [P, TT, 2 * PH, TOP], U32)
            tif = sb(q0, "tif", [P, TT, 2 * PH, TOP])
            cand = sb(q0, "cand", [P, TT, PH, TOP * TOP])
            bv = sb(q0, "bv", [P, TT, PH, TOP])
            bi = sb(q0, "bi", [P, TT, PH, TOP], U32)
            ba = sb(q0, "ba", [P, 2, TT, PH * TOP], U32)
            baf = sb(q0, "baf", [P, 2, TT, PH * TOP])
            eq = sb(q0, "eq", [P, TT, PH * TOP, TOP])
            hk = sb(q0, "hk", [P, 3, TT, PH * TOP])
            gsum = sb(q0, "gsum", [P, 2, TT, PH])
        g = sb(ctx, "g", [P, PK, T])
        hkT = sb(ctx, "hkT", [P, 3, T])
        iota = ident
        gel = sb(ctx, "gel", [P, 2, T])
        with ExitStack() as q2:
            oha = sb(q2, "oha", [P, 2, P])
            ohb = sb(q2, "ohb", [P, 2, P])
        with ExitStack() as q3:
            gback = sb(q3, "gback", [P, 2, T])
        v_lo = [wlo[:, 0, :], wlo[:, 1, :]] + [t1[:, kc:kc + 2].rearrange("p k s t -> p (k s t)")
                                                for kc in (CPB, CPB + 2)]
        x2_back = [t1[:, kc:kc + 4].rearrange("p k s t -> p (k s t)").bitcast(F32) for kc in (KC // 2, KC - 4)]
        out_sb = [g[:, 8 * tt:8 * tt + 8, :].rearrange("p k t -> p (k t)") for tt in range(TT)]
        PS = ctx.enter_context(nc.psum_tensor("PS", [P, 8, BLK], F32))

        pre, fab, fexp, fln, fmin = (gt[:, i, :, :] for i in range(5))
        logf, a_in, bsum = gt[:, 5, :, 0:8], gt[:, 5, :, 8:16], gt[:, 6, :, 0:8]
        mt, expnm = gt[:, 6, :, 8:16], gt[:, 7, :, 0:8]
        mfin = mrow[:, 2, :]

        raw_landed = [sem(f"raw_landed{i}") for i in range(RAW)]
        hi_made, lo_made, unit_used = sem("hi_made"), sem("lo_made"), sem("unit_used")
        block_out = sem("block_out")
        consts, eps_set, iota_set = sem("consts"), sem("eps_set"), sem("iota_set")
        x_in = [sem("x_in0"), sem("x_in1")]
        n1_in, w_small, wif_in, subk_in = sem("n1_in"), sem("w_small"), sem("wif_in"), sem("subk_in")
        if_rows, if_turned = sem("if_rows"), sem("if_turned")
        gate_sb, conv_first = sem("gate_sb"), sem("conv_first")
        gate_stored = [sem("gate_stored0"), sem("gate_stored1")]
        o_in, ga_in, gm_in, xr_in = sem("o_in"), sem("ga_in"), sem("gm_in"), sem("xr_in")
        x2_stored, x2_in, out_stored = sem("x2_stored"), sem("x2_in"), sem("out_stored")
        n_sq, n_root, n_rs, n_scaled = sem("n_sq"), sem("n_root"), sem("n_rs"), sem("n_scaled")
        turned, t_hi, t_lo = sem("turned"), sem("t_hi"), sem("t_lo")
        x2_sum = sem("x2_sum")
        wg_hi, wg_lo, if_mm, if_sb = sem("wg_hi"), sem("wg_lo"), sem("if_mm"), sem("if_sb")
        gate_act, f_min, logf_s, b_mm, b_sb, a_s = (sem("gate_act"), sem("f_min"), sem("logf_s"), sem("b_mm"),
                                                    sem("b_sb"), sem("a_s"))
        at_mm, m_step, mt_mm, mt_s, expnm_s = sem("at_mm"), sem("m_step"), sem("mt_mm"), sem("mt_s"), sem("expnm_s")
        qk_turned, conv_step, conv_done, sig_done, silu_done = (
            sem("qk_turned"), sem("conv_step"), sem("conv_done"), sem("sig_done"), sem("silu_done"))
        q_sq, q_sum, q_root, q_rs, q_scaled = sem("q_sq"), sem("q_sum"), sem("q_root"), sem("q_rs"), sem("q_scaled")
        k_zero, q_turned, q_out, vb2_s = sem("k_zero"), sem("q_turned"), sem("q_out"), sem("vb2_s")
        st_peak, st_sum, st_rec = sem("st_peak"), sem("st_sum"), sem("st_rec")
        logits_s, st_step, st_max, prob_exp, prob_norm = (
            sem("logits_s"), sem("st_step"), sem("st_max"), sem("prob_exp"), sem("prob_norm"))
        prob_turned, probT_sb, av_mm, av_hi, av_lo = (
            sem("prob_turned"), sem("probT_sb"), sem("av_mm"), sem("av_hi"), sem("av_lo"))
        ms_mm, ms_arg, ms_exp, ms_p, mn_mm, mn_step, h_out, h_sq = (
            sem("ms_mm"), sem("ms_arg"), sem("ms_exp"), sem("ms_p"), sem("mn_mm"), sem("mn_step"),
            sem("h_out"), sem("h_sq"))
        h_root, h_rs, h_gated, y_add = (sem("h_root"), sem("h_rs"), sem("h_gated"), sem("y_add"))
        qp_turned, qT_sb, score_mm, score_sb = sem("qp_turned"), sem("qT_sb"), sem("score_mm"), sem("score_sb")
        route, best_sub, best_exp, hk_turned, hkT_sb = (
            sem("route"), sem("best_sub"), sem("best_exp"), sem("hk_turned"), sem("hkT_sb"))
        hk_ready = sem("hk_ready")
        onehots, g_mm, g_out = sem("onehots"), sem("g_mm"), sem("g_out")
        a_summed, gelu_done, w_made = sem("a_summed"), sem("gelu_done"), sem("w_made")
        gel_stored = [sem("gel_stored0"), sem("gel_stored1")]
        gel_back = [sem("gel_back0"), sem("gel_back1")]
        wch_hi, wch_lo = sem("wch_hi"), sem("wch_lo")
        y_out = sem("y_out")
        block = ctx.enter_context(nc.Block())

        def load_unit(sp, u, k, first=False):
            if not first:
                sp.wait_ge(lo_made, u - RAW + 1)
            sp.dma_start(raw[:, k % RAW, :], units[bass.ds(u, 1), :, :].rearrange("a p n -> p (a n)")
                         ).then_inc(raw_landed[k % RAW], 16)

        def hi_unit(act, u, k, landed):
            act.wait_ge(raw_landed[k % RAW], landed)
            if not (isinstance(u, int) and u < HI):
                act.wait_ge(unit_used, u - HI + 1)
            act.activation(whi[:, k % HI, :], raw[:, k % RAW, :], ACT.Copy).then_inc(hi_made, 1)

        def lo_unit(dve, u, k):
            dve.wait_ge(hi_made, u + 1)
            if not (isinstance(u, int) and u < LO):
                dve.wait_ge(unit_used, u - LO + 1)
            dve.tensor_tensor(wlo[:, k % LO, :], raw[:, k % RAW, :], whi[:, k % HI, :].bitcast(F32),
                              ALU.subtract).then_inc(lo_made, 1)

        def hi_fix(act, u):
            hi_unit(act, u, u, (u // RAW + 1) * 16)

        def hi_block(act, b, evacuate=None):
            for k in range(BU):
                hi_unit(act, b * BU + k, k, b * (BU // RAW * 16) + (k // RAW + 1) * 16)
                if k == HI - 1 and evacuate is not None:
                    evacuate()

        def lo_block(dve, b):
            for k in range(BU):
                lo_unit(dve, b * BU + k, k)

        def mm_block(pe, b, odd, thi, tlo, after=None, ready=None):
            if not (isinstance(b, int) and b < 2):
                pe.wait_ge(block_out, b - 1)
            for k in range(BU):
                pe.wait_ge(lo_made, b * BU + k + 1)
                if ready is not None:
                    pe.wait_ge(t_lo, ready + 2 * k + 2)
                for kk in range(2):
                    kc = 2 * k + kk
                    vh = whi[:, k % HI, kk * BLK:(kk + 1) * BLK]
                    vl = wlo[:, k % LO, kk * BLK:(kk + 1) * BLK]
                    for tt in range(TT):
                        o = PS[:, 2 * odd + tt, :]
                        sh, sl = thi[:, kc, tt * P:(tt + 1) * P], tlo[:, kc, tt * P:(tt + 1) * P]
                        pe.matmul(o, sh, vh, start=(kc == 0), stop=False)
                        pe.matmul(o, sh, vl, start=False, stop=False)
                        mm = pe.matmul(o, sl, vh, start=False, stop=(kc == KC - 1))
                mm.then_inc(unit_used, 1)
                if after is not None:
                    after(k)

        def turn(pe, n, kc, src):
            if n or kc >= 4:
                pe.wait_ge(t_lo, KC * n + kc - 3)
            for tt in range(TT):
                mm = pe.transpose(PS[:, 4 + kc % 4, tt * P:(tt + 1) * P], src[:, tt, kc * P:(kc + 1) * P], ident[:])
            mm.then_inc(turned, 1)

        def turn_hi(act, n, kc, thi, w):
            act.wait_ge(turned, KC * n + kc + 1)
            act.activation(thi[:, kc, :], PS[:, 4 + kc % 4, 0:T], ACT.Copy,
                           scale=(1.0 if w is None else w[:, kc:kc + 1])).then_inc(t_hi, 1)

        def turn_lo(dve, n, kc, thi, tlo, w):
            dve.wait_ge(t_hi, KC * n + kc + 1)
            dve.scalar_tensor_tensor(tlo[:, kc, :], PS[:, 4 + kc % 4, 0:T],
                                     1.0 if w is None else w[:, kc:kc + 1],
                                     thi[:, kc, :].bitcast(F32), ALU.mult, ALU.subtract).then_inc(t_lo, 1)

        def norm_root(act, m):
            act.activation(sd, ss, ACT.Sqrt, scale=1.0 / D, bias=eps_t).then_inc(n_root, 1)

        def norm_rs(dve, m):
            dve.wait_ge(n_root, m + 1)
            dve.reciprocal(rs, sd).then_inc(n_rs, 1)
            dve.wait_ge(n_rs, m + 1)

        def norm_scale(dve, xin, out, q):
            for tt in range(TT):
                dve.tensor_scalar(out[:, tt, q * BLK:(q + 1) * BLK], xin[:, tt, q * BLK:(q + 1) * BLK],
                                  rs[:, tt:tt + 1], None, ALU.mult).then_inc(n_scaled, 1)

        def norm_tiles(k):
            return range(4) if k == -1 else range(2 * k + 4, 2 * k + 6) if 0 <= k < KC // 2 - 2 else ()

        def norm_turn(pe, m, n, src, k):
            for kc in norm_tiles(k):
                pe.wait_ge(n_scaled, TT * (4 * m + kc // 4 + 1))
                turn(pe, n, kc, src)

        def norm_hi(act, n, thi, w, k):
            for kc in norm_tiles(k):
                turn_hi(act, n, kc, thi, w)

        def norm_lo(dve, n, thi, tlo, w, k):
            for kc in (norm_tiles(-1) if k == -1 else norm_tiles(k - 1) if k > 0 else ()):
                turn_lo(dve, n, kc, thi, tlo, w)

        def window(c):
            return {0: [(0, 0, CH)], 1: [(0, 0, P)], 2: [(0, P, P + CH), (CH, CH, P)], 3: [(0, CH * 2, T)]}[c]

        def keys_of(c):
            return CH if c == 0 else P

        def y_tile(t):
            b, k = B_FIX + t // BU, t % BU
            return 4 * (b - B_PM - 1) + k - 1 if B_PM < b <= B_WO and 1 <= k <= 4 else None

        def mden(b):
            return PS[:, 5, 3 * P + TT * b:3 * P + TT * (b + 1)]

        @block.sync
        def _(sp):
            for tt in range(TT):
                sp.dma_start(R2[:, tt, :], x_d[:, tt, :]).then_inc(x_in[tt], 16)
            for u in range(RAW):
                load_unit(sp, u, u, first=True)
            with sp.Fori(1, U_U // RAW) as i:
                for k in range(RAW):
                    load_unit(sp, i * RAW + k, k)

            def store_gelu(c, k):
                sp.wait_ge(gelu_done, c + 1)
                sp.dma_start(gel_d[bass.ds(c, 1), :, :].rearrange("a p t -> p (a t)"), gel[:, k % 2, :]
                             ).then_inc(gel_stored[k % 2], 16)

            def load_gelu(c, k):
                if isinstance(c, int) and c < CPB + 2:
                    sp.wait_ge(gel_stored[k % 2], (c // 2 + 1) * 16)
                if isinstance(c, int) and c < 2:
                    sp.wait_ge(g_mm, T)
                else:
                    sp.wait_ge(w_made, c - 1)
                sp.dma_start(gback[:, k % 2, :], gel_d[bass.ds(c, 1), :, :].rearrange("a p t -> p (a t)")
                             ).then_inc(gel_back[k % 2], 16)

            def u_body(i, first, last=False):
                for k in range(CPB):
                    for j in range(CU):
                        n = CU * k + j
                        load_unit(sp, i * (CPB * CU) + (U_U + n), n)
                    if last and k == CPB - 2:
                        load_gelu(0, 0)
                        load_gelu(1, 1)
                    if not first:
                        store_gelu(i * CPB - CPB + k, k)

            u_body(0, True)
            with sp.Fori(1, PK // CPB - 1) as i:
                u_body(i, False)
            u_body(PK // CPB - 1, False, True)

            def v_body(i, first, last):
                for k in range(CPB):
                    if not (first or last and k >= CPB - 2):
                        load_gelu(i * CPB + (k + 2), k)
                    for j in range(CU):
                        n = CU * k + j
                        load_unit(sp, i * (CPB * CU) + (U_V + n), n)
                    if first:
                        load_gelu(i * CPB + (k + 2), k)
                        store_gelu(PK - CPB + k, k)

            v_body(0, True, False)
            for st in gel_stored:
                sp.wait_ge(st, PK // 2 * 16)
            with sp.Fori(1, PK // CPB - 1) as i:
                v_body(i, False, False)
            v_body(PK // CPB - 1, False, True)
            for n in range(CU * TT):
                j, tt = n // TT, n % TT
                sp.wait_ge(y_out, n + 1)
                sp.dma_start(out_d[:, tt, j * UW:(j + 1) * UW], out_sb[tt][:, j * UW:(j + 1) * UW]
                             ).then_inc(out_stored, 16)
            sp.wait_ge(out_stored, 16 * CU * TT)

        @block.gpsimd
        def _(pool):
            pool.memset(small[:, 0:8], EPS).then_inc(eps_set, 1)
            pool.dma_start(n1[:], norm1).then_inc(n1_in, 16)
            for dst, src in ((n2, norm2), (cw, conv_w), (ifb, if_bias), (mw, mnorm), (qkw, qk_w),
                             (sink, sinks)):
                pool.dma_start(dst[:], src).then_inc(w_small, 16)
            pool.dma_start(wg[:], w_if).then_inc(wif_in, 16)
            pool.memset(ones[:], 1.0).then_inc(consts, 1)
            pool.memset(ident[:], 0.0).then_inc(consts, 1)
            pool.memset(tri[:], 1.0).then_inc(consts, 1)
            pool.memset(mask[:], 0.0).then_inc(consts, 1)
            pool.iota(iota16, pattern=[[1, TOP]], base=0, channel_multiplier=0,
                      allow_small_or_imprecise_dtypes=True).then_inc(iota_set, 1)
            pool.wait_ge(consts, 4)
            pool.affine_select(out=ident[:], in_=ident[:], compare_op=ALU.not_equal, fill=1.0, base=0,
                               pattern=[[-1, P]], channel_multiplier=1).then_inc(consts, 1)
            pool.affine_select(out=tri[:], in_=tri[:], compare_op=ALU.is_ge, fill=0.0, base=0,
                               pattern=[[1, T]], channel_multiplier=-1).then_inc(consts, 1)
            pool.affine_select(out=mask[:], in_=mask[:], compare_op=ALU.is_ge, fill=NEG, base=0,
                               pattern=[[1, T]], channel_multiplier=-1).then_inc(consts, 1)
            def gates_away(first, last):
                for n in range(first, last):
                    for tt in range(TT):
                        if tt == 0:
                            pool.wait_ge(gate_sb, n + 1)
                        else:
                            pool.wait_ge(block_out, B_FIX + n + 1)
                        pool.dma_start(gates_d[n, :, tt * BLK:(tt + 1) * BLK], gate_out[:, tt, :]
                                       ).then_inc(gate_stored[tt], 16)

            def gates_back(dst, first, s):
                for st in gate_stored:
                    pool.wait_ge(st, 16 * (first + B_MAT))
                for n in range(B_MAT):
                    pool.dma_start(dst[:, :, n * BLK:(n + 1) * BLK],
                                   gates_d[first + n].rearrange("p (a n) -> p a n", a=TT)).then_inc(s, 16)

            gates_away(0, 2 * B_MAT)
            pool.wait_ge(av_lo, N_ITEM)
            gates_back(R0, B_MAT, ga_in)
            gates_away(2 * B_MAT, 2 * B_MAT + 1)
            pool.wait_ge(mn_mm, MH)
            gates_back(o_sb, 0, o_in)
            gates_away(2 * B_MAT + 1, B_GATE)
            gates_back(R1, 2 * B_MAT, gm_in)
            pool.wait_ge(turned, 2 * KC)
            pool.dma_start(R2, x_d).then_inc(xr_in, 16)
            pool.wait_ge(block_out, B_WO + B_MAT)
            pool.dma_start(x2_d, R2).then_inc(x2_stored, 16)
            pool.wait_ge(x2_stored, 16)
            pool.wait_ge(t_lo, 4 * KC)
            pool.dma_start(subk[:], subk_d).then_inc(subk_in, 16)
            pool.wait_ge(hk_turned, 3)
            pool.iota(iota[:], pattern=[[1, P]], base=0, channel_multiplier=0,
                      allow_small_or_imprecise_dtypes=True).then_inc(iota_set, 1)
            pool.wait_ge(unit_used, U_V)
            for tt in range(TT):
                pool.dma_start(x2_back[tt], x2_d[:, tt, :]).then_inc(x2_in, 16)

        @block.scalar
        def _(act):
            act.wait_ge(eps_set, 1)
            act.activation(sd, small[:, 0:2], ACT.Sqrt)
            for tt in range(TT):
                act.wait_ge(x_in[tt], 16)
                act.activation(sqj[tt], R2[:, tt, :], ACT.Square, accum_out=ss[:, tt:tt + 1]).then_inc(n_sq, 1)
            act.wait_ge(n_sq, TT)
            norm_root(act, 0)
            hi_fix(act, 0)
            act.wait_ge(n1_in, 16)
            norm_hi(act, 0, t1hi, n1, -1)
            for u in range(1, HI - 1):
                hi_fix(act, u)
            for k in range(BU):
                if k + HI - 1 < BU:
                    hi_fix(act, k + HI - 1)
                norm_hi(act, 0, t1hi, n1, k)
            act.wait_ge(w_small, 6 * 16)
            act.wait_ge(wif_in, 16)
            act.activation(wghi[:], wg[:], ACT.Copy).then_inc(wg_hi, 1)

            def out_kv():
                act.activation(kv[:], PS[:, 0:TT, :], ACT.Copy).then_inc(block_out, 1)

            def out_big(b, odd):
                act.activation(big[:, :, bass.ds((b - 1) * BLK, BLK)], PS[:, 2 * odd:2 * odd + TT, :], ACT.Copy
                               ).then_inc(block_out, 1)

            def out_gate(b):
                n = b - B_FIX
                for tt in range(TT):
                    if n:
                        act.wait_ge(gate_stored[tt], 16 * n)
                    act.activation(gate_out[:, tt, :], PS[:, 2 * (b % 2) + tt, :], ACT.Sigmoid
                                   ).then_inc(gate_sb if tt == 0 else block_out, 1)

            hi_block(act, 1, out_kv)
            with act.Fori(1, B_BIG // 2) as i:
                hi_block(act, i * 2, lambda: out_big(i * 2 - 1, 1))
                hi_block(act, i * 2 + 1, lambda: out_big(i * 2, 0))
            hi_block(act, B_BIG, lambda: out_big(B_BIG - 1, 1))

            def tick(t):
                if t % BU == 0 and t <= tick_of(B_IN):
                    b = B_FIX - 1 + t // BU
                    out_big(b, b % 2) if b < B_FIX else out_gate(b)

                if t == K_GATES + 3:
                    act.wait_ge(if_mm, 1)
                    act.activation(gate_rows, PS[0:16, 6, 0:T], ACT.Copy).then_inc(if_rows, 1)
                if t == K_GATES + 5:
                    act.wait_ge(consts, 7)
                    act.wait_ge(if_sb, 1)
                    act.activation(fab, pre, ACT.Abs).then_inc(gate_act, 1)
                    act.wait_ge(gate_act, 1)
                    act.activation(fexp, fab, ACT.Exp, scale=-1.0).then_inc(gate_act, 1)
                    act.wait_ge(gate_act, 2)
                    act.activation(fln, fexp, ACT.Ln, bias=ones[:, 0:1]).then_inc(gate_act, 1)
                if t == K_GATES + 13:
                    act.wait_ge(mt_s, 1)
                    act.activation(expnm, mt, ACT.Exp, scale=-1.0).then_inc(expnm_s, 1)

                n = t - K_CONV
                if n % 2 == 0 and n // 2 < KC:
                    n //= 2
                    act.wait_ge(qk_turned, n + 1)
                    act.activation(bt[:, n, :], PS[:, 4 + n % 2, 0:T], ACT.Copy, scale=cw[:, n, 3:4]
                                   ).then_inc(conv_first, 1)
                n = t - K_CONV - 8
                if n % 8 == 0 and 0 <= n // 8 < 4:
                    n //= 8
                    act.wait_ge(conv_done, 4 * n + 4)
                    if n >= 2:
                        act.wait_ge(silu_done, n - 1)
                    if n == 0:
                        act.wait_ge(if_turned, 1)
                    act.activation(stage[:, n % 2, :], bt[:, 4 * n:4 * n + 4, :].rearrange("p k t -> p (k t)"),
                                   ACT.Sigmoid).then_inc(sig_done, 1)

                if t in K_SQ:
                    m = K_SQ.index(t)
                    if m == 0:
                        act.wait_ge(block_out, B_FIX)
                    else:
                        act.wait_ge(q_sum, m)
                    act.activation(qsq, R2[:, m // 2, m % 2 * UW:(m % 2 + 1) * UW], ACT.Square).then_inc(q_sq, 1)
                if t == K_KSQ:
                    act.activation(ksq, kv[:, :, 0:T], ACT.Square).then_inc(q_sq, 1)
                if t == K_KSQ + 1:
                    act.wait_ge(q_sum, 2 * TT + 1)
                    act.activation(qs[:, 1, :, :], qs[:, 0, :, :], ACT.Sqrt, scale=1.0 / DH, bias=eps_t
                                   ).then_inc(q_root, 1)

                s = t - K_ATT
                if s == 0:
                    act.wait_ge(silu_done, 4)
                if 3 <= s < N_ITEM + 3:
                    i = s - 3
                    gq, c = i // NCH, i % NCH
                    act.wait_ge(av_mm, i + 1)
                    act.activation(t2hi[:, PAIRS * gq:PAIRS * (gq + 1), c * CH:(c + 1) * CH],
                                   PS[:, 7, 0:T].rearrange("p (j l) -> p j l", j=PAIRS), ACT.Copy
                                   ).then_inc(av_hi, 1)
                if 2 <= s < N_ITEM + 2:
                    i, b = s - 2, s % 2
                    act.wait_ge(prob_turned, i + 1)
                    if i >= 2:
                        act.wait_ge(av_mm, i - 1)
                    act.activation(probT[:, b], PS[:, 6, :].rearrange("p (j n) -> p j n", j=PAIRS), ACT.Copy
                                   ).then_inc(probT_sb, 1)
                if 0 <= s < N_ITEM:
                    b, w = s % 2, keys_of(s % NCH)
                    act.wait_ge(st_max, s + 1)
                    if s >= 2:
                        act.wait_ge(prob_turned, s - 1)
                    for j in range(PAIRS):
                        act.activation(prob[:, b, j, 0:w], PS[:, 4 + b, j * P:j * P + w], ACT.Exp,
                                       bias=ast[:, b, 1, j:j + 1], accum_out=ast[:, b, 3, j:j + 1])
                    act.activation(ast[:, b, 4, :], ast[:, b, 2, :], ACT.Exp).then_inc(prob_exp, 1)

                s = t - K_MLSTM
                if s % 2 == 0 and 0 <= s <= 2 * MH:
                    h = s // 2 - 1
                    if h >= 0:
                        act.wait_ge(h_out, h + 1)
                        if h >= 2:
                            act.wait_ge(h_sq, 2 * (h - 1))
                        for tt in range(TT):
                            act.activation(hsq[:, (2 * h + tt) % 4, :], R2[:, tt, h * MV:(h + 1) * MV], ACT.Square,
                                           accum_out=hs[:, 0, tt, h:h + 1]).then_inc(h_sq, 1)
                    h, b = s // 2, s // 2 % 2
                    if h < MH:
                        act.wait_ge(ms_arg, h + 1)
                        act.activation(ee[:, b, 0:T], ee[:, b, 0:T], ACT.Exp, bias=a_in[:, 0, h:h + 1])
                        act.activation(ee[:, b, T:3 * P], ee[:, b, T:3 * P], ACT.Exp, bias=a_in[:, 1, h:h + 1]
                                       ).then_inc(ms_exp, 1)
                if t == K_HNORM:
                    act.wait_ge(h_sq, 2 * MH)
                    act.activation(hs[:, 1], hs[:, 0], ACT.Sqrt, scale=1.0 / MV, bias=eps_t).then_inc(h_root, 1)

                if 0 <= t - K_HM < KC:
                    turn_hi(act, 1, t - K_HM, t1hi, mw)
                if y_tile(t) is not None:
                    turn_hi(act, 2, y_tile(t), t2hi, None)

                n = (t - 1 - tick_of(B_WO + 1)) // BU
                if t == K_X2 - 1:
                    act.activation(sd, small[:, 0:2], ACT.Sqrt)
                if t == K_X2 or (t % BU == 1 and 0 <= n < B_MAT - 1):
                    n = B_MAT - 1 if t == K_X2 else n
                    act.wait_ge(block_out, B_WO + n + 1)
                    for tt in range(TT):
                        act.activation(x2sq[TT * n + tt], R2[:, tt, n * BLK:(n + 1) * BLK], ACT.Square,
                                       accum_out=ss_blk[:, tt, n:n + 1]).then_inc(n_sq, 1)
                if t == K_X2:
                    act.wait_ge(x2_sum, 1)
                    norm_root(act, 1)
                norm_hi(act, 3, t1hi, n2, t - K_X2 - 1) if t >= K_X2 else None

            for u in range(B_FIX * BU, B_END * BU):
                hi_fix(act, u)
                if u - B_FIX * BU >= HI - 1:
                    tick(u - B_FIX * BU - (HI - 1))

            def qT_copy(n):
                act.wait_ge(qp_turned, n + 1)
                act.activation(qT[:, n, :], PS[:, 4 + n % 4, 0:T], ACT.Copy).then_inc(qT_sb, 1)

            def score_copy(n):
                act.wait_ge(score_mm, n + 1)
                act.activation(sc[:, :, 2 * n:2 * n + 2, :].rearrange("p a c k -> p c a k"),
                               PS[:, 4 + n % 4, :].rearrange("p (c a k) -> p c a k", c=2, a=TT), ACT.Copy
                               ).then_inc(score_sb, 1)

            def gelu_chunk(c, k):
                act.wait_ge(a_summed, c + 1)
                act.activation(gel[:, k % 2, :], gel[:, k % 2, :], ACT.Gelu).then_inc(gelu_done, 1)

            def g_copy(c, k):
                act.wait_ge(g_mm, c * TPC - (C_G - 1) * TPC)
                act.activation(g[:, :, bass.ds(c * TPC - C_G * TPC, TPC)].rearrange("p k t -> p t k"),
                               PS[:, 4 + k % 4, :].rearrange("p (t k) -> p t k", t=TPC), ACT.Copy).then_inc(g_out, 1)

            def u_hi(i, n):
                hi_unit(act, i * (CPB * CU) + (U_U + n), n,
                        i * (CPB * CU // RAW * 16) + (U_U // RAW + n // RAW + 1) * 16)

            def u_body(i, first=False, build=(False, False)):
                for k in range(CPB):
                    for j in range(CU):
                        u_hi(i, CU * k + j)
                    if not first or k >= 2:
                        gelu_chunk(i * CPB + (k - 2), k - 2 + CPB)
                    if build[0] if k >= 2 else build[1]:
                        g_copy(i * CPB + (k - 2), k - 2 + CPB)

            n_unit = CPB * CU
            for n in range(2 * n_unit):
                i, k = n // n_unit, n % n_unit // CU
                u_hi(i, n % n_unit)
                if n % CU == CU - 1 and CPB * i + k >= 2:
                    gelu_chunk(i * CPB + k - 2, k - 2 + CPB)
                if 3 <= n < 3 + n_unit:
                    qT_copy(2 * (n - 3))
                    qT_copy(2 * (n - 3) + 1)
                if n >= 3 + n_unit:
                    score_copy(n - 3 - n_unit)
            for n in range(PH - 3, PH):
                u_hi(2, n - (PH - 3))
                score_copy(n)
            u_hi(2, 3)
            gelu_chunk(2 * CPB - 2, CPB - 2)
            gelu_chunk(2 * CPB - 1, CPB - 1)
            for k in range(2, CPB):
                for j in range(CU):
                    u_hi(2, CU * k + j)
                gelu_chunk(2 * CPB + k - 2, k - 2)
            with act.Fori(3, EXP_BODY) as i:
                u_body(i)
            act.wait_ge(best_sub, 1)
            act.activation(bv[:], bv[:], ACT.Exp).then_inc(best_exp, 1)
            with act.Fori(EXP_BODY, C_G // CPB) as i:
                u_body(i)
            u_body(C_G // CPB, build=(True, False))
            with act.Fori(C_G // CPB + 1, (C_G + T // TPC) // CPB) as i:
                u_body(i, build=(True, True))
            for i in range((C_G + T // TPC) // CPB, PK // CPB):
                u_body(i, build=(False, i == (C_G + T // TPC) // CPB))
            def w_hi(c, k):
                act.wait_ge(w_made, c + 1)
                if isinstance(c, int) and c < CPB:
                    act.wait_ge(unit_used, U_V)
                else:
                    act.wait_ge(unit_used, c * CU + (U_V - CU * (CPB - 1)))
                act.activation(t1hi[:, k % CPB, :], g[:, bass.ds(c, 1), :].rearrange("p a t -> p (a t)"), ACT.Copy
                               ).then_inc(wch_hi, 1)

            def v_body(i, last=False, made=0):
                for k in range(CPB):
                    for j in range(CU):
                        n = CU * k + j
                        if n < made:
                            continue
                        hi_unit(act, i * (CPB * CU) + (U_V + n), n,
                                i * (CPB * CU // RAW * 16) + (U_V // RAW + n // RAW + 1) * 16)
                    if not (last and k == CPB - 1):
                        w_hi(i * CPB + (k + 1), k + 1)

            for n in range(HI - 1):
                hi_fix(act, U_V + n)
                if n == 1:
                    gelu_chunk(PK - 2, PK - 2)
            w_hi(0, 0)
            gelu_chunk(PK - 1, PK - 1)
            v_body(0, made=HI - 1)
            with act.Fori(1, PK // CPB - 1) as i:
                v_body(i)
            v_body(PK // CPB - 1, True)

        @block.tensor
        def _(pe):
            pe.wait_ge(consts, 7)
            norm_turn(pe, 0, 0, R2, -1)
            mm_block(pe, 0, 0, t1hi, t1lo, after=lambda k: norm_turn(pe, 0, 0, R2, k), ready=0)
            mm_block(pe, 1, 1, t1hi, t1lo)
            with pe.Fori(1, B_BIG // 2) as i:
                mm_block(pe, i * 2, 0, t1hi, t1lo)
                mm_block(pe, i * 2 + 1, 1, t1hi, t1lo)
            mm_block(pe, B_BIG, 0, t1hi, t1lo)

            def tick(t):
                m = t - K_GATES
                if 0 <= m < 4:
                    pe.wait_ge(wg_lo, 1)
                    for kc in range(4 * m, 4 * m + 4):
                        o = PS[0:16, 6, 0:T]
                        pe.matmul(o, wghi[:, kc, :], t1hi[:, kc, :], start=(kc == 0), stop=False)
                        pe.matmul(o, wglo[:, kc, :], t1hi[:, kc, :], start=False, stop=False)
                        mm = pe.matmul(o, wghi[:, kc, :], t1lo[:, kc, :], start=False, stop=(kc == KC - 1))
                    if m == 3:
                        mm.then_inc(if_mm, 1)
                if m == 4:
                    pe.wait_ge(if_rows, 1)
                    for tt in range(TT):
                        mm = pe.matmul(PS[:, 6, tt * 16:(tt + 1) * 16], gate_rows[:, tt * P:(tt + 1) * P],
                                       ident[0:16, 0:16], start=True, stop=True)
                    mm.then_inc(if_turned, 1)
                if t == K_GATES + 6:
                    pe.wait_ge(logf_s, 1)
                    pe.matmul(PS[:, 7, 0:MH], tri[:, 0:P], logf[:, 0, :], start=True, stop=True)
                    pe.matmul(PS[:, 7, MH:2 * MH], tri[:, P:T], logf[:, 0, :], start=True, stop=False)
                    pe.matmul(PS[:, 7, MH:2 * MH], tri[:, 0:P], logf[:, 1, :], start=False, stop=True
                              ).then_inc(b_mm, 1)
                if t == K_GATES + 7:
                    pe.wait_ge(a_s, 1)
                    for tt in range(TT):
                        mm = pe.matmul(PS[0:MH, 6, tt * P:(tt + 1) * P], a_in[:, tt, :], ident[:],
                                       start=True, stop=True)
                    mm.then_inc(at_mm, 1)
                if t == K_GATES + 12:
                    pe.wait_ge(m_step, 10)
                    for tt in range(TT):
                        mm = pe.matmul(PS[:, 7, tt * MH:(tt + 1) * MH], mfin[:, tt * P:(tt + 1) * P],
                                       ident[0:MH, 0:MH], start=True, stop=True)
                    mm.then_inc(mt_mm, 1)

                n = t - K_CONV
                if n % 2 == 0 and n // 2 < KC:
                    n //= 2
                    if n >= 2:
                        pe.wait_ge(conv_done, n - 1)
                    for tt in range(TT):
                        mm = pe.transpose(PS[:, 4 + n % 2, tt * P:(tt + 1) * P], R0[:, tt, n * P:(n + 1) * P], ident[:])
                    mm.then_inc(qk_turned, 1)

                for n in range(2 * (t - K_QK), 2 * (t - K_QK) + 2):
                    if not 0 <= n < KC + KVH:
                        continue
                    if n < 2:
                        pe.wait_ge(conv_done, KC - 1 + n)
                    elif n < 4:
                        pe.wait_ge(mt_s, 1)
                    else:
                        pe.wait_ge(q_out, n - 3)
                    if n in (0, KC // 2, KC):
                        pe.wait_ge(q_scaled, {0: TT, KC // 2: 2 * TT, KC: 4 * TT}[n])
                    for tt in range(TT):
                        src = (R2[:, tt, n * P:(n + 1) * P] if n < KC else
                               kd[:, tt, n - KC, :, :].rearrange("p r d -> p (r d)"))
                        mm = pe.transpose(PS[:, 4 + n % 4, tt * P:(tt + 1) * P], src, ident[:])
                    mm.then_inc(q_turned, 1)

                s = t - K_ATT
                if s == 0:
                    pe.wait_ge(q_out, KC + KVH)
                    pe.wait_ge(vb2_s, 1)
                if 3 <= s < N_ITEM + 3:
                    i, b = s - 3, (s - 3) % 2
                    gq, c = i // NCH, i % NCH
                    pe.wait_ge(probT_sb, i + 1)
                    if i >= 1:
                        pe.wait_ge(av_lo, i)
                    cols = slice(T + gq * DH, T + (gq + 1) * DH)
                    v = (kv[:, 0, cols], kv[:, 0, cols], vb2[:, gq * DH:(gq + 1) * DH], kv[:, 1, cols])[c]
                    for par in range(2):
                        mm = pe.matmul(PS[par * DH:(par + 1) * DH, 7, 0:T], v,
                                       probT[:, b, :, par * CH:(par + 1) * CH], start=True, stop=True)
                    mm.then_inc(av_mm, 1)
                if 0 <= s < N_ITEM:
                    b, gq, c = s % 2, s // NCH, s % NCH
                    if s >= 2:
                        pe.wait_ge(prob_exp, s - 1)
                    for j in range(PAIRS):
                        qj = qT_of(PAIRS * gq + j)[:, c * CH:(c + 1) * CH]
                        for par, kt in ((0, kte), (1, kto)):
                            for at, k0, k1 in window(c):
                                mm = pe.matmul(PS[par * CH:(par + 1) * CH, 4 + b, j * P + at:j * P + at + k1 - k0],
                                               qj, kt[:, gq, k0:k1], start=True, stop=True)
                    mm.then_inc(logits_s, 1)
                if 2 <= s < N_ITEM + 2:
                    i, b = s - 2, s % 2
                    pe.wait_ge(prob_norm, i + 1)
                    if i >= 1:
                        pe.wait_ge(probT_sb, i)
                    for j in range(PAIRS):
                        mm = pe.transpose(PS[:, 6, j * P:(j + 1) * P], prob[:, b, j, :], ident[:])
                    mm.then_inc(prob_turned, 1)

                s = t - K_MLSTM
                if s == 0:
                    pe.wait_ge(silu_done, 4)
                    pe.wait_ge(av_lo, N_ITEM)
                h, b = s // 2, s // 2 % 2
                if s % 2 == 0 and 0 <= h < MH:
                    if h >= 1:
                        pe.wait_ge(ms_p, h)
                        pe.wait_ge(mn_step, 4 * h - 3)
                    pe.matmul(PS[:, 4, 0:T], ident[0:MH, h:h + 1].to_broadcast([MH, P]), mfin,
                              start=True, stop=True)
                    pe.matmul(PS[:, 5, 0:T], bt[:, MH + h, 0:P], bt[:, h, :], start=True, stop=True)
                    pe.matmul(PS[:, 5, T:3 * P], bt[:, MH + h, P:T], bt[:, h, P:T], start=True, stop=True
                              ).then_inc(ms_mm, 1)
                if s % 2 == 1 and 0 <= h < MH:
                    pe.wait_ge(ms_p, h + 1)
                    if h >= 2:
                        pe.wait_ge(h_out, h - 1)
                    v = [R1[:, tt, h * MV:(h + 1) * MV] for tt in range(TT)]
                    for rhs, at in ((v, [PS[:, 6 + b, tt * MV:(tt + 1) * MV] for tt in range(TT)]),
                                    ([ones[:, 0:1]] * TT, [mden(b)[:, tt:tt + 1] for tt in range(TT)])):
                        pe.matmul(at[0], pp[:, b, 0:P], rhs[0], start=True, stop=True)
                        pe.matmul(at[1], pp[:, b, P:T], rhs[0], start=True, stop=False)
                        mm = pe.matmul(at[1], pp[:, b, T:3 * P], rhs[1], start=False, stop=True)
                    mm.then_inc(mn_mm, 1)

                if 0 <= t - K_HM < KC:
                    if t == K_HM:
                        pe.wait_ge(h_gated, 2 * TT)
                    turn(pe, 1, t - K_HM, R2)
                if y_tile(t) is not None:
                    pe.wait_ge(y_add, y_tile(t) // 4 + 1)
                    turn(pe, 2, y_tile(t), R0)
                if t >= K_X2:
                    norm_turn(pe, 1, 3, R0, t - K_X2 - 1)

            for b in range(B_FIX, B_END):
                if b == B_PM:
                    pe.wait_ge(t_lo, 2 * KC)
                thi, tlo = (t2hi, t2lo) if B_PA <= b < B_PM or B_WO <= b < B_PQ else (t1hi, t1lo)
                mm_block(pe, b, b % 2, thi, tlo, after=lambda k: tick(tick_of(b, k)),
                         ready={B_WO: 2 * KC, B_PQ: 3 * KC}.get(b))

            def turn_query(n):
                if n == 0:
                    pe.wait_ge(block_out, B_END)
                if n >= 4:
                    pe.wait_ge(qT_sb, n - 3)
                for tt in range(TT):
                    mm = pe.transpose(PS[:, 4 + n % 4, tt * P:(tt + 1) * P], qp[:, tt, n * P:(n + 1) * P], ident[:])
                mm.then_inc(qp_turned, 1)

            def scores(n):
                if n == 0:
                    pe.wait_ge(subk_in, 16)
                pe.wait_ge(qT_sb, 2 * PH)
                if n >= 4:
                    pe.wait_ge(score_sb, n - 3)
                for c in range(2):
                    for tt in range(TT):
                        at = (c * TT + tt) * PK
                        mm = pe.matmul(PS[:, 4 + n % 4, at:at + PK], qT[:, 2 * n + c, tt * P:(tt + 1) * P],
                                       subk[:, c, :], start=True, stop=True)
                mm.then_inc(score_mm, 1)

            def g_token(i, k, m):
                t = i * (CPB * TPC) + (k * TPC + m - C_G * TPC)
                pe.wait_ge(onehots, t + 1)
                pe.matmul(PS[:, 4 + k, m * PK:(m + 1) * PK], oha[:, m % 2, :], ohb[:, m % 2, :],
                          start=True, stop=True).then_inc(g_mm, 1)

            def u_unit(i, n, build=False):
                k, j = n // CU, n % CU
                pe.wait_ge(lo_made, i * (CPB * CU) + (U_U + n + 1))
                for kk in range(UW // P):
                    kc = j * (UW // P) + kk
                    wh = whi[:, n % HI, kk * P:(kk + 1) * P]
                    wl = wlo[:, n % LO, kk * P:(kk + 1) * P]
                    def hi_pass(stop):
                        return pe.matmul(PS[:, A_BANK[k % 4], :], wh, t1[:, kc].rearrange("p s t -> p (s t)"),
                                         start=(kc == 0), stop=stop)

                    def lo_pass():
                        return pe.matmul(PS[:, A_BANK[k % 4], 0:T], wl, t1hi[:, kc, :], start=False, stop=False)

                    if kc < KC - 1:
                        hi_pass(False)
                        mm = lo_pass()
                    else:
                        lo_pass()
                        mm = hi_pass(True)
                    if kk == UW // P - 1:
                        mm.then_inc(unit_used, 1)
                    if build and kk % (UW // P // 2) == UW // P // 2 - 1:
                        g_token(i, k, j * 2 + kk // (UW // P // 2))

            def u_body(i, first=False, build=False, g_waits=False, turn_hk=False):
                for k in range(CPB):
                    if not first:
                        pe.wait_ge(a_summed, i * CPB + (k - 3))
                    if g_waits:
                        pe.wait_ge(g_out, i * CPB + (k - C_G - 3))
                    if turn_hk and k == CPB - 1:
                        pe.wait_ge(hk_ready, 1)
                        for n in range(3):
                            for tt in range(TT):
                                mm = pe.transpose(PS[:, 4 + n, tt * P:(tt + 1) * P], hk[:, n, tt, :], ident[:])
                            mm.then_inc(hk_turned, 1)
                    for j in range(CU):
                        u_unit(i, CU * k + j, build)

            pe.wait_ge(block_out, B_END - 1)
            n_unit = CPB * CU
            for n in range(2 * n_unit):
                i, k = n // n_unit, n % n_unit // CU
                if i and n % CU == 0:
                    pe.wait_ge(a_summed, k + 1)
                u_unit(i, n % n_unit)
                if i == 0:
                    turn_query(2 * n)
                    turn_query(2 * n + 1)
                else:
                    scores(n - n_unit)
            with pe.Fori(2, C_G // CPB - 1) as i:
                u_body(i)
            u_body(C_G // CPB - 1, turn_hk=True)
            pe.wait_ge(hkT_sb, 3)
            u_body(C_G // CPB, build=True)
            with pe.Fori(C_G // CPB + 1, (C_G + T // TPC) // CPB) as i:
                u_body(i, build=True, g_waits=True)
            for i in range((C_G + T // TPC) // CPB, PK // CPB):
                u_body(i)

            pe.wait_ge(a_summed, PK - 1)
            pe.wait_ge(g_out, T // TPC)

            def v_body(i, first, last):
                for k in range(CPB):
                    pe.wait_ge(wch_lo, i * CPB + (k + 1))
                    for j in range(CU):
                        n = CU * k + j
                        if first and n == 1:
                            pe.wait_ge(a_summed, PK)
                        pe.wait_ge(lo_made, i * (CPB * CU) + (U_V + n + 1))
                        for tt in range(TT):
                            sh, sl = t1hi[:, k, tt * P:(tt + 1) * P], t1lo[:, k, tt * P:(tt + 1) * P]
                            for half in range(2):
                                o = PS[:, 4 * tt + 2 * j + half, :]
                                vh = whi[:, n % HI, half * BLK:(half + 1) * BLK]
                                vl = v_lo[n % len(v_lo)][:, half * BLK:(half + 1) * BLK]
                                pe.matmul(o, sh, vh, start=(first and k == 0), stop=False)
                                pe.matmul(o, sh, vl, start=False, stop=False)
                                mm = pe.matmul(o, sl, vh, start=False, stop=(last and k == CPB - 1))
                        mm.then_inc(unit_used, 1)

            v_body(0, True, False)
            with pe.Fori(1, PK // CPB - 1) as i:
                v_body(i, False, False)
            v_body(PK // CPB - 1, False, True)

        @block.vector
        def _(dve):
            for tt in range(TT):
                dve.wait_ge(x_in[tt], 16)
            norm_rs(dve, 0)
            norm_scale(dve, R2, R2, 0)
            norm_scale(dve, R2, R2, 1)
            dve.wait_ge(n1_in, 16)
            lo_unit(dve, 0, 0)
            norm_lo(dve, 0, t1hi, t1lo, n1, -1)
            norm_scale(dve, R2, R2, 2)
            for k in range(BU):
                if k + 1 < BU:
                    lo_unit(dve, k + 1, k + 1)
                norm_lo(dve, 0, t1hi, t1lo, n1, k)
                if k == 0:
                    norm_scale(dve, R2, R2, 3)
            dve.wait_ge(w_small, 6 * 16)
            dve.wait_ge(wg_hi, 1)
            dve.tensor_tensor(wglo[:], wg[:], wghi[:].bitcast(F32), ALU.subtract).then_inc(wg_lo, 1)
            with dve.Fori(1, B_FIX) as b:
                lo_block(dve, b)

            def cols(b):
                n = (b - B_IN) % B_MAT
                return slice(n * BLK, (n + 1) * BLK)

            def out_block(b):
                dve.wait_ge(unit_used, (b + 1) * BU)
                banks = PS[:, 2 * (b % 2):2 * (b % 2) + TT, :]
                if b < B_PM:
                    if b == B_PA:
                        dve.wait_ge(ga_in, 16 * B_MAT)
                    dve.tensor_tensor(R0[:, :, cols(b)], banks, R0[:, :, cols(b)], ALU.mult).then_inc(block_out, 1)
                elif b < B_WO:
                    if b == B_PM:
                        dve.wait_ge(gm_in, 16 * B_MAT)
                    dve.tensor_tensor(R1[:, :, cols(b)], banks, R1[:, :, cols(b)], ALU.mult).then_inc(block_out, 1)
                    dve.wait_ge(block_out, b + 1)
                    dve.tensor_tensor(R0[:, :, cols(b)], R0[:, :, cols(b)], R1[:, :, cols(b)], ALU.add
                                      ).then_inc(y_add, 1)
                elif b < B_PQ:
                    if b == B_WO:
                        dve.wait_ge(xr_in, 16)
                    dve.tensor_tensor(R2[:, :, cols(b)], banks, R2[:, :, cols(b)], ALU.add).then_inc(block_out, 1)
                else:
                    dve.tensor_copy(qp[:, :, cols(b)], banks).then_inc(block_out, 1)

            def tick(t):
                b = B_FIX + t // BU - 1
                if t % BU == 0 and b >= B_IN and b != B_PQ - 1:
                    out_block(b)

                if t == K_GATES + 5:
                    dve.wait_ge(if_turned, 1)
                    dve.tensor_tensor(pre, PS[:, 6, 0:TT * 16].rearrange("p (a n) -> p a n", a=TT),
                                      ifb[:].unsqueeze(1).to_broadcast([P, TT, 16]), ALU.add).then_inc(if_sb, 1)
                    dve.wait_ge(if_sb, 1)
                    dve.tensor_scalar(fmin, pre, 0.0, None, ALU.min).then_inc(f_min, 1)
                if t == K_GATES + 6:
                    dve.wait_ge(f_min, 1)
                    dve.wait_ge(gate_act, 3)
                    dve.tensor_tensor(logf, fmin[:, :, 8:16], fln[:, :, 8:16], ALU.subtract).then_inc(logf_s, 1)
                if t == K_GATES + 7:
                    dve.wait_ge(b_mm, 1)
                    dve.tensor_copy(bsum, PS[:, 7, 0:TT * MH].rearrange("p (a n) -> p a n", a=TT)
                                    ).then_inc(b_sb, 1)
                    dve.wait_ge(b_sb, 1)
                    dve.tensor_tensor(a_in, pre[:, :, 0:8], bsum, ALU.subtract).then_inc(a_s, 1)
                if t == K_GATES + 8:
                    dve.wait_ge(at_mm, 1)
                    dve.tensor_copy(mrow[:, 0, :], PS[0:MH, 6, 0:T]).then_inc(m_step, 1)
                if 0 <= t - K_GATES - 8 < 4:
                    for n in range(2 * (t - K_GATES - 8), 2 * (t - K_GATES - 8) + 2):
                        w, src, dst = 1 << n, mrow[:, n % 2, :], mrow[:, (n + 1) % 2, :]
                        dve.wait_ge(m_step, n + 1)
                        dve.tensor_copy(dst[:, 0:w], src[:, 0:w])
                        dve.tensor_tensor(dst[:, w:T], src[:, w:T], src[:, 0:T - w], ALU.max).then_inc(m_step, 1)
                if t == K_GATES + 12:
                    dve.wait_ge(m_step, 9)
                    dve.tensor_scalar(mfin, mrow[:, 0, :], 0.0, None, ALU.max).then_inc(m_step, 1)
                if t == K_GATES + 13:
                    dve.wait_ge(mt_mm, 1)
                    dve.tensor_tensor(mt, PS[:, 7, 0:TT * MH].rearrange("p (a n) -> p a n", a=TT), bsum, ALU.add
                                      ).then_inc(mt_s, 1)

                for at, backs in ((1, (1,)), (2, (2, 3))):
                    n = t - K_CONV - at
                    if n % 2 or not 0 <= n // 2 < KC:
                        continue
                    n //= 2
                    x, y = PS[:, 4 + n % 2, 0:T], bt[:, n, :]
                    for back in backs:
                        if back == 1:
                            dve.wait_ge(conv_first, n + 1)
                        else:
                            dve.wait_ge(conv_step, 2 * n + back - 1)
                        dve.scalar_tensor_tensor(y[:, back:T], x[:, 0:T - back], cw[:, n, 3 - back:4 - back],
                                                 y[:, back:T], ALU.mult, ALU.add
                                                 ).then_inc(conv_step if back < 3 else conv_done, 1)
                n = t - K_CONV - 9
                if n % 8 == 0 and 0 <= n // 8 < 4:
                    n //= 8
                    dve.wait_ge(sig_done, n + 1)
                    y = bt[:, 4 * n:4 * n + 4, :].rearrange("p k t -> p (k t)")
                    dve.tensor_tensor(y, y, stage[:, n % 2, :], ALU.mult).then_inc(silu_done, 1)

                if t - 1 in K_SQ:
                    m = K_SQ.index(t - 1)
                    dve.wait_ge(q_sq, m + 1)
                    dve.tensor_reduce(qs[:, 0, m // 2, m % 2 * 16:(m % 2 + 1) * 16],
                                      qsq.rearrange("p (h d) -> p h d", d=DH), AX.X, ALU.add).then_inc(q_sum, 1)
                if t == K_KSQ + 1:
                    dve.wait_ge(q_sq, 2 * TT + 1)
                    dve.tensor_reduce(qs[:, 0, :, AH:AH + KVH], ksq.rearrange("p a (h d) -> p a h d", d=DH), AX.X,
                                      ALU.add).then_inc(q_sum, 1)
                if t == K_KZERO:
                    dve.wait_ge(q_sum, 2 * TT + 1)
                    dve.memset(kte[DH:P, :, :], 0.0).then_inc(k_zero, 1)
                    dve.memset(kto[0:DH, :, :], 0.0).then_inc(k_zero, 1)
                    dve.tensor_copy(vb2[0:CH, :], kv[0:CH, 1, T:2 * T]).then_inc(k_zero, 1)
                    dve.tensor_copy(vb2[CH:P, :], kv[CH:P, 0, T:2 * T]).then_inc(k_zero, 1)
                    dve.wait_ge(q_root, 1)
                    dve.reciprocal(qs[:, 2], qs[:, 1]).then_inc(q_rs, 1)
                    dve.wait_ge(q_rs, 1)
                if t in K_SCALE:
                    half, tt = divmod(K_SCALE.index(t), TT)
                    q = R2[:, tt, half * UW:(half + 1) * UW].rearrange("p (h d) -> p h d", d=DH)
                    dve.tensor_tensor(q, q, qs[:, 2, tt, half * 16:(half + 1) * 16].unsqueeze(2)
                                      .to_broadcast([P, 16, DH]), ALU.mult).then_inc(q_scaled, 1)
                if t in K_KD:
                    tt = K_KD.index(t)
                    for r in range(2):
                        dve.tensor_tensor(kd[:, tt, :, r, :], kv[:, tt, 0:T].rearrange("p (h d) -> p h d", d=DH),
                                          qs[:, 2, tt, AH:AH + KVH].unsqueeze(2).to_broadcast([P, KVH, DH]), ALU.mult
                                          ).then_inc(q_scaled, 1)
                for n in range(2 * (t - K_QK - 1), 2 * (t - K_QK - 1) + 2):
                    if not 0 <= n < KC + KVH:
                        continue
                    dve.wait_ge(q_turned, n + 1)
                    x = PS[:, 4 + n % 4, 0:T]
                    if n < KC:
                        dve.tensor_scalar(qT_of(n), x, qkw[:, 0:1], float(DH) ** -0.5, ALU.mult, ALU.mult
                                          ).then_inc(q_out, 1)
                    else:
                        if n == KC:
                            dve.wait_ge(k_zero, 4)
                        dve.tensor_scalar(kte[0:DH, n - KC, :], x[0:DH], qkw[0:DH, 1:2], None, ALU.mult)
                        dve.tensor_scalar(kto[DH:P, n - KC, :], x[DH:P], qkw[DH:P, 1:2], None, ALU.mult
                                          ).then_inc(q_out, 1)
                if t == K_QK + 4:
                    dve.wait_ge(silu_done, 4)
                    dve.memset(stage[:, 0, :], 0.0).then_inc(vb2_s, 1)

                s = t - K_ATT
                if 1 <= s <= N_ITEM:
                    i, b, w = s - 1, (s - 1) % 2, keys_of((s - 1) % NCH)
                    dve.wait_ge(prob_exp, i + 1)
                    if w < P:
                        dve.memset(prob[:, b, :, w:P], 0.0)
                    dve.tensor_tensor(ast[:, b, 5, :], ast[:, b, 3, :], ast[:, b, 4, :], ALU.add).then_inc(st_sum, 1)
                    dve.wait_ge(st_sum, i + 1)
                    dve.reciprocal(ast[:, b, 6, :], ast[:, b, 5, :]).then_inc(st_rec, 1)
                    dve.wait_ge(st_rec, i + 1)
                    dve.tensor_tensor(prob[:, b, :, 0:w], prob[:, b, :, 0:w],
                                      ast[:, b, 6, :].unsqueeze(2).to_broadcast([P, PAIRS, w]), ALU.mult
                                      ).then_inc(prob_norm, 1)
                if 3 <= s < N_ITEM + 3:
                    i = s - 3
                    gq, c = i // NCH, i % NCH
                    dve.wait_ge(av_hi, i + 1)
                    at = (slice(None), slice(PAIRS * gq, PAIRS * (gq + 1)), slice(c * CH, (c + 1) * CH))
                    dve.tensor_tensor(t2lo[at], PS[:, 7, 0:T].rearrange("p (j l) -> p j l", j=PAIRS),
                                      t2hi[at].bitcast(F32), ALU.subtract).then_inc(av_lo, 1)
                if 0 <= s < N_ITEM:
                    b, gq, w = s % 2, s // NCH, keys_of(s % NCH)
                    sk = sink[:, PAIRS * gq:PAIRS * (gq + 1)]
                    dve.wait_ge(logits_s, s + 1)
                    dve.tensor_reduce(ast[:, b, 0, :], PS[:, 4 + b, :].rearrange("p (j n) -> p j n", j=PAIRS)[:, :, 0:w],
                                      AX.X, ALU.max).then_inc(st_step, 1)
                    dve.wait_ge(st_step, s + 1)
                    dve.tensor_tensor(ast[:, b, 0, :], ast[:, b, 0, :], sk, ALU.max).then_inc(st_peak, 1)
                    dve.wait_ge(st_peak, s + 1)
                    dve.tensor_scalar(ast[:, b, 1, :], ast[:, b, 0, :], -1.0, None, ALU.mult)
                    dve.tensor_tensor(ast[:, b, 2, :], sk, ast[:, b, 0, :], ALU.subtract).then_inc(st_max, 1)

                s = t - K_MLSTM
                if s % 2 == 0 and 0 < s <= 2 * MH:
                    h, b = s // 2 - 1, (s // 2 - 1) % 2
                    if h == 0:
                        dve.wait_ge(expnm_s, 1)
                    dve.wait_ge(mn_mm, h + 1)
                    den = hd[:, b, 0, :]
                    dve.tensor_copy(den, mden(b)).then_inc(mn_step, 1)
                    dve.wait_ge(mn_step, 4 * h + 1)
                    dve.scalar_tensor_tensor(den, den, -1.0, den, ALU.mult, ALU.max).then_inc(mn_step, 1)
                    dve.wait_ge(mn_step, 4 * h + 2)
                    dve.tensor_tensor(den, den, expnm[:, :, h], ALU.max).then_inc(mn_step, 1)
                    dve.wait_ge(mn_step, 4 * h + 3)
                    dve.reciprocal(hd[:, b, 1, :], den).then_inc(mn_step, 1)
                    dve.wait_ge(mn_step, 4 * h + 4)
                    for tt in range(TT):
                        mm = dve.tensor_scalar(R2[:, tt, h * MV:(h + 1) * MV], PS[:, 6 + b, tt * MV:(tt + 1) * MV],
                                               hd[:, b, 1, tt:tt + 1], None, ALU.mult)
                    mm.then_inc(h_out, 1)
                h, b = s // 2, s // 2 % 2
                if s % 2 == 0 and 0 <= h < MH:
                    dve.wait_ge(ms_mm, h + 1)
                    if h >= 2:
                        dve.wait_ge(ms_p, h - 1)
                    dve.scalar_tensor_tensor(ee[:, b, 0:T], PS[:, 4, 0:T], -1.0, mask[:], ALU.mult,
                                             ALU.add)
                    dve.scalar_tensor_tensor(ee[:, b, T:3 * P], PS[:, 4, P:T], -1.0, mask[:, 0:P],
                                             ALU.mult, ALU.add).then_inc(ms_arg, 1)
                if s % 2 == 1 and 0 <= h < MH:
                    dve.wait_ge(ms_exp, h + 1)
                    if h >= 2:
                        dve.wait_ge(mn_mm, h - 1)
                    dve.scalar_tensor_tensor(pp[:, b, :], PS[:, 5, 0:3 * P], float(P) ** -0.5, ee[:, b, :],
                                             ALU.mult, ALU.mult).then_inc(ms_p, 1)

                if t == K_HNORM + 1:
                    dve.wait_ge(h_root, 1)
                    dve.reciprocal(hs[:, 2], hs[:, 1]).then_inc(h_rs, 1)
                m = t - K_GATED
                if 0 <= m < 2 * TT:
                    if m == 0:
                        dve.wait_ge(h_rs, 1)
                        dve.wait_ge(o_in, 16 * B_MAT)
                    tt = m // 2
                    for h in range(m % 2 * MH // 2, (m % 2 + 1) * MH // 2):
                        at = slice(h * MV, (h + 1) * MV)
                        mm = dve.scalar_tensor_tensor(R2[:, tt, at], R2[:, tt, at], hs[:, 2, tt, h:h + 1],
                                                      o_sb[:, tt, at], ALU.mult, ALU.mult)
                    mm.then_inc(h_gated, 1)

                if 0 <= t - K_HM - 1 < KC:
                    turn_lo(dve, 1, t - K_HM - 1, t1hi, t1lo, mw)
                if y_tile(t - 1) is not None:
                    turn_lo(dve, 2, y_tile(t - 1), t2hi, t2lo, None)
                if t == K_X2:
                    out_block(B_PQ - 1)
                    dve.wait_ge(n_sq, TT + TT * B_MAT)
                    dve.tensor_reduce(ss, ss_blk, AX.X, ALU.add).then_inc(x2_sum, 1)
                    norm_rs(dve, 1)
                    norm_scale(dve, R2, R0, 0)
                    norm_scale(dve, R2, R0, 1)
                if t >= K_X2:
                    norm_lo(dve, 3, t1hi, t1lo, n2, t - K_X2 - 1)
                if 0 <= t - K_X2 < 2:
                    norm_scale(dve, R2, R0, 2 + t - K_X2)

            for u in range(B_FIX * BU, B_END * BU):
                lo_unit(dve, u, u)
                if u > B_FIX * BU:
                    tick(u - B_FIX * BU - 1)
            lo_unit(dve, U_U, 0)
            out_block(B_END - 1)

            done = [0]

            def step(ins):
                done[0] += 1
                ins.then_inc(route, 1)
                dve.wait_ge(route, done[0])

            def top16(rows, finer=False):
                def positions(at):
                    for n, (v, tv_, ti_) in enumerate(rows):
                        ins = dve.max_index(ti_[:, at:at + 8], tv_[:, at:at + 8], v)
                        if finer and n == len(rows) // 2 - 1:
                            step(ins)
                            yield
                    step(ins)
                    yield

                for v, tv_, _ in rows:
                    ins = dve.max(tv_[:, 0:8], v)
                step(ins)
                yield
                yield from positions(0)
                for v, tv_, _ in rows:
                    ins = dve.match_replace(v, tv_[:, 0:8], v, NEG)
                step(ins)
                yield
                for v, tv_, _ in rows:
                    ins = dve.max(tv_[:, 8:16], v)
                step(ins)
                yield
                yield from positions(8)

            def routing():
                for n in range(PH):
                    dve.wait_ge(score_sb, n + 1)
                    yield from top16([(sc[:, tt, 2 * n + c, :], tv[:, tt, 2 * n + c, :], ti[:, tt, 2 * n + c, :])
                                      for tt in range(TT) for c in range(2)])
                step(dve.tensor_copy(tif[:], ti[:]))
                yield
                for tt in range(TT):
                    for hh in (slice(0, PH // 2), slice(PH // 2, PH)):
                        v = tv[:, tt, :, :].rearrange("p (h c) k -> p h c k", c=2)[:, hh]
                        step(dve.tensor_tensor(cand[:, tt, hh].rearrange("p h (a b) -> p h a b", a=TOP),
                                               v[:, :, 0, :].unsqueeze(3).to_broadcast([P, PH // 2, TOP, TOP]),
                                               v[:, :, 1, :].unsqueeze(2).to_broadcast([P, PH // 2, TOP, TOP]),
                                               ALU.add))
                        yield
                for tt in range(TT):
                    for h0 in range(0, PH, 4):
                        yield from top16([(cand[:, tt, h, :], bv[:, tt, h, :], bi[:, tt, h, :])
                                          for h in range(h0, h0 + 4)], finer=True)
                step(dve.tensor_copy(gsum[:, 0], bv[:, :, :, 0]))
                dve.tensor_tensor(bv[:], bv[:], gsum[:, 0].unsqueeze(3).to_broadcast([P, TT, PH, TOP]), ALU.subtract
                                  ).then_inc(best_sub, 1)
                yield
                flat = bi[:].rearrange("p a h k -> p a (h k)")
                dve.tensor_scalar(ba[:, 0], flat, 4, None, ALU.logical_shift_right)
                step(dve.tensor_scalar(ba[:, 1], flat, TOP - 1, None, ALU.bitwise_and))
                step(dve.tensor_copy(baf[:], ba[:]))
                yield
                half = PH * TOP // 2
                parts = [(tt, slice(m * half, (m + 1) * half), slice(m * PH // 2, (m + 1) * PH // 2))
                         for tt in range(TT) for m in range(2)]
                for c in range(2):
                    for tt, hks, _ in parts:
                        step(dve.tensor_tensor(eq[:, tt, hks], baf[:, c, tt, hks].unsqueeze(2)
                                               .to_broadcast([P, half, TOP]),
                                               iota16.unsqueeze(1).to_broadcast([P, half, TOP]), ALU.is_equal))
                        yield
                    for tt, hks, hh in parts:
                        e = eq[:, tt, hks].rearrange("p (h k) a -> p h k a", k=TOP)
                        side = tif[:, tt].rearrange("p (h c) k -> p h c k", c=2)[:, hh, c, :]
                        step(dve.tensor_tensor(e, e, side.unsqueeze(2).to_broadcast([P, PH // 2, TOP, TOP]), ALU.mult))
                        yield
                    for tt, hks, _ in parts:
                        step(dve.tensor_reduce(hk[:, c, tt, hks], eq[:, tt, hks], AX.X, ALU.add))
                        yield
                dve.wait_ge(best_exp, 1)
                step(dve.tensor_reduce(gsum[:, 0], bv[:], AX.X, ALU.add))
                step(dve.reciprocal(gsum[:, 1], gsum[:, 0]))
                dve.tensor_tensor(hk[:, 2].rearrange("p a (h k) -> p a h k", h=PH), bv[:],
                                  gsum[:, 1].unsqueeze(3).to_broadcast([P, TT, PH, TOP]), ALU.mult
                                  ).then_inc(hk_ready, 1)
                yield

            def a_sum(c, k):
                if not (isinstance(c, int) and c < 2):
                    dve.wait_ge(gel_stored[k % 2], (c // 2) * 16 if isinstance(c, int) else c * 8 - (k % 2) * 8)
                halves = PS[:, A_BANK[k % 4], :].rearrange("p (s t) -> p t s", s=2)
                dve.tensor_reduce(gel[:, k % 2, :], halves, AX.X, ALU.add).then_inc(a_summed, 1)

            def u_lo(u):
                lo_unit(dve, U_U + u, u)
                if u % CU == CU - 1 and u > CU:
                    a_sum(u // CU - 1, u // CU - 1)

            dve.wait_ge(iota_set, 1)
            steps = routing()
            first_step = 2 * CPB * CU + 2
            for u in range(1, C_G * CU - CU):
                u_lo(u)
                if u >= first_step:
                    next(steps, None)
            assert next(steps, "over") == "over"
            for n in range(3):
                if n < CU:
                    u_lo(C_G * CU - CU + n)
                dve.wait_ge(hk_turned, n + 1)
                dve.tensor_copy(hkT[:, n, :], PS[:, 4 + n, 0:T]).then_inc(hkT_sb, 1)

            dve.wait_ge(hkT_sb, 3)
            dve.wait_ge(iota_set, 2)

            def onehot(t, k, first=False):
                if not first:
                    dve.wait_ge(g_mm, t - 1)
                at = bass.ds(t, 1)
                dve.tensor_scalar(oha[:, k, :], iota[:], hkT[:, 0, at], hkT[:, 2, at], ALU.is_equal, ALU.mult)
                dve.tensor_scalar(ohb[:, k, :], iota[:], hkT[:, 1, at], None, ALU.is_equal).then_inc(onehots, 1)

            def onehot_body(i, first=False):
                for n in range(CPB * CU):
                    lo_unit(dve, i * (CPB * CU) + (U_U + C_G * CU + n), n)
                    if n % CU == CU - 1:
                        a_sum(i * CPB + (C_G + n // CU - 1), (n // CU - 1) % CPB)
                    for k in range(2):
                        onehot(i * (CPB * CU * 2) + (2 * n + k), k, first and n == 0)

            onehot_body(0, True)
            with dve.Fori(1, T // TPC // CPB) as i:
                onehot_body(i)
            def w_chunk(c, k, back):
                dve.wait_ge(gel_back[k % 2], back)
                gc = g[:, bass.ds(c, 1), :].rearrange("p a t -> p (a t)")
                dve.tensor_tensor(gc, gback[:, k % 2, :], gc, ALU.mult).then_inc(w_made, 1)

            def w_lo(c, k):
                dve.wait_ge(wch_hi, c + 1)
                dve.tensor_tensor(t1lo[:, k % CPB, :], g[:, bass.ds(c, 1), :].rearrange("p a t -> p (a t)"),
                                  t1hi[:, k % CPB, :].bitcast(F32), ALU.subtract).then_inc(wch_lo, 1)

            def v_lo_unit(i, n):
                u = i * (CPB * CU) + (U_V + n)
                dve.wait_ge(hi_made, u + 1)
                if isinstance(u, int) and u < U_V + LO:
                    dve.wait_ge(unit_used, u - LO + 1)
                elif isinstance(u, int) and u < U_V + len(v_lo):
                    dve.wait_ge(unit_used, U_V)
                else:
                    dve.wait_ge(unit_used, u - len(v_lo) + 1)
                dve.tensor_tensor(v_lo[n % len(v_lo)], raw[:, n % RAW, :], whi[:, n % HI, :].bitcast(F32),
                                  ALU.subtract).then_inc(lo_made, 1)

            def v_body(i, last=False, made=0):
                for k in range(CPB):
                    for j in range(CU):
                        if CU * k + j >= made:
                            v_lo_unit(i, CU * k + j)
                        if j == 0 and not (last and k >= CPB - 2):
                            w_chunk(i * CPB + (k + 2), k, i * 32 + (k // 2 + 2) * 16)
                        if j == 1 and not (last and k == CPB - 1):
                            w_lo(i * CPB + (k + 1), k + 1)

            for u in range(C_G * CU + T // TPC * CU, PK * CU):
                u_lo(u)
                if u == (PK - 1) * CU:
                    dve.wait_ge(g_out, T // TPC)
                    w_chunk(0, 0, 16)
            w_chunk(1, 1, 16)
            v_lo_unit(0, 0)
            w_lo(0, 0)
            a_sum(PK - 1, PK - 1)
            v_body(0, made=1)
            with dve.Fori(1, PK // CPB - 1) as i:
                v_body(i)
            v_body(PK // CPB - 1, True)

            dve.wait_ge(x2_in, 16 * TT)
            for j in range(CU):
                dve.wait_ge(unit_used, UNITS - CU + 1 + j)
                for tt in range(TT):
                    dve.tensor_tensor(out_sb[tt][:, j * UW:(j + 1) * UW],
                                      PS[:, 4 * tt + 2 * j:4 * tt + 2 * j + 2, :].rearrange("p b n -> p (b n)"),
                                      x2_back[tt][:, j * UW:(j + 1) * UW], ALU.add).then_inc(y_out, 1)


def lay_out(inputs):
    a = {k: np.asarray(v) for k, v in inputs.items()}
    w = a["w_in"][0]
    cut = np.cumsum([0, 1024, 1024, 2048, 2048, 8, 8, 2048, 256, 256, 2048, 2048])
    qm, km, vm, om, im, fm, qa, ka, va, gm, ga = (w[:, cut[i]:cut[i + 1]] for i in range(11))

    def blocks(m):
        n = m.shape[1] // BLK
        return m.reshape(BU, 2, P, n, BLK).transpose(3, 0, 2, 1, 4).reshape(n * BU, P, UW)

    u = a["expert_u"][0].reshape(PK, PK, CU, UW // P, P)
    u = u.transpose(1, 2, 4, 3, 0).reshape(PK * CU, P, UW)
    v = a["expert_v"][0].reshape(PK, PK, CU, UW).transpose(1, 2, 0, 3).reshape(PK * CU, P, UW)
    units = np.concatenate([blocks(m) for m in (ka_va(ka, va), qm, km, vm, qa, om, ga, gm, a["w_proj_a"][0],
                                                a["w_proj_m"][0], a["w_out"][0], a["w_peer_q"][0])] + [u, v])

    def column(x):
        return np.ascontiguousarray(x.reshape(KC, P).T)

    def rep(x, n):
        return np.ascontiguousarray(np.broadcast_to(x, (n,) + x.shape))

    x = a["x"][0].reshape(TT, P, D).transpose(1, 0, 2)
    wi = np.concatenate([im, fm], axis=1).reshape(KC, P, 16).transpose(1, 0, 2)
    sinks = np.repeat(a["sinks"][0].reshape(KC, 2).T, CH, axis=0)
    qk = np.stack([np.tile(a["q_norm_w"][0], 2), np.tile(a["k_norm_w"][0], 2)], axis=1)
    return {
        "units": units,
        "w_if": wi,
        "x": x,
        "norm1": column(a["norm1_w"][0]),
        "norm2": column(a["norm2_w"][0]),
        "conv_w": a["conv_w"][0].reshape(4, KC, P).transpose(2, 1, 0),
        "if_bias": rep(np.concatenate([a["b_igate"][0], a["b_fgate"][0]]), P),
        "mnorm": column(np.tile(a["mlstm_norm_w"][0], MH)),
        "qk_w": qk,
        "sinks": sinks,
        "subk": a["sub_keys"][0].transpose(2, 0, 1),
    }


def ka_va(ka, va):
    return np.concatenate([ka, va], axis=1)


def kernel(**inputs):
    import concourse.bacc as _bacc
    from concourse.bass_utils import run_bass_kernel_spmd as _run

    nc = _bacc.Bacc("TRN2", target_bir_lowering=False, num_devices=1)
    arrays, args = {}, []
    for name, v in lay_out(inputs).items():
        v = np.ascontiguousarray(v)
        arrays[f"in_{name}"] = v
        args.append(nc.dram_tensor(f"in_{name}", v.shape, F32, kind="ExternalInput").ap())
    out = nc.dram_tensor("out", (P, TT, D), F32, kind="ExternalOutput").ap()
    gates = nc.dram_tensor("gates_spill", (B_GATE, P, TT * BLK), F32, kind="Internal").ap()
    x2 = nc.dram_tensor("x2_spill", (P, TT, D), F32, kind="Internal").ap()
    gel = nc.dram_tensor("gelu_spill", (PK, P, T), F32, kind="Internal").ap()
    block_program(nc, *args, out, gates, x2, gel)
    r = _run(nc, [arrays], core_ids=[0])
    return np.ascontiguousarray(r.results[0]["out"].transpose(1, 0, 2)).reshape(1, T, D)
```
